# Optimizing a Trainium2 kernel written in Bass

```python
import math
import jax, jax.numpy as jnp
from jax import lax
import numpy as np

D_MODEL = 1024
BATCH = 1
SEQ = 256
DEPTH = 1
DEC_BATCH = 8
DEC_SEQ = 4
PAST_LEN = 2048
PAGE_SIZE = 128

MIX_WIDTH = D_MODEL
POOL_WINDOWS = (2, 4, 8, 16)
N_POOL_GROUPS = len(POOL_WINDOWS)
POOL_WIDTH = MIX_WIDTH // 4
POOL_GROUP = POOL_WIDTH // N_POOL_GROUPS
POOL_BUF = max(POOL_WINDOWS) - 1
GDN_WIDTH = MIX_WIDTH - POOL_WIDTH
GDN_HEAD_DIM = 128
GDN_HEADS = GDN_WIDTH // GDN_HEAD_DIM
CONV_WIDTH = 4
CONV_CH = 3 * GDN_WIDTH
GDN_CHUNK = 64
IN_WIDTH = POOL_WIDTH + CONV_CH + GDN_WIDTH + 2 * GDN_HEADS
N_EXPERTS = 32
TOP_K = 4
D_FF = D_MODEL
SWIGLU_LIMIT = 7.0
SWIGLU_ALPHA = 1.702
MOE_BLOCK = 128
EPS = 1e-6

kernel_name = 'hybrid_pool_gdn_moe_step'

def rmsnorm(x, g):
    xf = x.astype(jnp.float32)
    y = xf * lax.rsqrt(jnp.mean(xf * xf, axis=-1, keepdims=True) + EPS)
    return (y * g.astype(jnp.float32)).astype(x.dtype)

def l2norm(x):
    return x * lax.rsqrt(jnp.sum(x * x, axis=-1, keepdims=True) + EPS)

def pool_mixer(u, buf, start_pos, w_pool, pool_scale):
    bsz, t, _ = u.shape
    ext = jnp.concatenate([buf.astype(u.dtype), u], axis=1)
    extf = ext.astype(jnp.float32)
    cs = jnp.concatenate([jnp.zeros((bsz, 1, POOL_WIDTH), jnp.float32), jnp.cumsum(extf, axis=1)], axis=1)
    pos = start_pos + jnp.arange(t)
    means = []
    for gi, w in enumerate(POOL_WINDOWS):
        lo_c, hi_c = gi * POOL_GROUP, (gi + 1) * POOL_GROUP
        hi = cs[:, POOL_BUF + 1:POOL_BUF + 1 + t, lo_c:hi_c]
        lo = cs[:, POOL_BUF + 1 - w:POOL_BUF + 1 - w + t, lo_c:hi_c]
        cnt = jnp.minimum(pos + 1, w).astype(jnp.float32)[None, :, None]
        means.append((hi - lo) / cnt)
    pooled = jnp.concatenate(means, axis=-1) - extf[:, POOL_BUF:]
    pooled = pooled.reshape(bsz, t, N_POOL_GROUPS, POOL_GROUP)
    out = jnp.einsum('btgc,gcd->btgd', pooled, w_pool.astype(jnp.float32)).reshape(bsz, t, POOL_WIDTH)
    out = out * pool_scale.astype(jnp.float32)
    return out.astype(u.dtype), ext[:, -POOL_BUF:].astype(buf.dtype)

def causal_conv(x, buf, w):
    t = x.shape[1]
    ext = jnp.concatenate([buf.astype(x.dtype), x], axis=1)
    out = sum(ext[:, j:j + t] * w[j] for j in range(CONV_WIDTH))
    return jax.nn.silu(out), ext[:, -(CONV_WIDTH - 1):].astype(buf.dtype)

def gated_delta_rule(q, k, v, g, beta, s0):
    b, t, h, dk = q.shape
    dv = v.shape[-1]
    c = math.gcd(t, GDN_CHUNK)
    n = t // c

    def blocks(a):
        return jnp.moveaxis(a.reshape((b, n, c) + a.shape[2:]), 2, 3)

    q, k, v, g, beta = (blocks(a) for a in (q, k, v, g, beta))
    gc = jnp.cumsum(g, axis=-1)
    idx = jnp.arange(c)
    tril = idx[:, None] >= idx[None, :]
    strict = idx[:, None] > idx[None, :]
    diff = gc[..., :, None] - gc[..., None, :]
    decay = jnp.where(tril, jnp.exp(jnp.where(tril, diff, 0.0)), 0.0)
    kb = k * beta[..., None]
    vb = v * beta[..., None]
    lmat = jnp.where(strict, jnp.einsum('bnhid,bnhjd->bnhij', kb, k) * decay, 0.0)
    eye = jnp.eye(c, dtype=q.dtype)
    tinv = lax.linalg.triangular_solve(eye + lmat, jnp.broadcast_to(eye, lmat.shape),
                                       left_side=True, lower=True, unit_diagonal=True)
    u = jnp.einsum('bnhij,bnhje->bnhie', tinv, vb)
    w = jnp.einsum('bnhij,bnhjd->bnhid', tinv, kb * jnp.exp(gc)[..., None])
    qk = jnp.where(tril, jnp.einsum('bnhid,bnhjd->bnhij', q, k) * decay, 0.0)
    q_dec = q * jnp.exp(gc)[..., None]
    g_last = gc[..., -1]
    k_dec = k * jnp.exp(g_last[..., None] - gc)[..., None]

    def step(s, xs):
        q_i, k_i, u_i, w_i, qk_i, gl_i = xs
        v_new = u_i - jnp.einsum('bhcd,bhde->bhce', w_i, s)
        o_i = jnp.einsum('bhcd,bhde->bhce', q_i, s) + jnp.einsum('bhij,bhje->bhie', qk_i, v_new)
        s = s * jnp.exp(gl_i)[..., None, None] + jnp.einsum('bhcd,bhce->bhde', k_i, v_new)
        return s, o_i

    xs = tuple(jnp.moveaxis(a, 1, 0) for a in (q_dec, k_dec, u, w, qk, g_last))
    s_final, o = lax.scan(step, s0, xs)
    o = jnp.moveaxis(jnp.moveaxis(o, 0, 1), 3, 2).reshape(b, t, h, dv)
    return o, s_final

def moe_ffn(h, router_w, router_b, w_gu, b_gu, w_down, b_down):
    n, d = h.shape
    logits = (h @ router_w + router_b).astype(jnp.float32)
    top_vals, top_idx = lax.top_k(logits, TOP_K)
    gates = jax.nn.softmax(top_vals, axis=-1)
    nk = n * TOP_K
    flat_e = top_idx.reshape(nk)
    order = jnp.argsort(flat_e)
    sorted_e = flat_e[order]
    sorted_tok = (order // TOP_K).astype(jnp.int32)
    sorted_gate = gates.reshape(nk)[order]
    counts = jnp.bincount(flat_e, length=N_EXPERTS)
    padded = (counts + MOE_BLOCK - 1) // MOE_BLOCK * MOE_BLOCK
    start = jnp.cumsum(counts) - counts
    padded_end = jnp.cumsum(padded)
    padded_start = padded_end - padded
    dest = padded_start[sorted_e] + jnp.arange(nk) - start[sorted_e]
    n_blocks = -(-nk // MOE_BLOCK) + N_EXPERTS
    rows = n_blocks * MOE_BLOCK
    row_tok = jnp.full((rows,), n, jnp.int32).at[dest].set(sorted_tok)
    row_gate = jnp.zeros((rows,), jnp.float32).at[dest].set(sorted_gate)
    block_e = jnp.minimum(jnp.searchsorted(padded_end, jnp.arange(n_blocks) * MOE_BLOCK, side='right'),
                          N_EXPERTS - 1)
    h_pad = jnp.concatenate([h, jnp.zeros((1, d), h.dtype)], axis=0)
    xb = h_pad[row_tok].reshape(n_blocks, MOE_BLOCK, d)

    def expert_block(args):
        x_blk, e = args
        gu = x_blk @ w_gu[e] + b_gu[e]
        gate = jnp.minimum(gu[:, :D_FF], SWIGLU_LIMIT)
        up = jnp.clip(gu[:, D_FF:], -SWIGLU_LIMIT, SWIGLU_LIMIT)
        glu = gate * jax.nn.sigmoid(SWIGLU_ALPHA * gate)
        return ((up + 1.0) * glu) @ w_down[e] + b_down[e]

    yb = lax.map(expert_block, (xb, block_e)).reshape(rows, d)
    out = jnp.zeros((n + 1, d), jnp.float32).at[row_tok].add(yb.astype(jnp.float32) * row_gate[:, None])
    return out[:n].astype(h.dtype)

def hybrid_layer(x, c, pool_buf, conv_buf, s0, start_pos,
                 w_ada, b_ada, g_pre_mix, g_post_mix, g_pre_ffn, g_post_ffn,
                 w_in, w_pool, pool_scale, conv_w, a_log, dt_bias, gdn_norm_w, w_out,
                 router_w, router_b, w_gu, b_gu, w_down, b_down):
    bsz, t, _ = x.shape
    f32 = jnp.float32
    mod = (jax.nn.silu(c) @ w_ada + b_ada)[:, None, :]
    sh_mix, sc_mix, gt_mix, sh_ffn, sc_ffn, gt_ffn = jnp.split(mod, 6, axis=-1)

    h = rmsnorm(x, g_pre_mix) * (1.0 + sc_mix) + sh_mix
    proj = h @ w_in
    o1 = POOL_WIDTH
    o2 = o1 + CONV_CH
    o3 = o2 + GDN_WIDTH
    o4 = o3 + GDN_HEADS
    u, qkv, z, a, bb = proj[..., :o1], proj[..., o1:o2], proj[..., o2:o3], proj[..., o3:o4], proj[..., o4:]
    pool_out, pool_buf_new = pool_mixer(u, pool_buf, start_pos, w_pool, pool_scale)
    qkv_c, conv_buf_new = causal_conv(qkv, conv_buf, conv_w)
    qkv_c = qkv_c.astype(f32).reshape(bsz, t, 3, GDN_HEADS, GDN_HEAD_DIM)
    q = l2norm(qkv_c[:, :, 0]) * (GDN_HEAD_DIM ** -0.5)
    k = l2norm(qkv_c[:, :, 1])
    v = qkv_c[:, :, 2]
    g = -jnp.exp(a_log.astype(f32)) * jax.nn.softplus(a.astype(f32) + dt_bias.astype(f32))
    beta = jax.nn.sigmoid(bb.astype(f32))
    o, s_new = gated_delta_rule(q, k, v, g, beta, s0.astype(f32))
    zf = z.astype(f32).reshape(bsz, t, GDN_HEADS, GDN_HEAD_DIM)
    o = o * lax.rsqrt(jnp.mean(o * o, axis=-1, keepdims=True) + EPS) * gdn_norm_w.astype(f32) * jax.nn.silu(zf)
    mix = jnp.concatenate([pool_out, o.reshape(bsz, t, GDN_WIDTH).astype(x.dtype)], axis=-1) @ w_out
    x = x + gt_mix * rmsnorm(mix, g_post_mix)

    h = rmsnorm(x, g_pre_ffn) * (1.0 + sc_ffn) + sh_ffn
    f = moe_ffn(h.reshape(bsz * t, D_MODEL), router_w, router_b, w_gu, b_gu, w_down, b_down)
    x = x + gt_ffn * rmsnorm(f.reshape(bsz, t, D_MODEL), g_post_ffn)
    return x, pool_buf_new, conv_buf_new, s_new.astype(s0.dtype)

def setup_inputs(seed: int = 0) -> dict:
    key = jax.random.key(seed)
    ks = jax.random.split(key, 32)

    def nrm(k, shape, s):
        return jax.random.normal(k, shape, jnp.float32) * s

    L = DEPTH
    return {
        'x_prompt': nrm(ks[0], (BATCH, SEQ, D_MODEL), 1.0),
        'x_sample': nrm(ks[1], (DEC_BATCH, DEC_SEQ, D_MODEL), 1.0),
        'c_prompt': nrm(ks[2], (BATCH, D_MODEL), 1.0),
        'c_sample': nrm(ks[3], (DEC_BATCH, D_MODEL), 1.0),
        'state_pool': nrm(ks[4], (L, DEC_BATCH, POOL_BUF, POOL_WIDTH), 1.0),
        'state_conv': nrm(ks[5], (L, DEC_BATCH, CONV_WIDTH - 1, CONV_CH), 1.0),
        'state_ssm': nrm(ks[6], (L, DEC_BATCH, GDN_HEADS, GDN_HEAD_DIM, GDN_HEAD_DIM), 0.1),
        'w_ada': nrm(ks[7], (L, D_MODEL, 6 * D_MODEL), D_MODEL ** -0.5),
        'b_ada': nrm(ks[8], (L, 6 * D_MODEL), 0.02),
        'g_pre_mix': 1.0 + nrm(ks[9], (L, D_MODEL), 0.05),
        'g_post_mix': 1.0 + nrm(ks[10], (L, D_MODEL), 0.05),
        'g_pre_ffn': 1.0 + nrm(ks[11], (L, D_MODEL), 0.05),
        'g_post_ffn': 1.0 + nrm(ks[12], (L, D_MODEL), 0.05),
        'w_in': nrm(ks[13], (L, D_MODEL, IN_WIDTH), D_MODEL ** -0.5),
        'w_pool': nrm(ks[14], (L, N_POOL_GROUPS, POOL_GROUP, POOL_GROUP), POOL_GROUP ** -0.5),
        'pool_scale': 1.0 + nrm(ks[15], (L, POOL_WIDTH), 0.1),
        'conv_w': nrm(ks[16], (L, CONV_WIDTH, CONV_CH), CONV_WIDTH ** -0.5),
        'a_log': jnp.log(jax.random.uniform(ks[17], (L, GDN_HEADS), jnp.float32, 1.0, 16.0)),
        'dt_bias': nrm(ks[18], (L, GDN_HEADS), 0.1),
        'gdn_norm_w': 1.0 + nrm(ks[19], (L, GDN_HEAD_DIM), 0.05),
        'w_out': nrm(ks[20], (L, MIX_WIDTH, D_MODEL), MIX_WIDTH ** -0.5),
        'router_w': nrm(ks[21], (L, D_MODEL, N_EXPERTS), D_MODEL ** -0.5),
        'router_b': nrm(ks[22], (L, N_EXPERTS), 0.01),
        'w_gu': nrm(ks[23], (L, N_EXPERTS, D_MODEL, 2 * D_FF), D_MODEL ** -0.5),
        'b_gu': nrm(ks[24], (L, N_EXPERTS, 2 * D_FF), 0.01),
        'w_down': nrm(ks[25], (L, N_EXPERTS, D_FF, D_MODEL), D_FF ** -0.5),
        'b_down': nrm(ks[26], (L, N_EXPERTS, D_MODEL), 0.01),
    }

def reference(x_prompt, x_sample, c_prompt, c_sample, state_pool, state_conv, state_ssm,
              w_ada, b_ada, g_pre_mix, g_post_mix, g_pre_ffn, g_post_ffn,
              w_in, w_pool, pool_scale, conv_w, a_log, dt_bias, gdn_norm_w, w_out,
              router_w, router_b, w_gu, b_gu, w_down, b_down):
    y_prompt, y_sample = x_prompt, x_sample
    bp = x_prompt.shape[0]
    pool_p, conv_p, ssm_p, pool_s, conv_s, ssm_s = [], [], [], [], [], []
    for l in range(DEPTH):
        lp = (w_ada[l], b_ada[l], g_pre_mix[l], g_post_mix[l], g_pre_ffn[l], g_post_ffn[l],
              w_in[l], w_pool[l], pool_scale[l], conv_w[l], a_log[l], dt_bias[l], gdn_norm_w[l], w_out[l],
              router_w[l], router_b[l], w_gu[l], b_gu[l], w_down[l], b_down[l])
        zero_pool = jnp.zeros((bp, POOL_BUF, POOL_WIDTH), state_pool.dtype)
        zero_conv = jnp.zeros((bp, CONV_WIDTH - 1, CONV_CH), state_conv.dtype)
        zero_ssm = jnp.zeros((bp, GDN_HEADS, GDN_HEAD_DIM, GDN_HEAD_DIM), state_ssm.dtype)
        y_prompt, pp, cp, sp = hybrid_layer(y_prompt, c_prompt, zero_pool, zero_conv, zero_ssm, 0, *lp)
        y_sample, ps, cs, ss = hybrid_layer(y_sample, c_sample, state_pool[l], state_conv[l], state_ssm[l],
                                            PAST_LEN, *lp)
        pool_p.append(pp)
        conv_p.append(cp)
        ssm_p.append(sp)
        pool_s.append(ps)
        conv_s.append(cs)
        ssm_s.append(ss)
    return (y_prompt, y_sample, jnp.stack(pool_p), jnp.stack(conv_p), jnp.stack(ssm_p),
            jnp.stack(pool_s), jnp.stack(conv_s), jnp.stack(ssm_s))


_drawn_inputs = setup_inputs


def setup_inputs(seed=0):
    import zlib

    import numpy as np

    out = dict(_drawn_inputs(seed))
    spreads = {}
    factors = {'a_log': 5.004, 'dt_bias': 3.477, 'router_b': 4.292, 'b_gu': 8.0, 'b_down': 8.0}
    for name, (base, spread) in spreads.items():
        noise = np.random.default_rng([zlib.crc32(name.encode()), seed]).standard_normal(out[name].shape)
        drawn = base * np.exp(spread * noise) if base else spread * noise
        out[name] = __import__('jax').numpy.asarray(drawn.astype(out[name].dtype))
    for name, factor in factors.items():
        out[name] = (out[name] * factor).astype(out[name].dtype)
    return out
```

```python
from contextlib import ExitStack

import numpy as np
import concourse.bass as bass
from concourse import mybir

F32 = mybir.dt.float32
BF16 = mybir.dt.bfloat16
I32 = mybir.dt.int32
ALU = mybir.AluOpType
ACT = mybir.ActivationFunctionType
AX = mybir.AxisListType

P = 128
D = 1024
KT = D // P
SEQ, NSEQ, DSEQ = 256, 8, 4
NS = NSEQ * DSEQ
TOK = SEQ + NS
ROWS = (P, P, NS)
AT = (0, P, SEQ)
POOLW, PBUF = 256, 15
H, DH = 6, 128
GW = H * DH
CW = 3 * GW
CT = CW // P
NU = POOLW // P
NT = NU + CT
IN_W = POOLW + CW + GW + 2 * H
NE, TOPK, FF = 32, 4, 1024
SLOTS = 64
LIMIT, ALPHA = 7.0, 1.702
EPS = 1e-6
LEVELS = 7
SLEVELS = 2
TAIL = PBUF + NS
RING = 4
SEQS = 1 + NSEQ


CONST = {}


def shape_constants():
    k = np.arange(P)[:, None]
    j = np.arange(P)[None, :]
    ks, js = np.arange(P)[:, None], np.arange(NS)[None, :]
    same = (ks // DSEQ == js // DSEQ) & (ks < NS)
    parts = [
        ("ident", k == j),
        ("ones", np.ones((P, P))),
        ("before", k < j),
        ("iota", np.broadcast_to(j % SLOTS, (P, P))),
        ("upto", k <= j),
        ("after", k > j),
        ("tril", j <= k),
        ("upto_s", (ks <= js) & same),
        ("after_s", (ks > js) & same),
        ("tril_s", (js <= ks) & same),
        ("of_seq", (ks // DSEQ == np.arange(NSEQ)[None, :]) & (ks < NS)),
        ("valid", np.broadcast_to(ks[:, 0:1] < NS, (P, 2))),
        ("seqmask", np.broadcast_to((np.arange(NS)[None, :] // DSEQ == np.arange(NSEQ)[:, None])
                                    .reshape(1, -1), (P, NSEQ * NS))),
    ]
    win = np.array([[2, 8], [4, 16]])[(np.arange(P) >= 64).astype(int)]
    parts.append(("invwin", 1.0 / win))
    cnt = np.minimum(np.arange(16)[None, None, :] + 1, win[:, :, None])
    parts.append(("invcnt", (1.0 / cnt).reshape(P, -1)))
    at = 0
    for name, a in parts:
        CONST[name] = (at, a.shape[1])
        at += a.shape[1]
    CONST["all"] = (0, at)
    masks = [((k >> (l + 1)) == (j >> (l + 1))) & ((k >> l) % 2 == 1) & ((j >> l) % 2 == 0)
             for l in range(LEVELS)]
    masks_s = [((ks >> (l + 1)) == (js >> (l + 1))) & ((ks >> l) % 2 == 1) & ((js >> l) % 2 == 0) & (ks < NS)
               for l in range(SLEVELS)]
    flat = np.concatenate([np.asarray(a, np.float32) for _, a in parts], axis=1)
    level = np.concatenate([np.where(m, 0x3F80, 0).astype(np.uint16) for m in masks + masks_s], axis=1)
    CONST["levels"] = (at, level.shape[1] // 2)
    return np.concatenate([flat, np.ascontiguousarray(level).view(np.float32)], axis=1)


shape_constants()
LEVEL_COLS = LEVELS * P + SLEVELS * NS

IN_SLOTS = [(3072, IN_W - 3072)] + [(512 * n, 512) for n in range(6)]
N_IN = len(IN_SLOTS)
ADA_FIRST = 4
RING_SLOTS = [("ada", s) for s in range(ADA_FIRST)] + [("in", s) for s in range(N_IN)] \
    + [("ada", s) for s in range(ADA_FIRST, 12)]


class Arena:

    def __init__(self, tensor, words):
        self.t, self.words = tensor, words

    def at(self, off, *shape):
        n = int(np.prod(shape))
        assert off + n <= self.words, (off, n, self.words)
        v = self.t[:, off:off + n]
        if len(shape) == 2:
            v = v.rearrange("p (a b) -> p a b", a=shape[0])
        if len(shape) == 3:
            v = v.rearrange("p (a b c) -> p a b c", a=shape[0], b=shape[1])
        return v


class Chain:

    def __init__(self, eng, sem):
        self.eng, self.sem, self.n = eng, sem, 0

    def __call__(self, ins):
        self.n += 1
        ins.then_inc(self.sem, 1)
        self.eng.wait_ge(self.sem, self.n)


SEMS = """acc_add bguT c_in c_silu ch_act ch_dve ch_pool const_in conv_done cum cur_set d_in0 d_in1 dexp
 diff_ps egates eps_set fin_in fin_y gT g_ready ga gate_done gate_ps gated gates gex gm_in gu_a gu_in00
 gu_in01 gu_in02 gu_in03 gu_in10 gu_in11 gu_in12 gu_in13 gu_ps gu_v h2 h2T h2_ps hT_a hT_s hid hid_ps hid_step
 hist_in kdec kk_ps kqm ks_ps kvT_ps kv_tok lmat mix_ps ml modG modG_st modT modT_ps mod_sb ms
 n_exp norm_ps oT oT_ps o_ms o_ps o_rstd o_tok p1 p1_ps poolT pool_ps pooled proj_ps qk_n qk_ps qkd qkdT
 qkdT_ps qs_sb rank_done ring0 ring1 ring2 ring3 rl_sb router_ps rr rstd rt_in s_new s_ps s_silu s_taps sc_ps
 sel sel_step selg setup_ps setup_sb sgT sgT_ps sig silu_done slot_used small_in softplus_a
 softplus_v sp_e sq ssm_in ssm_out ssq t0 tailT_ps tail_rows tail_st tap3 tn_ps top_e tu_done u0 u0_ps u_sb
 vec_in vmask vn vn_ps wout_in wpool_in x1 x1_st x2T_ps xT_ps xTm xTm_ps x_in xg xg_ps xn xn2 y_ps y_sb y_st
 z_sb zeroed""".split()


def build(nc, x_prompt, x_sample, c_prompt, c_sample, state_pool, state_conv, state_ssm, w_ada, b_ada,
          g_pre_mix, g_post_mix, g_pre_ffn, g_post_ffn, w_in, w_pool, pool_scale, conv_w, a_log, dt_bias,
          gdn_norm_w, w_out, router_w, router_b, w_gu, b_gu, w_down, b_down, consts,
          y_prompt, y_sample, pool_prompt, conv_prompt, ssm_prompt, pool_sample, conv_sample, ssm_sample):
    x1_dram = nc.dram_tensor("x1_scratch", (TOK, D), F32, kind="Internal").ap()
    gm_dram = nc.dram_tensor("gate_mod_scratch", (4, 32, 4, P), F32, kind="Internal").ap()
    ctx = ExitStack()
    with ctx:
        def sb(name, shape, dt=F32):
            return ctx.enter_context(nc.sbuf_tensor(name, shape, dt))

        s = {n: ctx.enter_context(nc.semaphore(n)) for n in SEMS}

        G0t, G1t, Dt = sb("gu_even", [P, 16384]), sb("gu_odd", [P, 16384]), sb("down_w", [P, 8192])
        WM = 11664
        Mt = sb("work", [P, WM])
        lmask_t = sb("level_masks_sb", [P, LEVEL_COLS // 2])
        lmask = lmask_t[:, :].bitcast(BF16)
        ps_t = ctx.enter_context(nc.psum_tensor("psum", [P, 8, 512], F32))
        G0, G1, DD, M = Arena(G0t, 16384), Arena(G1t, 16384), Arena(Dt, 8192), Arena(Mt, WM)

        def bank(b, n=1):
            return ps_t[:, b:b + n, :].rearrange("p b n -> p (b n)")

        ring = [G0.at(4096 * i, KT, 512) for i in range(RING)]
        qkvT = G1.at(0, CT, TOK)
        xn = G1.at(0, 3, D)
        junk = G1.at(3072, D)
        tokK, tokV = G1.at(5184, 3, GW), G1.at(7488, 3, GW)
        Lm = [G1.at(9792 + 768 * c, H, P) for c in range(2)]
        Tm = [G1.at(11328 + 768 * c, H, P) for c in range(2)]
        Um = [G1.at(12864 + 768 * c, H, P) for c in range(2)]
        QKT = [G1.at(14400 + 768 * c, H, P) for c in range(2)]
        Us, QKTs = G1.at(15936, H, NS), G1.at(15936 + 192, H, NS)
        Sp = Lm[0]
        gm_tok = [G1.at(11328, D), G1.at(11328, D), G1.at(12352, D)]
        fin_x = G0.at(0, 3, D)
        fin_g = [G0.at(3072, D), G0.at(3072, D), G0.at(4096, D)]
        fin_junk, fin_t = G0.at(5120, D), G0.at(6144, 3, D)
        xt = G1.at(0, D)
        mixjunk = G1.at(13376, D)
        c_sb, v1, v2 = G1.at(9792, D), G1.at(10816, P), G1.at(10944, P)
        hist_rows, phist_rows = G1.at(11072, CW), G1.at(13376, POOLW)
        uext = G1.at(13632, NU, PBUF + SEQ)
        uexs = G1.at(14176, NU, NSEQ * (PBUF + DSEQ)).rearrange("p m (b t) -> p m b t", b=NSEQ)
        win_a = G1.at(14480, NU, PBUF + SEQ)
        win_b = G1.at(15024, NU, PBUF + SEQ)
        win_sa = G1.at(15568, NU, NSEQ * 19).rearrange("p m (b t) -> p m b t", b=NSEQ)
        win_sb = G1.at(15872, NU, NSEQ * 19).rearrange("p m (b t) -> p m b t", b=NSEQ)
        cexs = DD.at(0, CT, NSEQ * (3 + DSEQ)).rearrange("p m (b t) -> p m b t", b=NSEQ)
        wpbd = DD.at(1008, NU, P)
        pooled = DD.at(1264, NU, TOK)
        b_row, gpost = DD.at(1840, 4, P), DD.at(2352, 4, P)
        modG = DD.at(2864, 4, P)
        tail_rows = DD.at(3376, NT * P)
        sq = [DD.at(5936 + 288 * i, TOK) for i in range(4)]
        s_tmp = DD.at(5936, CT, NS)
        s_tap = DD.at(7088, CT, NS)
        mraw = DD.at(7664, P)
        Ssm = DD.at(0, NSEQ, H, DH)
        kq_mask, vmask = DD.at(6144, NSEQ, 2 * NS), DD.at(6656, NSEQ, DH)
        seqmask = DD.at(7680, NSEQ, NS)
        w_out_sb = DD.at(0, KT, D)
        x_sb = M.at(0, 3, D)
        hT = M.at(3072, KT, TOK)
        Dm = M.at(3072, H, P)
        Ml = [M.at(3840 + 768 * c, H, P) for c in range(2)]
        oT = M.at(3072, H, TOK)
        z = M.at(5376, 3, GW)
        h2T = M.at(5376, KT, TOK)
        R0 = 7680
        ident, iota = M.at(R0, P), M.at(R0 + 128, P)
        F0 = R0 + 256
        ones, gdnw, upto, after, tril = [M.at(F0 + P * i, P) for i in range(5)]
        f = F0 + 5 * P
        upto_s, after_s, tril_s = [M.at(f + NS * i, NS) for i in range(3)]
        f += 3 * NS
        of_seq = M.at(f, NSEQ); f += NSEQ
        invwin = M.at(f, NU); f += NU
        invcnt = M.at(f, NU, 16); f += NU * 16
        poolT = M.at(f, NU, TOK); f += NU * TOK
        P1 = [M.at(f + 768 * c, H, P) for c in range(2)]
        tail = M.at(f, NT, TAIL)
        ab = M.at(f + NT * TAIL, 3, 2 * H); f += 1536
        cT = M.at(f, KT, 32)
        spt = [M.at(f + 18 * i, 3, H) for i in range(3)]
        gseq = M.at(f + 54, NSEQ, H)
        negeb, orr = M.at(f + 102, 3, H), M.at(f + 120, 3, H)
        f += 256
        assert f >= F0 + 3 * D
        modT = M.at(f, 4, KT * SEQS).rearrange("p g (k q) -> p g k q", k=KT); f += 4 * KT * SEQS
        vecT = M.at(f, 66 + 72); f += 138
        gg = M.at(f, 3, H); f += 18
        beta = M.at(f, 3, H); f += 18
        egc = M.at(f, 3, H); f += 18
        egr = M.at(f, 3, H); f += 18
        egl = M.at(f, 3, H); f += 18
        egls = M.at(f, NSEQ, H); f += 48
        alog = M.at(f, H); f += H
        dtb = M.at(f, H); f += H
        assert f <= WM, f
        acc = M.at(0, 3, D)
        h2 = M.at(F0, 3, D)
        lgT = M.at(0, TOK)
        lg = M.at(288, 3, NE)
        top8 = M.at(384, 3, 8)
        eqm = M.at(408, 3, NE)
        sel01 = M.at(504, 3, NE)
        exg = M.at(600, 3, NE)
        rk_t = M.at(696, 3, NE)
        rst = M.at(800, 16)
        cnt = M.at(816, NE)
        cntb = M.at(848, NE)
        cumf = M.at(880, NE + 2)
        rones, rbefore = M.at(1024, P), M.at(1152, P)
        bgu_rows = M.at(1280, 4, P)
        b_down_sb = M.at(3072, D)
        gT = M.at(4096, TOK)
        rw = M.at(4384, KT, NE)
        E0 = 3072
        xTm = M.at(E0, 4, 2, SLOTS)
        xg = M.at(E0 + 512, 512)
        gu_sb = M.at(E0 + 1024, 2, 512)
        hidg, hidu = gu_sb[:, 0, :], gu_sb[:, 1, :]
        sig = M.at(E0 + 2048, 512)
        y_sb = M.at(E0 + 2560, D)
        selGT = M.at(E0 + 3584, TOK)
        selA = M.at(E0 + 3872, 3, SLOTS)
        f = F0 + 3 * D
        bguT = M.at(f, NE * 2 * KT); f += NE * 2 * KT
        cur = M.at(f, 3, 3); f += 9
        f2 = E0 + 3872 + 192
        rank_gate = M.at(f2, 2, 3, NE)
        rank, gate = rank_gate[:, 0], rank_gate[:, 1]
        assert f2 + 6 * NE <= R0 and f <= WM
        selG = Arena(lmask_t, LEVEL_COLS // 2).at(0, 3, P)
        rvalid, rb_row = M.at(914, 2), M.at(916, NE)
        st, fst = sb("stats", [P, 16]), sb("final_stats", [P, 16])
        cum_i = sb("first_rounds", [1, NE + 2], I32)
        ends_i = sb("through_rounds", [1, NE], I32)

        def cc(name):
            off, n = CONST[name]
            return consts[:, off:off + n]

        def gate_rows(sp, g, dst, name):
            for t in range(2):
                row = gm_dram[:, :, 2 * g + t, :].rearrange("j q n -> q j n")
                sp.dma_start(dst[0].rearrange("p (t j n) -> p t j n", t=2, j=4)[:, t],
                             row[0:1].to_broadcast([P, 4, P])).then_inc(s[name], 16)
                for b in range(NSEQ):
                    sp.dma_start(dst[2].rearrange("p (t j n) -> p t j n", t=2, j=4)[DSEQ * b:DSEQ * b + DSEQ, t],
                                 row[1 + b:2 + b].to_broadcast([DSEQ, 4, P])).then_inc(s[name], 16)

        ORDER = (2, 0, 1)
        STEPS = [(0, 1)] + [(o, l) for l in range(1, LEVELS) for o in (1, 2)]

        def step_of(o, l):
            return STEPS.index((o, l)) + 1

        def last_step(o):
            return step_of(o, (SLEVELS if o == 0 else LEVELS) - 1)

        def buffers(o):
            if o == 0:
                return (M.at(4608 + 192, H, NS), M.at(4608, H, NS), Us, M.at(3840, H, NS),
                        P1[0].rearrange("p h t -> p (h t)")[:, 0:H * NS].rearrange("p (h t) -> p h t", h=H), QKTs, 0, 2)
            c = ORDER[o]
            return Lm[c], Tm[c], Um[c], Ml[c], P1[c], QKT[c], 4 * c, 4 * c + 2

        def dmat(o):
            return M.at(3072, H, NS) if o == 0 else Dm

        def masks(o):
            return (upto_s, after_s, tril_s) if o == 0 else (upto, after, tril)

        def heads(b, n, m=P):
            return bank(b, 2)[0:n, 0:H * m].rearrange("p (h t) -> p h t", h=H)

        def span(c):
            return slice(AT[c], AT[c] + ROWS[c])

        N_UNITS = 3 + NT + 3
        Z_UNITS = (0, 1, 2, N_UNITS - 3, N_UNITS - 2, N_UNITS - 1)

        def unit_slot(u):
            if u < 3:
                return ADA_FIRST, u == 2
            if u < 3 + NT:
                return ADA_FIRST + 1 + (u - 3) // 4, (u - 3) % 4 == 3
            return ADA_FIRST + N_IN - 1, u == N_UNITS - 1

        def unit_bank(u):
            return bank(4 + u % 4)

        def wait_unit(eng, u):
            slot, last = unit_slot(u)
            if last:
                eng.wait_ge(s["slot_used"], slot + 1)
            else:
                eng.wait_ge(s["proj_ps"], sum(not unit_slot(v)[1] for v in range(u + 1)))

        def wait_unit_read(eng, u):
            if u in Z_UNITS:
                eng.wait_ge(s["z_sb"], Z_UNITS.index(u) + 1)
            elif u < 3 + NU:
                eng.wait_ge(s["u_sb"], u - 3 + 1)
            else:
                eng.wait_ge(s["conv_done"], u - 3 - NU + 1)

        ADA_SLOTS = [n for n, (kind, _) in enumerate(RING_SLOTS) if kind == "ada"]
        TAIL_BANKS = (3, 0, 1, 2, 3)
        N_CONST, N_VEC, N_HIST, N_SMALL = 12, 5, 2, 20

        def levels(pe, mm, steps):
            for i in steps:
                o, l = STEPS[i]
                c = ORDER[o]
                n = ROWS[c]
                _, T, U, Mk, Pb, _, A, B = buffers(o)
                pe.wait_ge(s["ml"], i + 1)
                if i in (1, 2):
                    for name in ("lmat", "qkd", "qkdT", "u0"):
                        pe.wait_ge(s[name], 3)
                if i == 0:
                    pe.wait_ge(s["u0"], 1)
                    pe.wait_ge(s["lmat"], 1)
                if l > 1:
                    pe.wait_ge(s["tu_done"], step_of(o, l - 1))
                for h in range(H):
                    last = mm(heads(A, n, n)[:, h, :], Mk[0:n, h, :], U[0:n, h, :], start=True, stop=True)
                last.then_inc(s["p1_ps"], 1)
                if i in (0, 2) or i > 2 and o == 2:
                    for j in ([0] if i == 0 else [i - 1, i]):
                        finish_level(pe, mm, j)

        def finish_level(pe, mm, i):
            o, l = STEPS[i]
            n = ROWS[ORDER[o]]
            _, T, U, _, Pb, _, A, B = buffers(o)
            pe.wait_ge(s["p1"], i + 1)
            if i != 0 and l < LEVELS - 1:
                for h in range(H):
                    mm(heads(A, n, n)[:, h, :], Pb[0:n, h, :], T[0:n, h, :], start=True, stop=True)
            for h in range(H):
                last = mm(heads(B, n, n)[:, h, :], T[0:n, h, :], Pb[0:n, h, :], start=True, stop=True)
            last.then_inc(s["tn_ps"], 1)

        def experts_pe(pe, mm, tr):
            XB, SB, GB, TB, YB = 0, 1, 2, 4, 6

            def gather(i, last_read=None):
                pe.wait_ge(s["sel"], i)
                if last_read is not None:
                    pe.wait_ge(s["xTm"], last_read)
                for c in range(3):
                    for half in range(2):
                        last = mm(bank(XB)[64 * half:64 * half + 64, :], selA[:, c, :],
                                  h2[:, c, 512 * half:512 * half + 512], start=c == 0, stop=c == 2)
                last.then_inc(s["xg_ps"], 1)

            def scatter(i, first=False):
                pe.wait_ge(s["y_sb"], i)
                pe.wait_ge(s["sgT"], i)
                for c in range(3):
                    for half in range(2):
                        u = 2 * c + half
                        if u >= 2:
                            pe.wait_ge(s["acc_add"], 6 * i + (u - 1))
                        mm(bank(YB + half)[0:ROWS[c], :], selGT[:, span(c)], y_sb[:, 512 * half:512 * half + 512],
                           start=True, stop=True).then_inc(s["sc_ps"], 1)

            pe.wait_ge(s["acc_add"], 6)
            pe.wait_ge(s["cum"], 2)
            pe.wait_ge(s["bguT"], 1)
            gather(1)
            transposes_x(pe, tr, 1)
            with pe.Fori(0, NE // 2) as pair:
                for par in range(2):
                    gu = (G0, G1)[par].at(0, KT, 2 * FF)
                    dn = DD.at(0, KT, D)
                    first = pe.value_load(cum_i[0:1, bass.ds(pair * 2 + par, 1)], min_val=1, max_val=257)
                    end = pe.value_load(cum_i[0:1, bass.ds(pair * 2 + par + 1, 1)], min_val=2, max_val=257)
                    with pe.Fori(first, end) as i:
                        pe.wait_ge(s["xTm"], i)
                        for k in range(KT):
                            if k % 2 == 0:
                                pe.wait_ge(s[f"gu_in{par}{k // 2}"], pair * 16 + 16)
                            for half in range(2):
                                for t in range(2):
                                    col = FF * t + 512 * half
                                    last = mm(bank(GB + half)[64 * t:64 * t + 64, :], xTm[:, k % 4, k // 4, :],
                                              gu[:, k, col:col + 512], start=k == 0, stop=k == KT - 1)
                        last.then_inc(s["gu_ps"], 1)
                        gather(i + 1, i)
                        pe.wait_ge(s["gu_a"], i)
                        pe.wait_ge(s["gu_v"], i)
                        for k in range(KT):
                            last = tr(bank(TB + k // 4)[:, P * (k % 4):P * (k % 4) + P],
                                      gu_sb[:, k // 4, P * (k % 4):P * (k % 4) + P], ident)
                        last.then_inc(s["hid_ps"], 1)
                        transposes_x(pe, tr, i + 1)
                        scatter(i)
                        pe.wait_ge(s["selg"], i)
                        for c in range(3):
                            last = tr(bank(SB)[:, span(c)], selG[0:ROWS[c], c, :], ident[0:ROWS[c], 0:ROWS[c]])
                        last.then_inc(s["sgT_ps"], 1)
                        pe.wait_ge(s["hid"], i)
                        pe.wait_ge(s["acc_add"], 6 * i + 6)
                        for k in range(KT // 2):
                            for half in range(2):
                                for t in range(2):
                                    kk = k + KT // 2 * t
                                    if half == 0 and k == 0:
                                        pe.wait_ge(s[f"d_in{t}"], pair * 32 + (par + 1) * 16)
                                    last = mm(bank(YB + half)[64 * t:64 * t + 64, :],
                                              hidg.rearrange("p (k t) -> p k t", k=KT)[:, kk, :],
                                              dn[:, kk, 512 * half:512 * half + 512],
                                              start=k == 0, stop=k == KT // 2 - 1)
                        last.then_inc(s["y_ps"], 1)
            rounds = pe.value_load(cum_i[0:1, NE:NE + 1], min_val=2, max_val=257)
            scatter(rounds)

        def transposes_x(pe, tr, i):
            pe.wait_ge(s["xg"], i)
            for j in range(4):
                last = tr(bank(0)[:, P * j:P * j + P], xg[:, P * j:P * j + P], ident)
            last.then_inc(s["xTm_ps"], 1)

        def rstd(act, fn, own, t, n):
            act.wait_ge(s["ms"], n)
            own(fn(t[:, 6:9], t[:, 3:6], ACT.Ln))
            fn(t[:, 9:12], t[:, 6:9], ACT.Exp, scale=-0.5).then_inc(s["rstd"], 1)

        block = ctx.enter_context(nc.Block())

        @block.sync
        def _(sp):
            sp.dma_start(x_sb[:, 0:2, :], x_prompt.rearrange("a (b p) d -> p (a b) d", p=P)).then_inc(s["x_in"], 16)
            sp.dma_start(x_sb[0:NS, 2, :], x_sample.rearrange("b t d -> (b t) d")).then_inc(s["x_in"], 16)
            sp.dma_start(ident, cc("ident")).then_inc(s["const_in"], 16)
            sp.dma_start(c_sb[0:1, :], c_prompt).then_inc(s["c_in"], 16)
            sp.dma_start(c_sb[1:SEQS, :], c_sample).then_inc(s["c_in"], 16)
            for name, dst in (("ones", ones), ("upto", upto), ("after", after), ("tril", tril), ("upto_s", upto_s),
                              ("after_s", after_s), ("tril_s", tril_s), ("of_seq", of_seq), ("invwin", invwin)):
                sp.dma_start(dst, cc(name)).then_inc(s["const_in"], 16)
            sp.dma_start(iota, cc("iota")).then_inc(s["const_in"], 16)
            sp.dma_start(invcnt, cc("invcnt").rearrange("p (m t) -> p m t", m=NU)).then_inc(s["const_in"], 16)

            def ring_load(n):
                kind, g = RING_SLOTS[n]
                if n >= RING:
                    sp.wait_ge(s["slot_used"], n - RING + 1)
                c0, w = (512 * g, 512) if kind == "ada" else IN_SLOTS[g]
                src = (w_ada if kind == "ada" else w_in)[0][:, c0:c0 + w].rearrange("(k p) n -> p k n", p=P)
                sp.dma_start(ring[n % RING][:, :, 0:w], src).then_inc(s[f"ring{n % RING}"], 16)

            for n in range(len(RING_SLOTS)):
                ring_load(n)
                if n == 1:
                    vr = b_ada.rearrange("a (r n) -> (a r) n", n=P)
                    sp.dma_start(v1[0:48, :], vr).then_inc(s["vec_in"], 16)
                    sp.dma_start(v1[48:56, :], g_pre_mix.rearrange("a (r n) -> (a r) n", n=P)).then_inc(s["vec_in"], 16)
                    sp.dma_start(v1[56:64, :], g_pre_ffn.rearrange("a (r n) -> (a r) n", n=P)).then_inc(s["vec_in"], 16)
                    sp.dma_start(v1[64:66, :], pool_scale.rearrange("a (r n) -> (a r) n", n=P)).then_inc(s["vec_in"], 16)
                    sp.dma_start(v2[0:72, :], conv_w.rearrange("a j (r n) -> (a j r) n", n=P)).then_inc(s["vec_in"], 16)
            sp.wait_ge(s["slot_used"], len(RING_SLOTS))
            gu_view = w_gu[0].rearrange("e (q j p) n -> e q p j n", p=P, j=2)
            d_view = w_down[0].rearrange("e (q j p) n -> e q p j n", p=P, j=4)
            gu_buf = [G0.at(0, KT, 2 * FF), G1.at(0, KT, 2 * FF)]
            d_buf = DD.at(0, KT, D)

            for q in range(4):
                sp.dma_start(gu_buf[0][:, 2 * q:2 * q + 2, :], gu_view[0, q]).then_inc(s[f"gu_in0{q}"], 16)

            sp.wait_ge(s["tail_rows"], 5)
            tr = tail_rows[0:TAIL, :]
            sp.dma_start(pool_prompt[0, 0], tr[0:PBUF, 0:POOLW]).then_inc(s["tail_st"], 16)
            sp.dma_start(conv_prompt[0, 0], tr[PBUF - 3:PBUF, POOLW:]).then_inc(s["tail_st"], 16)
            for b in range(NSEQ):
                r = PBUF + DSEQ * b
                sp.dma_start(pool_sample[0, b, PBUF - DSEQ:PBUF], tr[r:r + DSEQ, 0:POOLW]).then_inc(s["tail_st"], 16)
                sp.dma_start(conv_sample[0, b], tr[r + 1:r + DSEQ, POOLW:]).then_inc(s["tail_st"], 16)
            sp.dma_start(pool_sample[0, :, 0:PBUF - DSEQ, :], state_pool[0, :, DSEQ:PBUF, :]).then_inc(s["tail_st"], 16)
            sp.wait_ge(s["tail_st"], 16 * (3 + 2 * NSEQ))
            sp.wait_ge(s["modG_st"], 16)
            sp.wait_ge(s["pool_ps"], 2)
            sp.wait_ge(s["s_taps"], 1)
            sp.wait_ge(s["norm_ps"], 12)
            for b in range(NSEQ):
                sp.dma_start(Ssm[:, b], state_ssm[0, b].rearrange("h k v -> k h v")).then_inc(s["ssm_in"], 16)
            sp.dma_start(seqmask, cc("seqmask").rearrange("p (b t) -> p b t", b=NSEQ)).then_inc(s["ssm_in"], 16)

            sp.wait_ge(s["s_new"], H)
            sp.dma_start(ssm_sample[0].rearrange("b h k v -> k b h v"), Ssm).then_inc(s["ssm_out"], 16)
            sp.wait_ge(s["ssm_out"], 16)
            sp.dma_start(w_out_sb, w_out[0].rearrange("(k p) n -> p k n", p=P)).then_inc(s["wout_in"], 16)
            sp.wait_ge(s["vn_ps"], 3)
            gate_rows(sp, 0, gm_tok, "gm_in")
            sp.wait_ge(s["s_new"], H + 1)
            sp.dma_start(ssm_prompt[0, 0].rearrange("h k v -> k h v"), Sp).then_inc(s["ssm_out"], 16)

            for c in range(3):
                sp.wait_ge(s["x1"], c + 1)
                n = ROWS[c]
                sp.dma_start(x1_dram[AT[c]:AT[c] + n, :], x_sb[0:n, c, :]).then_inc(s["x1_st"], 16)
            for q in range(2):
                sp.dma_start(d_buf[:, 4 * q:4 * q + 4, :], d_view[0, q]).then_inc(s[f"d_in{q}"], 16)
            sp.wait_ge(s["ssm_out"], 32)
            sp.wait_ge(s["ssq"], 9)
            for q in range(4):
                sp.dma_start(gu_buf[1][:, 2 * q:2 * q + 2, :], gu_view[1, q]).then_inc(s[f"gu_in1{q}"], 16)
            sp.wait_ge(s["x1_st"], 48)
            sp.wait_ge(s["xn2"], 3)
            sp.dma_start(rones, cc("ones")).then_inc(s["rt_in"], 16)
            sp.dma_start(rvalid, cc("valid")).then_inc(s["rt_in"], 16)
            sp.dma_start(rbefore, cc("before")).then_inc(s["rt_in"], 16)
            sp.dma_start(rb_row[0:1, :], router_b).then_inc(s["rt_in"], 16)
            sp.dma_start(bgu_rows, b_gu[0].rearrange("e (c n) -> (e c) n", n=P).rearrange("(q p) n -> p q n", p=P)
                         ).then_inc(s["rt_in"], 16)
            sp.dma_start(rw, router_w[0].rearrange("(k p) n -> p k n", p=P)).then_inc(s["rt_in"], 16)
            sp.dma_start(b_down_sb[0:NE, :], b_down[0]).then_inc(s["rt_in"], 16)

            sp.wait_ge(s["cum"], 2)

            def load_gu(par, nxt, rounds):
                for q in range(4):
                    if q == 0:
                        sp.wait_ge(s["gu_ps"], rounds)
                    sp.dma_start(gu_buf[par][:, 2 * q:2 * q + 2, :],
                                 gu_view[bass.ds(nxt, 1), q].rearrange("e p j n -> p (e j) n")
                                 ).then_inc(s[f"gu_in{par}{q}"], 16)

            def load_d(nxt, rounds):
                for q in range(2):
                    if q == 0:
                        sp.wait_ge(s["y_ps"], rounds)
                    sp.dma_start(d_buf[:, 4 * q:4 * q + 4, :],
                                 d_view[bass.ds(nxt, 1), q].rearrange("e p j n -> p (e j) n")
                                 ).then_inc(s[f"d_in{q}"], 16)

            with sp.Fori(0, NE // 2 - 1) as pair:
                for par in range(2):
                    through = sp.value_load(ends_i[0:1, bass.ds(pair * 2 + par, 1)], min_val=1, max_val=256)
                    load_gu(par, pair * 2 + par + 2, through)
                    load_d(pair * 2 + par + 1, through)
            through = sp.value_load(ends_i[0:1, NE - 2:NE - 1], min_val=1, max_val=256)
            load_d(NE - 1, through)

            sp.wait_ge(s["gu_ps"], through)
            sp.dma_start(fin_x[:, 0:2, :], x1_dram[0:SEQ].rearrange("(b p) d -> p b d", p=P)).then_inc(s["fin_in"], 16)
            sp.dma_start(fin_x[0:NS, 2, :], x1_dram[SEQ:TOK]).then_inc(s["fin_in"], 16)
            gate_rows(sp, 1, fin_g, "fin_in")
            for c in range(3):
                sp.wait_ge(s["fin_y"], c + 1)
                dst = y_prompt[0, P * c:P * c + P, :] if c < 2 else y_sample.rearrange("b t d -> (b t) d")
                sp.dma_start(dst, fin_x[0:ROWS[c], c, :]).then_inc(s["y_st"], 16)
            sp.wait_ge(s["y_st"], 48)

        @block.tensor
        def _(pe):
            mm, tr = pe.matmul, pe.transpose

            pe.wait_ge(s["const_in"], 16 * N_CONST)
            pe.wait_ge(s["c_silu"], 1)
            for k in range(KT):
                last = tr(bank(0)[:, SEQS * k:SEQS * (k + 1)], c_sb[0:SEQS, P * k:P * (k + 1)], ident[0:SEQS, 0:SEQS])
            last.then_inc(s["setup_ps"], 1)
            pe.wait_ge(s["vec_in"], 16 * N_VEC)
            tr(bank(1)[:, 0:66], v1[0:66, :], ident[0:66, 0:66])
            tr(bank(1)[:, 66:138], v2[0:72, :], ident[0:72, 0:72]).then_inc(s["setup_ps"], 1)
            pe.wait_ge(s["hist_in"], 16 * N_HIST)
            for m in range(CT):
                last = tr(bank(2)[:, 24 * m:24 * m + 24], hist_rows[0:24, P * m:P * m + P], ident[0:24, 0:24])
            last.then_inc(s["setup_ps"], 1)
            for m in range(NU):
                last = tr(bank(3)[:, 120 * m:120 * m + 120], phist_rows[0:120, P * m:P * m + P], ident[0:120, 0:120])
            last.then_inc(s["setup_ps"], 1)

            pe.wait_ge(s["xn"], 3)
            pe.wait_ge(s["setup_sb"], 4)
            for k in range(KT):
                last = tr(bank(3)[:, 256 + NS * k:256 + NS * (k + 1)], xn[0:NS, 2, P * k:P * k + P], ident[0:NS, 0:NS])
            last.then_inc(s["xT_ps"], 1)
            for k in range(KT):
                for c in range(2):
                    at = 256 * (k % 2) + P * c
                    last = tr(bank(4 + k // 2)[:, at:at + P], xn[:, c, P * k:P * k + P], ident)
                if k % 2:
                    last.then_inc(s["xT_ps"], 1)

            def ada(i):
                n = ADA_SLOTS[i]
                pe.wait_ge(s[f"ring{n % RING}"], 16 * (n // RING + 1))
                if i < 2:
                    pe.wait_ge(s["setup_sb"], 1)
                    pe.wait_ge(s["setup_sb"], 2)
                else:
                    pe.wait_ge(s["mod_sb"], i - 1)
                for k in range(KT):
                    for j in range(4):
                        last = mm(bank(i % 2)[32 * j:32 * j + 32, 0:P], cT[:, k, :],
                                  ring[n % RING][:, k, P * j:P * j + P], start=k == 0, stop=k == KT - 1)
                last.then_inc(s["slot_used"], 1)

            MODT = [0, 1, 2, 3, 6, 7, 8, 9]

            def ada_T(i):
                t = MODT.index(i)
                pe.wait_ge(s["mod_sb"], i + 1)
                if t == 0:
                    pe.wait_ge(s["setup_sb"], 3)
                if t == 4:
                    pe.wait_ge(s["modT"], 1)
                tr(bank(2)[:, P * (t % 4):P * (t % 4) + P], mraw, ident).then_inc(s["modT_ps"], 1)

            for i in range(ADA_FIRST):
                ada(i)
                ada_T(i)

            pe.wait_ge(s["hT_a"], KT)
            pe.wait_ge(s["hT_s"], 1)
            for u in range(N_UNITS):
                slot, last_of_slot = unit_slot(u)
                pe.wait_ge(s[f"ring{slot % RING}"], 16 * (slot // RING + 1))
                if u >= 4:
                    wait_unit_read(pe, u - 4)
                w = ring[slot % RING]
                for k in range(KT):
                    if u in Z_UNITS:
                        c, cols = Z_UNITS.index(u) % 3, (IN_SLOTS[0][1] if u < 3 else 512)
                        last = mm(unit_bank(u)[0:ROWS[c], 0:cols], hT[:, k, span(c)], w[:, k, 0:cols],
                                  start=k == 0, stop=k == KT - 1)
                    else:
                        i = (u - 3) % 4
                        last = mm(unit_bank(u)[:, 0:TOK], w[:, k, P * i:P * i + P], hT[:, k, :],
                                  start=k == 0, stop=k == KT - 1)
                last.then_inc(s["slot_used" if last_of_slot else "proj_ps"], 1)

            for i in range(ADA_FIRST, 12):
                ada(i)
                if i in MODT:
                    ada_T(i)

            for q in range(5):
                b = TAIL_BANKS[q]
                if q == 0:
                    pe.wait_ge(s["hT_s"], 1)
                elif q < 3:
                    pe.wait_ge(s["mod_sb"], 12)
                elif q == 3:
                    pe.wait_ge(s["modT"], 2)
                else:
                    pe.wait_ge(s["tail_rows"], 1)
                for i in range(4):
                    last = tr(bank(b)[0:TAIL, P * i:P * i + P], tail[:, 4 * q + i, :], ident)
                last.then_inc(s["tailT_ps"], 1)

            pe.wait_ge(s["pooled"], 1)
            pe.wait_ge(s["wpool_in"], 64)
            wait_unit_read(pe, N_UNITS - 1)
            for m in range(NU):
                mm(bank(4 + m)[:, 0:TOK], wpbd[:, m, :], pooled[:, m, :], start=True, stop=True
                   ).then_inc(s["pool_ps"], 1)

            for h in range(2 * H):
                pe.wait_ge(s["sq"], h + 1)
                if h < 2:
                    pe.wait_ge(s["poolT"], h + 1)
                if h >= 4:
                    pe.wait_ge(s["qk_n"], h - 3)
                mm(bank(4 + h % 4)[:, 0:TOK], ones, sq[h % 4], start=True, stop=True).then_inc(s["norm_ps"], 1)

            pe.wait_ge(s["gates"], 1)
            pe.wait_ge(s["gates"], 2)
            pe.wait_ge(s["tail_rows"], 5)
            for c in range(2):
                mm(bank(3)[:, 8 * c:8 * c + H], upto, gg[:, c, :], start=True, stop=True)
                mm(bank(3)[:, 32 + 8 * c:32 + 8 * c + H], after, gg[:, c, :], start=True, stop=True)
                mm(bank(3)[:, 64 + 8 * c:64 + 8 * c + H], ones, gg[:, c, :], start=True, stop=True)
            mm(bank(3)[0:NS, 16:16 + H], upto_s[0:NS, :], gg[0:NS, 2, :], start=True, stop=True)
            mm(bank(3)[0:NS, 48:48 + H], after_s[0:NS, :], gg[0:NS, 2, :], start=True, stop=True)
            mm(bank(3)[:, 96:96 + NSEQ * H], ones[0:NS, :], gseq[0:NS].rearrange("p b h -> p (b h)"),
               start=True, stop=True).then_inc(s["gate_ps"], 1)

            for g in range(6):
                c, b = g % 3, 4 * (g % 2)
                pe.wait_ge(s["qk_n"], 2 * H)
                pe.wait_ge(s["s_silu"], 1)
                if g >= 2:
                    pe.wait_ge(s["kv_tok"], g - 1)
                for h in range(H):
                    src = qkvT[:, (12 if g < 3 else 6) + h, span(c)]
                    last = tr(bank(b, 2)[0:ROWS[c], P * h:P * h + P], src, ident)
                last.then_inc(s["kvT_ps"], 1)

            for o in range(3):
                c = ORDER[o]
                n = ROWS[c]
                L, T, U, Mk, Pb, QT, A, B = buffers(o)
                if o == 0:
                    pe.wait_ge(s["kv_tok"], 6)
                    pe.wait_ge(s["egates"], 1)
                else:
                    pe.wait_ge(s["u0"], o)
                pe.wait_ge(s["ga"], o + 1)
                ga = Mk[0:n].rearrange("p h t -> p (h t)")
                for lo in range(0, H * n, 512):
                    hi = min(lo + 512, H * n)
                    last = mm(bank(0, 2)[0:n, lo:hi], masks(o)[0][0:n, 0:n], ga[:, lo:hi], start=True, stop=True)
                last.then_inc(s["diff_ps"], 1)
                if o >= 1:
                    pe.wait_ge(s["lmat"], o)
                for h in range(H):
                    last = mm(heads(2, n, n)[:, h, :], qkvT[:, H + h, span(c)], qkvT[:, H + h, span(c)],
                              start=True, stop=True)
                last.then_inc(s["kk_ps"], 1)
                if o >= 1:
                    pe.wait_ge(s["qkd"], o)
                for h in range(H):
                    last = mm(heads(4, n, n)[:, h, :], qkvT[:, h, span(c)], qkvT[:, H + h, span(c)],
                              start=True, stop=True)
                last.then_inc(s["qk_ps"], 1)
                pe.wait_ge(s["qkd"], o + 1)
                if o >= 1:
                    pe.wait_ge(s["qkdT"], o)
                for h in range(H):
                    last = tr(heads(6, n, n)[:, h, :], dmat(o)[0:n, h, :], ident[0:n, 0:n])
                last.then_inc(s["qkdT_ps"], 1)
                pe.wait_ge(s["t0"], o + 1)
                pe.wait_ge(s["dexp"], o + 1)
                for h in range(H):
                    last = tr(heads(0, n, n)[:, h, :], T[0:n, h, :], ident[0:n, 0:n])
                last.then_inc(s["u0_ps"], 1)
                if o == 0:
                    levels(pe, mm, [0])
            levels(pe, mm, range(1, len(STEPS)))

            pe.wait_ge(s["ssm_in"], 16 * (NSEQ + 1))
            pe.wait_ge(s["tu_done"], len(STEPS))
            for h in range(H):
                pe.wait_ge(s["kqm"], h + 1)
                for b in range(NSEQ):
                    last = mm(bank(0, 2)[0:2 * NS, P * h:P * h + P], kq_mask[:, b, :], Ssm[:, b, h, :],
                              start=b == 0, stop=b == NSEQ - 1)
                last.then_inc(s["ks_ps"], 1)

            def new_values(o):
                n, c, U = ROWS[ORDER[o]], ORDER[o], buffers(o)[2]
                pe.wait_ge(s["rr"], o + 1)
                for h in range(H):
                    last = mm(heads(2, n)[:, h, :], U[0:n, h, :], tokV[0:n, c, P * h:P * h + P], start=True, stop=True)
                last.then_inc(s["vn_ps"], 1)

            def outputs(o):
                n, c, QT = ROWS[ORDER[o]], ORDER[o], buffers(o)[5]
                pe.wait_ge(s["vn"], o + 1)
                if o >= 1:
                    pe.wait_ge(s["o_tok"], o)
                for h in range(H):
                    last = mm(heads(4, n)[:, h, :], QT[0:n, h, :], tokV[0:n, c, P * h:P * h + P], start=True, stop=True)
                last.then_inc(s["o_ps"], 1)

            def state_products(o):
                c = ORDER[o]
                pe.wait_ge(s["kdec"], o + 1)
                for h in range(H):
                    last = mm(heads(0, P)[:, h, :], tokK[:, c, P * h:P * h + P], tokV[:, c, P * h:P * h + P],
                              start=True, stop=True)
                last.then_inc(s["s_ps"], 1)

            new_values(0)
            outputs(0)
            pe.wait_ge(s["kdec"], 1)
            for h in range(H):
                pe.wait_ge(s["vmask"], h + 1)
                if h >= 1:
                    pe.wait_ge(s["s_new"], h)
                vm = vmask.rearrange("p b v -> p (b v)")
                for half in range(2):
                    last = mm(bank(6 + half), tokK[:, 2, P * h:P * h + P], vm[:, 512 * half:512 * half + 512],
                              start=True, stop=True)
                last.then_inc(s["s_ps"], 1)
            new_values(1)
            pe.wait_ge(s["qs_sb"], 1)
            outputs(1)
            state_products(1)
            pe.wait_ge(s["sp_e"], 1)
            for h in range(H):
                last = mm(heads(0, P)[:, h, :], qkvT[:, H + h, span(1)], Sp[:, h, :], start=True, stop=True)
            last.then_inc(s["ks_ps"], 1)
            pe.wait_ge(s["s_new"], H)
            for h in range(H):
                last = mm(heads(6, P)[:, h, :], qkvT[:, h, span(1)], Sp[:, h, :], start=True, stop=True)
            last.then_inc(s["ks_ps"], 1)
            new_values(2)
            outputs(2)
            state_products(2)

            for o in range(3):
                c = ORDER[o]
                n = ROWS[c]
                pe.wait_ge(s["gated"], o + 1)
                pe.wait_ge(s["vn"], 3)
                if o >= 1:
                    pe.wait_ge(s["oT"], o)
                for h in range(H):
                    last = tr(bank(2, 2)[:, n * h:n * h + n], z[0:n, c, P * h:P * h + P], ident[0:n, 0:n])
                last.then_inc(s["oT_ps"], 1)

            pe.wait_ge(s["oT"], 3)
            pe.wait_ge(s["wout_in"], 16)
            pe.wait_ge(s["o_tok"], 3)
            pe.wait_ge(s["qs_sb"], 2)
            pe.wait_ge(s["s_new"], H + 1)
            for c in range(3):
                b = (4, 6, 0)[c]
                for k in range(KT):
                    lhsT = poolT[:, k, span(c)] if k < NU else oT[:, k - NU, span(c)]
                    for half in range(2):
                        last = mm(bank(b + half)[0:ROWS[c], :], lhsT, w_out_sb[:, k, 512 * half:512 * half + 512],
                                  start=k == 0, stop=k == KT - 1)
                last.then_inc(s["mix_ps"], 1)

            pe.wait_ge(s["xn2"], 3)
            for k in range(KT):
                last = tr(bank(2)[:, NS * k:NS * (k + 1)], h2[0:NS, 2, P * k:P * k + P], ident[0:NS, 0:NS])
            last.then_inc(s["x2T_ps"], 1)
            for k in range(KT):
                for c in range(2):
                    at = 256 * (k % 2) + P * c
                    last = tr(bank(4 + k // 2)[:, at:at + P], h2[:, c, P * k:P * k + P], ident)
                if k % 2:
                    last.then_inc(s["x2T_ps"], 1)
            pe.wait_ge(s["h2T"], KT + 1)
            pe.wait_ge(s["rt_in"], 16 * 7)
            for k in range(KT):
                last = mm(bank(3)[0:NE, 0:TOK], rw[:, k, :], h2T[:, k, :], start=k == 0, stop=False)
            for c in range(3):
                last = mm(bank(3)[0:NE, span(c)], rb_row[0:1, :], rones[0:1, 0:ROWS[c]], start=False, stop=c == 2)
            last.then_inc(s["router_ps"], 1)
            for c in range(3):
                for k in range(KT):
                    last = tr(bank((4, 6, 0)[c] + k // 4)[0:ROWS[c], P * (k % 4):P * (k % 4) + P],
                              h2T[:, k, span(c)], ident)
                last.then_inc(s["h2_ps"], 1)
            pe.wait_ge(s["rl_sb"], 1)
            for c in range(3):
                last = tr(bank(2)[0:ROWS[c], NE * c:NE * c + NE], lgT[0:NE, span(c)], ident[0:NE, 0:NE])
            last.then_inc(s["router_ps"], 1)
            pe.wait_ge(s["h2"], 3)
            for q in range(4):
                last = tr(bank(4)[:, P * q:P * q + P], bgu_rows[:, q, :], ident)
            last.then_inc(s["router_ps"], 1)
            pe.wait_ge(s["top_e"], 1)
            for c in range(3):
                for e in range(c + 1):
                    last = mm(bank(5)[0:P, NE * c:NE * c + NE], rbefore if e == c else rones, sel01[:, e, :],
                              start=e == 0, stop=e == c)
            last.then_inc(s["router_ps"], 1)
            for c in range(3):
                last = mm(bank(6)[:, 0:NE], rones, sel01[:, c, :], start=c == 0, stop=c == 2)
            last.then_inc(s["router_ps"], 1)
            pe.wait_ge(s["gate_done"], 1)
            for c in range(3):
                last = tr(bank(7)[0:NE, AT[c]:AT[c] + ROWS[c]], gate[0:ROWS[c], c, :], ident[0:ROWS[c], 0:ROWS[c]])
            last.then_inc(s["router_ps"], 1)
            pe.wait_ge(s["gT"], 1)
            for c in range(3):
                for half in range(2):
                    if c >= 1:
                        pe.wait_ge(s["acc_add"], 2 * c - 1 + half)
                    mm(bank(half)[0:ROWS[c], :], gT[0:NE, span(c)],
                       b_down_sb[0:NE, 512 * half:512 * half + 512], start=True, stop=True).then_inc(s["sc_ps"], 1)

            experts_pe(pe, mm, tr)

        @block.scalar
        def _(act):
            fn = act.activation
            own = Chain(act, s["ch_act"])

            act.wait_ge(s["zeroed"], 1)
            act.dma_start(hist_rows[0:24, :], state_conv[0].rearrange("b t c -> (b t) c")).then_inc(s["hist_in"], 16)
            act.dma_start(phist_rows[0:120, :], state_pool[0].rearrange("b t c -> (b t) c")).then_inc(s["hist_in"], 16)
            for g in range(4):
                r = 64 * (g % 2)
                act.dma_start(wpbd[r:r + 64, g // 2, r:r + 64], w_pool[0, g]).then_inc(s["wpool_in"], 16)
            act.dma_start(alog, a_log.to_broadcast([P, H])).then_inc(s["small_in"], 16)
            act.dma_start(dtb, dt_bias.to_broadcast([P, H])).then_inc(s["small_in"], 16)
            act.dma_start(gdnw, gdn_norm_w.to_broadcast([P, DH])).then_inc(s["small_in"], 16)
            ba = b_ada.rearrange("a (u j n) -> a u j n", j=4, n=P)
            for j in range(4):
                rows = slice(32 * j, 32 * j + 32)
                for g in range(2):
                    u = 4 + 6 * g
                    act.dma_start(b_row[rows, 2 * g:2 * g + 2, :], ba[:, u:u + 2, j].to_broadcast([32, 2, P])
                                  ).then_inc(s["small_in"], 16)
                    gp = (g_post_mix, g_post_ffn)[g].rearrange("a (u j n) -> a u j n", j=4, n=P)
                    act.dma_start(gpost[rows, 2 * g:2 * g + 2, :], gp[:, :, j].to_broadcast([32, 2, P])
                                  ).then_inc(s["small_in"], 16)
            act.dma_start(lmask_t[:, :], cc("levels")).then_inc(s["small_in"], 16)

            act.wait_ge(s["c_in"], 32)
            fn(c_sb[0:SEQS, :], c_sb[0:SEQS, :], ACT.Silu).then_inc(s["c_silu"], 1)
            act.wait_ge(s["x_in"], 32)
            act.wait_ge(s["eps_set"], 1)
            for c in range(3):
                n = ROWS[c]
                if c:
                    act.wait_ge(s["ssq"], c)
                fn(junk[0:n, :], x_sb[0:n, c, :], ACT.Square, accum_out=st[0:n, c:c + 1]).then_inc(s["ssq"], 1)
            rstd(act, fn, own, st, 1)

            act.wait_ge(s["modT"], 1)
            for k in range(KT):
                act.wait_ge(s["xT_ps"], 2 + k // 2)
                fn(hT[:, k, 0:SEQ], bank(4 + k // 2)[:, 256 * (k % 2):256 * (k % 2) + 256], ACT.Identity,
                   scale=modT[:, 1, k, 0:1], bias=modT[:, 0, k, 0:1]).then_inc(s["hT_a"], 1)

            def silu_tile(h):
                act.wait_ge(s["conv_done"], h + 1)
                fn(qkvT[:, h, 0:SEQ], qkvT[:, h, 0:SEQ], ACT.Silu).then_inc(s["silu_done"], 1)

            act.wait_ge(s["setup_sb"], 4)
            for u in range(N_UNITS):
                wait_unit(act, u)
                ps = unit_bank(u)
                if u in Z_UNITS:
                    c = Z_UNITS.index(u) % 3
                    n = ROWS[c]
                    if u < 3:
                        fn(z[0:n, c, 512:GW], ps[0:n, 0:256], ACT.Silu)
                        act.copy(ab[0:n, c, :], ps[0:n, 256:268]).then_inc(s["z_sb"], 1)
                    else:
                        fn(z[0:n, c, 0:512], ps[0:n, 0:512], ACT.Silu).then_inc(s["z_sb"], 1)
                elif u < 3 + NU:
                    m = u - 3
                    act.copy(tail[:, m, :], ps[:, SEQ - PBUF:TOK])
                    act.copy(uext[:, m, PBUF:], ps[:, 0:SEQ])
                    act.copy(uexs[:, m, :, PBUF:], ps[:, SEQ:TOK].rearrange("p (b t) -> p b t", b=NSEQ)
                             ).then_inc(s["u_sb"], 1)
                else:
                    h = u - 3 - NU
                    act.copy(tail[:, NU + h, :], ps[:, SEQ - PBUF:TOK])
                    act.copy(cexs[:, h, :, 3:], ps[:, SEQ:TOK].rearrange("p (b t) -> p b t", b=NSEQ))
                    tap = 66 + 3 * CT + h
                    fn(qkvT[:, h, 0:SEQ], ps[:, 0:SEQ], ACT.Identity, scale=vecT[:, tap:tap + 1]
                       ).then_inc(s["tap3"], 1)
                    if h >= 1:
                        silu_tile(h - 1)
            silu_tile(CT - 1)
            act.wait_ge(s["s_taps"], 1)
            fn(qkvT[:, :, SEQ:TOK], s_tap, ACT.Silu).then_inc(s["s_silu"], 1)

            for q in range(5):
                act.wait_ge(s["tailT_ps"], q + 1)
                act.copy(tail_rows[0:TAIL, 512 * q:512 * q + 512], bank(TAIL_BANKS[q])[0:TAIL, :]
                         ).then_inc(s["tail_rows"], 1)
            for m in range(NU):
                act.wait_ge(s["pool_ps"], m + 1)
                fn(poolT[:, m, :], bank(4 + m)[:, 0:TOK], ACT.Identity, scale=vecT[:, 64 + m:65 + m]
                   ).then_inc(s["poolT"], 1)
            act.wait_ge(s["modG"], 4)
            act.dma_start(gm_dram.rearrange("j q u n -> (j q) u n"), modG).then_inc(s["modG_st"], 16)

            act.wait_ge(s["softplus_v"], 1)
            act.wait_ge(s["small_in"], 16 * N_SMALL)
            fn(spt[1], spt[1], ACT.Exp)
            fn(beta, ab[:, :, H:2 * H], ACT.Exp, scale=-1.0)
            fn(alog, alog, ACT.Exp).then_inc(s["softplus_a"], 1)
            act.wait_ge(s["softplus_v"], 2)
            fn(spt[1], spt[1], ACT.Ln).then_inc(s["softplus_a"], 1)

            for h in range(2 * H):
                act.wait_ge(s["norm_ps"], h + 1)
                ps = bank(4 + h % 4)[:, 0:TOK]
                own(fn(ps, ps, ACT.Ln, bias=st[:, 12:13]))
                fn(ps, ps, ACT.Exp, scale=-0.5).then_inc(s["n_exp"], 1)

            act.wait_ge(s["gate_ps"], 1)
            ps = bank(3)
            two = lambda at: ps[:, at:at + 16].rearrange("p (c h) -> p c h", c=2)[:, :, 0:H]
            fn(egc[:, 0:2, :], two(0), ACT.Exp)
            fn(egr[:, 0:2, :], two(32), ACT.Exp)
            fn(egl[:, 0:2, :], two(64), ACT.Exp)
            fn(egc[0:NS, 2, :], ps[0:NS, 16:16 + H], ACT.Exp)
            fn(egr[0:NS, 2, :], ps[0:NS, 48:48 + H], ACT.Exp)
            fn(egls, ps[:, 96:96 + NSEQ * H].rearrange("p (b h) -> p b h", b=NSEQ), ACT.Exp
               ).then_inc(s["egates"], 1)

            for g in range(6):
                c = g % 3
                n = ROWS[c]
                act.wait_ge(s["kvT_ps"], g + 1)
                act.copy((tokV if g < 3 else tokK)[0:n, c, :], bank(4 * (g % 2), 2)[0:n, 0:GW]
                         ).then_inc(s["kv_tok"], 1)

            for o in range(3):
                n = ROWS[ORDER[o]]
                L, T, U, Mk, Pb, QT, A, B = buffers(o)
                act.wait_ge(s["diff_ps"], o + 1)
                if o >= 1:
                    act.wait_ge(s["qkdT_ps"], o)
                fn(dmat(o)[0:n], heads(0, n, n), ACT.Exp).then_inc(s["dexp"], 1)
                act.wait_ge(s["qkdT_ps"], o + 1)
                act.copy(QT[0:n], heads(6, n, n)).then_inc(s["qkdT"], 1)
                act.wait_ge(s["u0_ps"], o + 1)
                act.copy(U[0:n], heads(0, n, n)).then_inc(s["u0"], 1)
                if o == 0:
                    act.wait_ge(s["p1_ps"], 1)
                    act.wait_ge(s["tailT_ps"], 5)
                    act.copy(Pb[0:n], heads(A, n, n)).then_inc(s["p1"], 1)
            for i in range(1, len(STEPS)):
                o = STEPS[i][0]
                n = ROWS[ORDER[o]]
                _, _, _, _, Pb, _, A, _ = buffers(o)
                act.wait_ge(s["p1_ps"], i + 1)
                act.copy(Pb[0:n], heads(A, n, n)).then_inc(s["p1"], 1)

            def values(o):
                n, c = ROWS[ORDER[o]], ORDER[o]
                act.wait_ge(s["vn_ps"], o + 1)
                act.copy(tokV[0:n, c, :], bank(2, 2)[0:n, 0:GW]).then_inc(s["vn"], 1)

            def gdn_rstd(o):
                n, c = ROWS[ORDER[o]], ORDER[o]
                act.wait_ge(s["o_ms"], o + 1)
                own(fn(orr[0:n, c, :], orr[0:n, c, :], ACT.Ln))
                fn(orr[0:n, c, :], orr[0:n, c, :], ACT.Exp, scale=-0.5).then_inc(s["o_rstd"], 1)

            values(0)
            gdn_rstd(0)
            values(1)
            act.wait_ge(s["s_ps"], H + 1)
            act.copy(Sp, heads(0, P)).then_inc(s["sp_e"], 1)
            gdn_rstd(1)
            values(2)
            gdn_rstd(2)

            for o in range(3):
                n, c = ROWS[ORDER[o]], ORDER[o]
                act.wait_ge(s["oT_ps"], o + 1)
                act.copy(oT[:, :, span(c)], bank(2, 2)[:, 0:H * n].rearrange("p (h t) -> p h t", h=H)
                         ).then_inc(s["oT"], 1)

            for c in range(3):
                n = ROWS[c]
                act.wait_ge(s["mix_ps"], c + 1)
                act.wait_ge(s["vn_ps"], 3)
                act.wait_ge(s["ssq"], 3 + c)
                fn(mixjunk[0:n, :], bank((4, 6, 0)[c], 2)[0:n, :], ACT.Square, accum_out=st[0:n, c:c + 1]
                   ).then_inc(s["ssq"], 1)
                act.wait_ge(s["ms"], c + 2)
                own(fn(st[0:n, 6 + c:7 + c], st[0:n, 3 + c:4 + c], ACT.Ln))
                fn(st[0:n, 9 + c:10 + c], st[0:n, 6 + c:7 + c], ACT.Exp, scale=-0.5).then_inc(s["rstd"], 1)
            for c in range(3):
                n = ROWS[c]
                act.wait_ge(s["x1"], c + 1)
                act.wait_ge(s["ssq"], 6 + c)
                fn(mixjunk[0:n, :], x_sb[0:n, c, :], ACT.Square, accum_out=st[0:n, c:c + 1]).then_inc(s["ssq"], 1)
            rstd(act, fn, own, st, 5)

            for k in range(KT):
                act.wait_ge(s["x2T_ps"], 2 + k // 2)
                fn(h2T[:, k, 0:SEQ], bank(4 + k // 2)[:, 256 * (k % 2):256 * (k % 2) + 256], ACT.Identity,
                   scale=modT[:, 3, k, 0:1], bias=modT[:, 2, k, 0:1]).then_inc(s["h2T"], 1)
            act.wait_ge(s["rt_in"], 16 * 7)
            act.wait_ge(s["router_ps"], 1)
            act.copy(lgT[0:NE, :], bank(3)[0:NE, 0:TOK]).then_inc(s["rl_sb"], 1)
            for c in range(3):
                act.wait_ge(s["h2_ps"], c + 1)
                act.copy(h2[0:ROWS[c], c, :], bank((4, 6, 0)[c], 2)[0:ROWS[c], :]).then_inc(s["h2"], 1)
            act.wait_ge(s["router_ps"], 3)
            act.copy(bguT, bank(4)).then_inc(s["bguT"], 1)
            act.wait_ge(s["gex"], 1)
            fn(exg, exg, ACT.Exp).then_inc(s["gex"], 1)
            act.wait_ge(s["router_ps"], 6)
            act.copy(gT[0:NE, :], bank(7)[0:NE, 0:TOK]).then_inc(s["gT"], 1)
            act.wait_ge(s["cum"], 2)

            def take_x(i):
                act.wait_ge(s["xg_ps"], i)
                act.copy(xg, bank(0)).then_inc(s["xg"], 1)
                act.wait_ge(s["xTm_ps"], i)
                act.copy(xTm.rearrange("p j h t -> p (j h t)"), bank(0)).then_inc(s["xTm"], 1)

            act.wait_ge(s["y_sb"], 1)
            take_x(1)
            with act.Fori(0, NE // 2) as pair:
                for par in range(2):
                    first = act.value_load(cum_i[0:1, bass.ds(pair * 2 + par, 1)], min_val=1, max_val=257)
                    end = act.value_load(cum_i[0:1, bass.ds(pair * 2 + par + 1, 1)], min_val=2, max_val=257)
                    with act.Fori(first, end) as i:
                        act.wait_ge(s["gu_ps"], i)
                        act.copy(gu_sb[:, 0, :], bank(2)).then_inc(s["gu_a"], 1)
                        take_x(i + 1)
                        act.wait_ge(s["g_ready"], i)
                        fn(sig, hidg, ACT.Sigmoid, scale=ALPHA).then_inc(s["sig"], 1)
                        act.wait_ge(s["sgT_ps"], i + 1)
                        act.copy(selGT, bank(1)[:, 0:TOK]).then_inc(s["sgT"], 1)
                        act.wait_ge(s["y_ps"], i)
                        act.copy(y_sb, bank(6, 2)).then_inc(s["y_sb"], 1)

            rounds = act.value_load(cum_i[0:1, NE:NE + 1], min_val=2, max_val=257)
            act.wait_ge(s["acc_add"], rounds * 6 + 6)
            act.wait_ge(s["fin_in"], 16 * 20)
            for c in range(3):
                n = ROWS[c]
                act.wait_ge(s["ssq"], 9 + c)
                fn(fin_junk[0:n, :], acc[0:n, c, :], ACT.Square, accum_out=fst[0:n, c:c + 1]).then_inc(s["ssq"], 1)
            rstd(act, fn, own, fst, 6)

        @block.vector
        def _(v):
            own = Chain(v, s["ch_dve"])
            tt, ts, stt = v.tensor_tensor, v.tensor_scalar, v.scalar_tensor_tensor

            def per_head(a, n, m=P):
                return a.unsqueeze(2).to_broadcast([n, H, m])

            def every_head(a, n, m=P):
                return a.unsqueeze(1).to_broadcast([n, H, m])

            own(v.memset(st[:, :], 0.0))
            v.memset(fst[:, :], 0.0)
            v.memset(st[:, 12:13], EPS).then_inc(s["eps_set"], 1)
            own(v.memset(cT, 0.0))
            v.memset(ab, 0.0)
            v.wait_ge(s["setup_ps"], 1)
            v.tensor_copy(cT[:, :, 0:SEQS], bank(0)[:, 0:KT * SEQS].rearrange("p (k q) -> p k q", k=KT)
                          ).then_inc(s["setup_sb"], 1)
            v.wait_ge(s["setup_ps"], 2)
            v.tensor_copy(vecT, bank(1)[:, 0:138]).then_inc(s["setup_sb"], 1)
            v.wait_ge(s["setup_ps"], 3)
            v.tensor_copy(cexs[:, :, :, 0:3], bank(2)[:, 0:432].rearrange("p (m b t) -> p m b t", m=CT, b=NSEQ)
                          ).then_inc(s["setup_sb"], 1)
            v.wait_ge(s["setup_ps"], 4)
            v.tensor_copy(uexs[:, :, :, 0:PBUF], bank(3)[:, 0:240].rearrange("p (m b t) -> p m b t", m=NU, b=NSEQ)
                          ).then_inc(s["setup_sb"], 1)
            v.wait_ge(s["ssq"], 3)
            ts(st[:, 3:6], st[:, 0:3], 1.0 / D, EPS, ALU.mult, ALU.add).then_inc(s["ms"], 1)
            v.wait_ge(s["rstd"], 1)
            for c in range(3):
                n = ROWS[c]
                ts(xn[0:n, c, :], x_sb[0:n, c, :], st[0:n, 9 + c:10 + c], None, ALU.mult).then_inc(s["xn"], 1)

            MODT = [0, 1, 2, 3, 6, 7, 8, 9]

            def mod_evac(i):
                v.wait_ge(s["slot_used"], ADA_SLOTS[i] + 1)
                ps = bank(i % 2)[:, 0:P]
                if i in MODT:
                    if MODT.index(i):
                        v.wait_ge(s["modT_ps"], MODT.index(i))
                    v.tensor_copy(mraw, ps).then_inc(s["mod_sb"], 1)
                else:
                    u = (4, 5, 10, 11).index(i)
                    tt(modG[:, u, :], ps, b_row[:, u, :], ALU.add).then_inc(s["mod_sb"], 1)
                    v.wait_ge(s["mod_sb"], i + 1)
                    tt(modG[:, u, :], modG[:, u, :], gpost[:, u, :], ALU.mult).then_inc(s["modG"], 1)

            def mod_transposed(g, b0, gvec):
                v.wait_ge(s["modT_ps"], 4 * (g // 2) + 4)
                for t in range(2):
                    ps = bank(2)[:, 256 * t:256 * t + 256].rearrange("p (k q) -> p k q", k=KT)[:, :, 0:SEQS]
                    b = vecT[:, b0 + KT * t:b0 + KT * t + KT].unsqueeze(2).to_broadcast([P, KT, SEQS])
                    own(tt(modT[:, g + t], ps, b, ALU.add))
                stt(modT[:, g + 1], modT[:, g + 1], 1.0, gvec.unsqueeze(2).to_broadcast([P, KT, SEQS]),
                    ALU.add, ALU.mult).then_inc(s["modT"], 1)

            def modulate_samples(dst, ps, g, done):
                def per_seq(a):
                    return a[:, :, 1:SEQS].unsqueeze(3).to_broadcast([P, KT, NSEQ, DSEQ])
                out = dst[:, :, SEQ:TOK].rearrange("p k (b t) -> p k b t", b=NSEQ)
                own(tt(out, ps.rearrange("p (k b t) -> p k b t", k=KT, b=NSEQ), per_seq(modT[:, g + 1]), ALU.mult))
                tt(out, out, per_seq(modT[:, g]), ALU.add).then_inc(s[done], 1)

            for i in range(ADA_FIRST):
                mod_evac(i)
            mod_transposed(0, 0, vecT[:, 48:56])
            v.wait_ge(s["modT"], 1)
            v.wait_ge(s["xT_ps"], 1)
            modulate_samples(hT, bank(3)[:, 256:512], 0, "hT_s")

            for h in range(CT):
                v.wait_ge(s["tap3"], h + 1)
                ps = unit_bank(3 + NU + h)
                for j in (2, 1, 0):
                    sh = 3 - j
                    tap = 66 + j * CT + h
                    ins = stt(qkvT[:, h, sh:SEQ], ps[:, 0:SEQ - sh], vecT[:, tap:tap + 1], qkvT[:, h, sh:SEQ],
                              ALU.mult, ALU.add)
                    if j:
                        own(ins)
                    else:
                        ins.then_inc(s["conv_done"], 1)
            v.wait_ge(s["small_in"], 16 * N_SMALL)
            for i in range(ADA_FIRST, 12):
                mod_evac(i)
                if i == 10:
                    mod_transposed(2, 24, vecT[:, 56:64])

            def tap_of(j):
                return vecT[:, 66 + j * CT:66 + (j + 1) * CT].unsqueeze(2).unsqueeze(3).to_broadcast([P, CT, NSEQ, DSEQ])
            acc4 = s_tap.rearrange("p m (b t) -> p m b t", b=NSEQ)
            tmp4 = s_tmp.rearrange("p m (b t) -> p m b t", b=NSEQ)
            own(tt(acc4, cexs[:, :, :, 0:DSEQ], tap_of(0), ALU.mult))
            for j in (1, 2, 3):
                own(tt(tmp4, cexs[:, :, :, j:j + DSEQ], tap_of(j), ALU.mult))
                ins = tt(acc4, acc4, tmp4, ALU.add)
                own(ins) if j < 3 else ins.then_inc(s["s_taps"], 1)

            v.wait_ge(s["z_sb"], 3)
            own(tt(spt[0], ab[:, :, 0:H], dtb.unsqueeze(1).to_broadcast([P, 3, H]), ALU.add))
            own(ts(spt[1], spt[0], -1.0, None, ALU.mult))
            tt(spt[1], spt[0], spt[1], ALU.min).then_inc(s["softplus_v"], 1)
            v.wait_ge(s["softplus_a"], 1)
            ts(spt[1], spt[1], 1.0, None, ALU.add).then_inc(s["softplus_v"], 1)
            own(ts(spt[2], spt[0], 0.0, None, ALU.max))
            own(ts(beta, beta, 1.0, None, ALU.add))
            own(v.reciprocal(beta, beta))
            v.wait_ge(s["softplus_a"], 2)
            own(tt(spt[2], spt[1], spt[2], ALU.add))
            stt(gg, spt[2], -1.0, alog.unsqueeze(1).to_broadcast([P, 3, H]), ALU.mult, ALU.mult
                ).then_inc(s["gates"], 1)
            v.wait_ge(s["gates"], 1)
            tt(gseq[0:NS], gg[0:NS, 2, :].unsqueeze(1).to_broadcast([NS, NSEQ, H]),
               of_seq[0:NS, :].unsqueeze(2).to_broadcast([NS, NSEQ, H]), ALU.mult).then_inc(s["gates"], 1)

            v.wait_ge(s["s_silu"], 1)
            for h in range(2 * H + 2):
                if h < 2 * H:
                    v.wait_ge(s["silu_done"], h + 1)
                    if h >= 4:
                        v.wait_ge(s["norm_ps"], h - 3)
                    tt(sq[h % 4], qkvT[:, h, :], qkvT[:, h, :], ALU.mult).then_inc(s["sq"], 1)
                if h >= 2:
                    g = h - 2
                    v.wait_ge(s["n_exp"], g + 1)
                    stt(qkvT[:, g, :], qkvT[:, g, :], DH ** -0.5 if g < H else 1.0, bank(4 + g % 4)[:, 0:TOK],
                        ALU.mult, ALU.mult).then_inc(s["qk_n"], 1)

            v.wait_ge(s["egates"], 1)
            own(stt(negeb[:, 0:2, :], egc[:, 0:2, :], -1.0, beta[:, 0:2, :], ALU.mult, ALU.mult))
            own(stt(negeb[0:NS, 2, :], egc[0:NS, 2, :], -1.0, beta[0:NS, 2, :], ALU.mult, ALU.mult))

            def by_head(a, c, n):
                return a[0:n, c, :].rearrange("p (h d) -> p h d", h=H)

            def scale_values(o):
                n, c = ROWS[ORDER[o]], ORDER[o]
                return tt(by_head(tokV, c, n), by_head(tokV, c, n), per_head(beta[0:n, c, :], n), ALU.mult)

            def level_mask(o, l, n):
                at = LEVELS * P + NS * l if o == 0 else P * l
                return every_head(lmask[0:n, at:at + n], n, n)

            def masked(i):
                o, l = STEPS[i]
                n = ROWS[ORDER[o]]
                L, _, _, Mk = buffers(o)[:4]
                tt(Mk[0:n], L[0:n], level_mask(o, l, n), ALU.mult).then_inc(s["ml"], 1)

            def update(i):
                o, l = STEPS[i]
                n = ROWS[ORDER[o]]
                _, T, U, _, _, _, A, B = buffers(o)
                v.wait_ge(s["tn_ps"], i + 1)
                if o and l < LEVELS - 1:
                    tt(T[0:n], T[0:n], heads(A, n, n), ALU.subtract)
                tt(U[0:n], U[0:n], heads(B, n, n), ALU.subtract).then_inc(s["tu_done"], 1)

            for o in range(3):
                c = ORDER[o]
                n = ROWS[c]
                L, T, U, Mk = buffers(o)[:4]
                Dx = dmat(o)[0:n]
                upto_m, after_m, tril_m = masks(o)
                if o == 0:
                    v.wait_ge(s["slot_used"], ADA_FIRST + N_IN)
                else:
                    v.wait_ge(s["tn_ps"], 1)
                    v.wait_ge(s["tu_done"], 1)
                tt(Mk[0:n], every_head(after_m[0:n, 0:n], n, n), per_head(gg[0:n, c, :], n, n), ALU.mult
                   ).then_inc(s["ga"], 1)
                v.wait_ge(s["dexp"], o + 1)
                own(tt(Dx, Dx, every_head(tril_m[0:n, 0:n], n, n), ALU.mult))
                v.wait_ge(s["kk_ps"], o + 1)
                for h in range(H):
                    ins = stt(L[0:n, h, :], heads(2, n, n)[:, h, :], beta[0:n, c, h:h + 1], Dx[:, h, :],
                              ALU.mult, ALU.mult)
                ins.then_inc(s["lmat"], 1)
                v.wait_ge(s["qk_ps"], o + 1)
                v.wait_ge(s["lmat"], o + 1)
                tt(Dx, heads(4, n, n), Dx, ALU.mult).then_inc(s["qkd"], 1)
                own(tt(Mk[0:n], L[0:n], level_mask(o, 0, n), ALU.mult))
                tt(T[0:n], every_head(ident[0:n, 0:n], n, n), Mk[0:n], ALU.subtract).then_inc(s["t0"], 1)
                v.wait_ge(s["t0"], o + 1)
                if o == 0:
                    masked(0)
                    v.wait_ge(s["u0"], 1)
                    update(0)
            masked(1)
            masked(2)
            v.wait_ge(s["kv_tok"], 6)
            own(scale_values(0))
            own(scale_values(2))
            for i in range(1, len(STEPS)):
                v.wait_ge(s["u0"], 3)
                update(i)
                if i + 2 < len(STEPS):
                    masked(i + 2)

            v.wait_ge(s["ssm_in"], 16 * (NSEQ + 1))
            for h in range(H):
                if h:
                    v.wait_ge(s["ks_ps"], h)
                for t in range(2):
                    ins = tt(kq_mask[:, :, NS * t:NS * t + NS],
                             qkvT[:, H * (1 - t) + h, SEQ:TOK].unsqueeze(1).to_broadcast([P, NSEQ, NS]), seqmask,
                             ALU.mult)
                ins.then_inc(s["kqm"], 1)

            O, O2 = P1[0], P1[1]

            def residual(o, ps):
                n, c = ROWS[ORDER[o]], ORDER[o]
                for h in range(H):
                    val = tokV[0:n, c, P * h:P * h + P]
                    ins = stt(val, ps[0:n, h, :], negeb[0:n, c, h:h + 1], val, ALU.mult, ALU.add)
                ins.then_inc(s["rr"], 1)

            def decayed_keys(o):
                n, c = ROWS[ORDER[o]], ORDER[o]
                tt(by_head(tokK, c, n), by_head(tokK, c, n), per_head(egr[0:n, c, :], n), ALU.mult
                   ).then_inc(s["kdec"], 1)

            def gated_norm(o):
                n, c = ROWS[ORDER[o]], ORDER[o]
                v.wait_ge(s["o_tok"], o + 1)
                own(tt(O2[0:n], O[0:n], O[0:n], ALU.mult))
                own(v.tensor_reduce(orr[0:n, c, :], O2[0:n], AX.X, ALU.add))
                ts(orr[0:n, c, :], orr[0:n, c, :], 1.0 / DH, EPS, ALU.mult, ALU.add).then_inc(s["o_ms"], 1)
                v.wait_ge(s["o_rstd"], o + 1)
                own(tt(O[0:n], O[0:n], per_head(orr[0:n, c, :], n), ALU.mult))
                own(tt(O[0:n], O[0:n], every_head(gdnw[0:n, :], n), ALU.mult))
                tt(by_head(z, c, n), by_head(z, c, n), O[0:n], ALU.mult).then_inc(s["gated"], 1)

            v.wait_ge(s["ks_ps"], H)
            own(v.tensor_copy(O[0:NS], bank(0, 2)[NS:2 * NS, 0:GW].rearrange("p (h d) -> p h d", h=H)))
            residual(0, heads(0, NS))
            tt(O[0:NS], O[0:NS], per_head(egc[0:NS, 2, :], NS), ALU.mult).then_inc(s["qs_sb"], 1)
            decayed_keys(0)
            scale_values(1).then_inc(s["rr"], 1)
            decayed_keys(1)
            decayed_keys(2)
            v.wait_ge(s["o_ps"], 1)
            v.wait_ge(s["qs_sb"], 1)
            tt(O[0:NS], O[0:NS], heads(4, NS), ALU.add).then_inc(s["o_tok"], 1)
            for h in range(H):
                v.wait_ge(s["s_ps"], h + 1)
                for b in range(NSEQ):
                    ins = stt(Ssm[:, b, h, :], Ssm[:, b, h, :], egls[:, b, h:h + 1],
                              bank(6, 2)[:, DH * b:DH * b + DH], ALU.mult, ALU.add)
                ins.then_inc(s["s_new"], 1)
            v.wait_ge(s["z_sb"], 6)
            gated_norm(0)
            v.wait_ge(s["gated"], 1)
            v.wait_ge(s["o_ps"], 2)
            v.tensor_copy(O, heads(4, P)).then_inc(s["o_tok"], 1)
            gated_norm(1)
            v.wait_ge(s["ks_ps"], H + 1)
            residual(2, heads(0, P))
            v.wait_ge(s["gated"], 2)
            v.wait_ge(s["ks_ps"], H + 2)
            tt(O, heads(6, P), per_head(egc[:, 1, :], P), ALU.mult).then_inc(s["qs_sb"], 1)
            v.wait_ge(s["o_ps"], 3)
            v.wait_ge(s["qs_sb"], 2)
            tt(O, O, heads(4, P), ALU.add).then_inc(s["o_tok"], 1)
            v.wait_ge(s["s_ps"], H + 2)
            v.wait_ge(s["sp_e"], 1)
            for h in range(H):
                ins = stt(Sp[:, h, :], Sp[:, h, :], egl[:, 1, h:h + 1], heads(0, P)[:, h, :], ALU.mult, ALU.add)
            ins.then_inc(s["s_new"], 1)
            gated_norm(2)

            v.wait_ge(s["gm_in"], 16 * 18)
            for c in range(3):
                n = ROWS[c]
                v.wait_ge(s["ssq"], c + 4)
                ts(st[0:n, 3 + c:4 + c], st[0:n, c:c + 1], 1.0 / D, EPS, ALU.mult, ALU.add).then_inc(s["ms"], 1)
                v.wait_ge(s["rstd"], c + 2)
                own(stt(xt[0:n, :], bank((4, 6, 0)[c], 2)[0:n, :], st[0:n, 9 + c:10 + c], gm_tok[c][0:n, :],
                        ALU.mult, ALU.mult))
                tt(x_sb[0:n, c, :], x_sb[0:n, c, :], xt[0:n, :], ALU.add).then_inc(s["x1"], 1)
            own(v.memset(h2[:, 2, :], 0.0))
            v.wait_ge(s["ssq"], 9)
            ts(st[:, 3:6], st[:, 0:3], 1.0 / D, EPS, ALU.mult, ALU.add).then_inc(s["ms"], 1)
            v.wait_ge(s["rstd"], 5)
            for c in range(3):
                n = ROWS[c]
                ts(h2[0:n, c, :], x_sb[0:n, c, :], st[0:n, 9 + c:10 + c], None, ALU.mult).then_inc(s["xn2"], 1)
            v.wait_ge(s["x2T_ps"], 1)
            v.wait_ge(s["modT"], 2)
            modulate_samples(h2T, bank(2)[:, 0:256], 2, "h2T")

            v.wait_ge(s["rt_in"], 16 * 7)
            own(v.memset(lg, 0.0))
            v.wait_ge(s["router_ps"], 2)
            v.tensor_copy(lg[:, 0:2, :], bank(2)[:, 0:2 * NE].rearrange("p (c e) -> p c e", c=2))
            own(v.tensor_copy(lg[0:NS, 2, :], bank(2)[0:NS, 2 * NE:3 * NE]))
            for c in range(3):
                own(v.max(top8[:, c, :], lg[:, c, :]))
            tt(exg, lg, top8[:, :, 0:1].to_broadcast([P, 3, NE]), ALU.subtract).then_inc(s["gex"], 1)
            own(v.memset(top8[:, :, TOPK:8], 3.0e38))
            for c in range(3):
                own(v.match_replace(eqm[:, c, :], top8[:, c, :], lg[:, c, :], -3.0e38))
            own(tt(sel01, eqm, lg, ALU.not_equal))
            v.wait_ge(s["gex"], 2)
            own(tt(exg, exg, sel01, ALU.mult))
            own(v.tensor_reduce(rst[:, 0:3], exg, AX.X, ALU.add))
            ts(sel01[:, 2, :], sel01[:, 2, :], rvalid[:, 0:1], None, ALU.mult).then_inc(s["top_e"], 1)
            own(v.reciprocal(rst[:, 3:6], rst[:, 0:3]))
            v.wait_ge(s["h2_ps"], 3)
            tt(gate, exg, rst[:, 3:6].unsqueeze(2).to_broadcast([P, 3, NE]), ALU.mult).then_inc(s["gate_done"], 1)
            v.wait_ge(s["router_ps"], 5)
            step = Chain(v, s["hid_step"])
            step(ts(cntb, bank(6)[:, 0:NE], float(SLOTS), 1.0, ALU.is_gt, ALU.add))
            for r in range(2, (TOK + SLOTS - 1) // SLOTS):
                step(stt(cntb, bank(6)[:, 0:NE], float(SLOTS * r), cntb, ALU.is_gt, ALU.add))
            own(v.memset(cumf, 1.0))
            own(v.memset(cnt, 0.0))
            own(v.tensor_tensor_scan(cumf[:, 1:NE + 1], cntb, cnt, 1.0, ALU.add, ALU.add))
            ts(ends_i[0:1, :], cumf[0:1, 1:NE + 1], -1.0, None, ALU.add).then_inc(s["cum"], 1)
            v.tensor_copy(cum_i[0:1, :], cumf[0:1, :]).then_inc(s["cum"], 1)
            v.wait_ge(s["router_ps"], 4)
            v.wait_ge(s["top_e"], 1)
            own(stt(rank, bank(5)[:, 0:3 * NE].rearrange("p (c e) -> p c e", c=3), 1.0, sel01, ALU.add, ALU.mult))
            ts(rank, rank, -1.0, None, ALU.add).then_inc(s["rank_done"], 1)
            v.memset(y_sb, 0.0).then_inc(s["y_sb"], 1)
            v.memset(selGT, 0.0).then_inc(s["sgT"], 1)

            v.wait_ge(s["rank_done"], 1)
            v.wait_ge(s["cum"], 2)
            for u in range(6):
                c, half = u // 2, u % 2
                v.wait_ge(s["sc_ps"], u + 1)
                v.tensor_copy(acc[0:ROWS[c], c, 512 * half:512 * half + 512], bank(half)[0:ROWS[c], :]
                              ).then_inc(s["acc_add"], 1)
            v.wait_ge(s["bguT"], 1)
            hg = hidg.rearrange("p (k t) -> p k t", k=KT)
            hu = hidu.rearrange("p (k t) -> p k t", k=KT)
            T2 = bank(4, 2).rearrange("p (k x t) -> p k x t", k=KT, x=2)

            def add_back(i, u):
                c, half = u // 2, u % 2
                n = ROWS[c]
                a = acc[0:n, c, 512 * half:512 * half + 512]
                v.wait_ge(s["sc_ps"], i * 6 + (u + 1))
                tt(a, a, bank(6 + half)[0:n, :], ALU.add).then_inc(s["acc_add"], 1)

            with v.Fori(0, NE // 2) as pair:
                for par in range(2):
                    first = v.value_load(cum_i[0:1, bass.ds(pair * 2 + par, 1)], min_val=1, max_val=257)
                    end = v.value_load(cum_i[0:1, bass.ds(pair * 2 + par + 1, 1)], min_val=2, max_val=257)
                    with v.Fori(first, end) as i:
                        v.wait_ge(s["gu_ps"], i)
                        v.tensor_copy(gu_sb[:, 1, :], bank(3)).then_inc(s["gu_v"], 1)
                        v.wait_ge(s["hid_ps"], i)
                        bias = [bguT[:, bass.ds((pair * 2 + par) * 16 + KT * t, KT)].unsqueeze(2)
                                .to_broadcast([P, KT, SLOTS]) for t in range(2)]
                        tt(hg, T2[:, :, 0, :], bias[0], ALU.add).then_inc(s["hid_step"], 1)
                        tt(hu, T2[:, :, 1, :], bias[1], ALU.add).then_inc(s["hid_step"], 1)
                        v.wait_ge(s["hid_step"], i * 4 + 1)
                        ts(hidg, hidg, LIMIT, None, ALU.min).then_inc(s["g_ready"], 1)
                        v.wait_ge(s["hid_step"], i * 4 + 2)
                        ts(hidu, hidu, LIMIT, -LIMIT, ALU.min, ALU.max).then_inc(s["hid_step"], 1)
                        add_back(i, 0)
                        v.wait_ge(s["hid_step"], i * 4 + 3)
                        v.wait_ge(s["g_ready"], i)
                        v.wait_ge(s["sig"], i)
                        stt(hidg, hidu, 1.0, hidg, ALU.add, ALU.mult).then_inc(s["hid_step"], 1)
                        add_back(i, 1)
                        v.wait_ge(s["hid_step"], i * 4 + 4)
                        tt(hidg, hidg, sig, ALU.mult).then_inc(s["hid"], 1)
                        for u in range(2, 6):
                            add_back(i, u)
            rounds = v.value_load(cum_i[0:1, NE:NE + 1], min_val=2, max_val=257)
            for u in range(6):
                add_back(rounds, u)

            v.wait_ge(s["ssq"], 12)
            ts(fst[:, 3:6], fst[:, 0:3], 1.0 / D, EPS, ALU.mult, ALU.add).then_inc(s["ms"], 1)
            v.wait_ge(s["rstd"], 6)
            v.wait_ge(s["fin_in"], 16 * 20)
            for c in range(3):
                n = ROWS[c]
                own(stt(fin_t[0:n, c, :], acc[0:n, c, :], fst[0:n, 9 + c:10 + c], fin_g[c][0:n, :], ALU.mult, ALU.mult))
                tt(fin_x[0:n, c, :], fin_x[0:n, c, :], fin_t[0:n, c, :], ALU.add).then_inc(s["fin_y"], 1)

        @block.gpsimd
        def _(g):
            own = Chain(g, s["ch_pool"])
            own(g.memset(wpbd, 0.0))
            own(g.memset(uext[:, :, 0:PBUF], 0.0))
            g.memset(tokK[:, 2, :], 0.0).then_inc(s["zeroed"], 1)

            g.wait_ge(s["u_sb"], 2)
            g.wait_ge(s["setup_sb"], 4)
            g.wait_ge(s["const_in"], 16 * N_CONST)
            add = lambda o, a, b: g.tensor_tensor(o, a, b, ALU.add)
            E = PBUF + SEQ
            own(add(win_a[:, :, 1:E], uext[:, :, 1:E], uext[:, :, 0:E - 1]))
            own(add(win_b[:, :, 3:E], win_a[:, :, 3:E], win_a[:, :, 1:E - 2]))
            own(add(win_a[:, 1, 7:E], win_b[:, 1, 7:E], win_b[:, 1, 3:E - 4]))
            own(add(win_b[64:, 1, 15:E], win_a[64:, 1, 15:E], win_a[64:, 1, 7:E - 8]))
            F = PBUF + DSEQ
            own(add(win_sa[:, :, :, 1:F], uexs[:, :, :, 1:F], uexs[:, :, :, 0:F - 1]))
            own(add(win_sb[:, :, :, 3:F], win_sa[:, :, :, 3:F], win_sa[:, :, :, 1:F - 2]))
            own(add(win_sa[:, 1, :, 7:F], win_sb[:, 1, :, 7:F], win_sb[:, 1, :, 3:F - 4]))
            own(add(win_sb[64:, 1, :, 15:F], win_sa[64:, 1, :, 15:F], win_sa[64:, 1, :, 7:F - 8]))
            for lo, m, w, ws in ((0, 0, win_a, win_sa), (64, 0, win_b, win_sb), (0, 1, win_a, win_sa),
                                 (64, 1, win_b, win_sb)):
                r = slice(lo, lo + 64)
                own(g.tensor_scalar(pooled[r, m, 0:SEQ], w[r, m, PBUF:], invwin[r, m:m + 1], None, ALU.mult))
                own(g.tensor_scalar(pooled[r, m, SEQ:TOK].rearrange("p (b t) -> p b t", b=NSEQ), ws[r, m, :, PBUF:],
                                    invwin[r, m:m + 1], None, ALU.mult))
                own(g.tensor_tensor(pooled[r, m, 0:16], w[r, m, PBUF:PBUF + 16], invcnt[r, m, :], ALU.mult))
            own(g.tensor_tensor(pooled[:, :, 0:SEQ], pooled[:, :, 0:SEQ], uext[:, :, PBUF:], ALU.subtract))
            for m in range(NU):
                ps = pooled[:, m, SEQ:TOK].rearrange("p (b t) -> p b t", b=NSEQ)
                ins = g.tensor_tensor(ps, ps, uexs[:, m, :, PBUF:], ALU.subtract)
                own(ins) if m == 0 else ins.then_inc(s["pooled"], 1)

            g.wait_ge(s["ssm_in"], 16 * (NSEQ + 1))
            own(g.memset(vmask, 0.0))
            g.wait_ge(s["vn"], 1)
            for h in range(H):
                if h:
                    g.wait_ge(s["s_ps"], h)
                g.tensor_tensor(vmask[0:NS], tokV[0:NS, 2, P * h:P * h + P].unsqueeze(1).to_broadcast([NS, NSEQ, DH]),
                                of_seq[0:NS, :].unsqueeze(2).to_broadcast([NS, NSEQ, DH]), ALU.mult
                                ).then_inc(s["vmask"], 1)

            g.wait_ge(s["rank_done"], 1)
            g.wait_ge(s["gate_done"], 1)
            g.wait_ge(s["cum"], 2)
            g.wait_ge(s["bguT"], 1)

            g.memset(cur[:, 2, :], float(SLOTS)).then_inc(s["sgT_ps"], 1)
            g.wait_ge(s["sgT_ps"], 1)

            def select():
                for c in range(3):
                    ins = g.tensor_scalar(selA[:, c, :], iota[:, 0:SLOTS], cur[:, 0, c:c + 1], None, ALU.is_equal)
                ins.then_inc(s["sel"], 1)

            with g.Fori(1, NE + 1) as e:
                first = g.value_load(cum_i[0:1, bass.ds(e - 1, 1)], min_val=1, max_val=257)
                end = g.value_load(cum_i[0:1, bass.ds(e, 1)], min_val=2, max_val=257)
                g.tensor_copy(cur[:, 0:2, :], rank_gate[:, :, :, bass.ds(e - 1, 1)].rearrange("p x c e -> p x (c e)")
                              ).then_inc(s["cur_set"], 1)
                with g.Fori(first, end) as i:
                    g.wait_ge(s["bguT"], 1)
                    g.wait_ge(s["cur_set"], e)
                    select()
                    g.wait_ge(s["bguT"], 1)
                    g.wait_ge(s["sgT_ps"], i)
                    for c in range(3):
                        ins = g.tensor_scalar(selG[:, c, :], iota, cur[:, 0, c:c + 1], cur[:, 1, c:c + 1],
                                              ALU.is_equal, ALU.mult)
                    ins.then_inc(s["selg"], 1)
                    g.wait_ge(s["selg"], i)
                    g.tensor_tensor(cur[:, 0, :], cur[:, 0, :], cur[:, 2, :], ALU.subtract).then_inc(s["sel_step"], 1)
                    g.wait_ge(s["xg_ps"], i)
                    g.wait_ge(s["sel_step"], i)
            select()


_INS = ["x_prompt", "x_sample", "c_prompt", "c_sample", "state_pool", "state_conv", "state_ssm", "w_ada", "b_ada",
        "g_pre_mix", "g_post_mix", "g_pre_ffn", "g_post_ffn", "w_in", "w_pool", "pool_scale", "conv_w", "a_log",
        "dt_bias", "gdn_norm_w", "w_out", "router_w", "router_b", "w_gu", "b_gu", "w_down", "b_down"]
_OUTS = [(1, SEQ, D), (NSEQ, DSEQ, D), (1, 1, PBUF, POOLW), (1, 1, 3, CW), (1, 1, H, DH, DH),
         (1, NSEQ, PBUF, POOLW), (1, NSEQ, 3, CW), (1, NSEQ, H, DH, DH)]


def program(nc, inputs):
    arrays, args = {}, []
    for name in _INS:
        a = np.ascontiguousarray(inputs[name])
        arrays[f"in_{name}"] = a
        args.append(nc.dram_tensor(f"in_{name}", a.shape, mybir.dt.from_np(a.dtype), kind="ExternalInput").ap())
    arrays["shape_consts"] = shape_constants()
    args.append(nc.dram_tensor("shape_consts", arrays["shape_consts"].shape, F32, kind="ExternalInput").ap())
    for i, shape in enumerate(_OUTS):
        args.append(nc.dram_tensor(f"out_{i}", shape, F32, kind="ExternalOutput").ap())
    build(nc, *args)
    return arrays


def kernel(**inputs):
    import concourse.bacc as bacc
    from concourse.bass_utils import run_bass_kernel_spmd

    nc = bacc.Bacc("TRN2", target_bir_lowering=False, num_devices=1)
    arrays = program(nc, inputs)
    r = run_bass_kernel_spmd(nc, [arrays], core_ids=[0])
    return tuple(r.results[0][f"out_{i}"] for i in range(len(_OUTS)))
```

```python
from contextlib import ExitStack

import numpy as np
import concourse.bass as bass
from concourse import mybir

F32 = mybir.dt.float32
BF16 = mybir.dt.bfloat16
I32 = mybir.dt.int32
ALU = mybir.AluOpType
ACT = mybir.ActivationFunctionType
AX = mybir.AxisListType

P = 128
D = 1024
KT = D // P
SEQ, NSEQ, DSEQ = 256, 8, 4
NS = NSEQ * DSEQ
TOK = SEQ + NS
ROWS = (P, P, NS)
AT = (0, P, SEQ)
POOLW, PBUF = 256, 15
H, DH = 6, 128
GW = H * DH
CW = 3 * GW
CT = CW // P
NU = POOLW // P
NT = NU + CT
IN_W = POOLW + CW + GW + 2 * H
NE, TOPK, FF = 32, 4, 1024
SLOTS = 64
LIMIT, ALPHA = 7.0, 1.702
EPS = 1e-6
LEVELS = 7
SLEVELS = 2
TAIL = PBUF + NS
RING = 4
SEQS = 1 + NSEQ


CONST = {}


def shape_constants():
    k = np.arange(P)[:, None]
    j = np.arange(P)[None, :]
    ks, js = np.arange(P)[:, None], np.arange(NS)[None, :]
    same = (ks // DSEQ == js // DSEQ) & (ks < NS)
    parts = [
        ("ident", k == j),
        ("iota", np.broadcast_to(j % SLOTS, (P, P))),
        ("ones", np.ones((P, P))),
        ("upto", k <= j),
        ("after", k > j),
        ("tril", j <= k),
        ("upto_s", (ks <= js) & same),
        ("after_s", (ks > js) & same),
        ("tril_s", (js <= ks) & same),
        ("of_seq", (ks // DSEQ == np.arange(NSEQ)[None, :]) & (ks < NS)),
    ]
    win = np.array([[2, 8], [4, 16]])[(np.arange(P) >= 64).astype(int)]
    parts.append(("invwin", 1.0 / win))
    cnt = np.minimum(np.arange(16)[None, None, :] + 1, win[:, :, None])
    parts.append(("invcnt", (1.0 / cnt).reshape(P, -1)))
    parts += [
        ("before", k < j),
        ("valid", np.broadcast_to(ks[:, 0:1] < NS, (P, 2))),
        ("seqmask", np.broadcast_to((np.arange(NS)[None, :] // DSEQ == np.arange(NSEQ)[:, None])
                                    .reshape(1, -1), (P, NSEQ * NS))),
    ]
    at = 0
    for name, a in parts:
        CONST[name] = (at, a.shape[1])
        at += a.shape[1]
    CONST["all"] = (0, at)
    masks = [((k >> (l + 1)) == (j >> (l + 1))) & ((k >> l) % 2 == 1) & ((j >> l) % 2 == 0)
             for l in range(LEVELS)]
    masks_s = [((ks >> (l + 1)) == (js >> (l + 1))) & ((ks >> l) % 2 == 1) & ((js >> l) % 2 == 0) & (ks < NS)
               for l in range(SLEVELS)]
    flat = np.concatenate([np.asarray(a, np.float32) for _, a in parts], axis=1)
    level = np.concatenate([np.where(m, 0x3F80, 0).astype(np.uint16) for m in masks + masks_s], axis=1)
    CONST["levels"] = (at, level.shape[1] // 2)
    return np.concatenate([flat, np.ascontiguousarray(level).view(np.float32)], axis=1)


shape_constants()
LEVEL_COLS = LEVELS * P + SLEVELS * NS

IN_SLOTS = [(3072, IN_W - 3072)] + [(512 * n, 512) for n in range(6)]
N_IN = len(IN_SLOTS)
ADA_FIRST = 4
RING_SLOTS = [("ada", n) for n in range(ADA_FIRST)] + [("in", 0)]
for n in range(1, N_IN):
    RING_SLOTS += [("in", n)] + [("ada", g) for g in {1: [4], 2: [5], 3: [6], 4: [7], 5: [8, 9], 6: [10, 11]}[n]]


class Arena:

    def __init__(self, tensor, words):
        self.t, self.words = tensor, words

    def at(self, off, *shape):
        n = int(np.prod(shape))
        assert off + n <= self.words, (off, n, self.words)
        v = self.t[:, off:off + n]
        if len(shape) == 2:
            v = v.rearrange("p (a b) -> p a b", a=shape[0])
        if len(shape) == 3:
            v = v.rearrange("p (a b c) -> p a b c", a=shape[0], b=shape[1])
        return v


class Chain:

    def __init__(self, eng, sem):
        self.eng, self.sem, self.n = eng, sem, 0

    def __call__(self, ins):
        self.n += 1
        ins.then_inc(self.sem, 1)
        self.eng.wait_ge(self.sem, self.n)


SEMS = """acc_add bguT c_in c_silu ch_act ch_dve ch_pool const_in conv_done cum cur_set d_in0 d_in1 dexp diff_ps egates
 fin_in fin_y gT g_ready ga gate_done gate_ps gated gates gex gm_in gu_a gu_in00 gu_in01 gu_in02 gu_in03
 gu_in10 gu_in11 gu_in12 gu_in13 gu_ps gu_read gu_v h2 h2T h2_ps hT_a hT_s hid hid_ps hid_step hist_in kdec kk_ps kqm
 ks_ps kvT_ps kv_tok lmat mix_ps ml modG modG_st modT modT_ps mod_sb norm_ps norm_root oT oT_ps o_ms o_ps
 o_root o_tok p1 p1_ps poolT pool_ps pooled proj_ps qk_n qk_ps qkd qkdT qkdT_ps qs_sb rank_done ring0 ring1
 ring2 ring3 rl_sb root router_ps rr rt_in s_new s_ps s_silu s_taps sc_ps sel sel_step selg setup_ps setup_sb
 sgT sgT_ps sig silu_done slot_used small_in softplus_a softplus_v sp_e sq ssm_in ssm_out ssq stats_set t0
 tailT_ps tail_rows tail_st tap3 tn_ps top_e tu_done u0 u0_ps u_sb vec_in vmask vn vn_ps wout_in wpool_in x1
 x1_st x2T_ps xT_ps xTm xTm_ps x_in xg xg_ps xn xn2 y_ps y_sb y_st z_sb zeroed""".split()


def build(nc, x_prompt, x_sample, c_prompt, c_sample, state_pool, state_conv, state_ssm, w_ada, b_ada,
          g_pre_mix, g_post_mix, g_pre_ffn, g_post_ffn, w_in, w_pool, pool_scale, conv_w, a_log, dt_bias,
          gdn_norm_w, w_out, router_w, router_b, w_gu, b_gu, w_down, b_down, consts,
          y_prompt, y_sample, pool_prompt, conv_prompt, ssm_prompt, pool_sample, conv_sample, ssm_sample):
    x1_dram = nc.dram_tensor("x1_scratch", (TOK, D), F32, kind="Internal").ap()
    gm_dram = nc.dram_tensor("gate_mod_scratch", (4, 32, 4, P), F32, kind="Internal").ap()
    ctx = ExitStack()
    with ctx:
        def sb(name, shape, dt=F32):
            return ctx.enter_context(nc.sbuf_tensor(name, shape, dt))

        s = {n: ctx.enter_context(nc.semaphore(n)) for n in SEMS}

        G0t, G1t, Dt = sb("gu_even", [P, 16384]), sb("gu_odd", [P, 16384]), sb("down_w", [P, 8192])
        WM = 11664
        Mt = sb("work", [P, WM])
        lmask_t = sb("level_masks_sb", [P, LEVEL_COLS // 2])
        lmask = lmask_t[:, :].bitcast(BF16)
        ps_t = ctx.enter_context(nc.psum_tensor("psum", [P, 8, 512], F32))
        G0, G1, DD, M = Arena(G0t, 16384), Arena(G1t, 16384), Arena(Dt, 8192), Arena(Mt, WM)

        def bank(b, n=1):
            return ps_t[:, b:b + n, :].rearrange("p b n -> p (b n)")

        ring = [G0.at(4096 * i, KT, 512) for i in range(RING)]
        qkvT = G1.at(0, CT, TOK)
        xn = G1.at(0, 3, D)
        junk = G1.at(3072, D)
        tokK, tokV = G1.at(5184, 3, GW), G1.at(7488, 3, GW)
        Lm = [G1.at(9792 + 768 * c, H, P) for c in range(2)]
        Tm = [G1.at(11328 + 768 * c, H, P) for c in range(2)]
        Um = [G1.at(12864 + 768 * c, H, P) for c in range(2)]
        QKT = [G1.at(14400 + 768 * c, H, P) for c in range(2)]
        Us, QKTs = G1.at(15936, H, NS), G1.at(15936 + 192, H, NS)
        Sp = Lm[0]
        gm_tok = [G1.at(11328, D), G1.at(11328, D), G1.at(12352, D)]
        fin_x = G0.at(0, 3, D)
        fin_g = [G0.at(3072, D), G0.at(3072, D), G0.at(4096, D)]
        fin_junk, fin_t = G0.at(5120, D), G0.at(6144, 3, D)
        xt = [M.at(5376, D), M.at(6400, D)]
        mixjunk = G1.at(13376, D)
        c_sb, v1, v2 = G1.at(9792, D), G1.at(10816, P), G1.at(10944, P)
        hist_rows, phist_rows = G1.at(11072, CW), G1.at(13376, POOLW)
        uext = G1.at(13632, NU, PBUF + SEQ)
        uexs = G1.at(14176, NU, NSEQ * (PBUF + DSEQ)).rearrange("p m (b t) -> p m b t", b=NSEQ)
        win_a = G1.at(14480, NU, PBUF + SEQ)
        win_b = G1.at(15024, NU, PBUF + SEQ)
        win_sa = G1.at(15568, NU, NSEQ * 19).rearrange("p m (b t) -> p m b t", b=NSEQ)
        win_sb = G1.at(15872, NU, NSEQ * 19).rearrange("p m (b t) -> p m b t", b=NSEQ)
        cexs = DD.at(0, CT, NSEQ * (3 + DSEQ)).rearrange("p m (b t) -> p m b t", b=NSEQ)
        wpbd = DD.at(1008, NU, P)
        pooled = DD.at(1264, NU, TOK)
        b_row, gpost = DD.at(1840, 4, P), DD.at(2352, 4, P)
        modG = DD.at(2864, 4, P)
        tail_rows = DD.at(3376, NT * P)
        sq = [DD.at(5936 + 288 * i, TOK) for i in range(4)]
        s_tmp = DD.at(5936, CT, NS)
        sq_s = DD.at(5936, 2 * H * NS)
        rnorm = DD.at(3376, 2 * SEQ)
        s_tap = DD.at(7088, CT, NS)
        mraw = DD.at(7664, P)
        Ssm = DD.at(0, NSEQ, H, DH)
        kq_mask = [DD.at(6144, NSEQ, 2 * NS), M.at(4096, NSEQ, 2 * NS)]
        vmask = [DD.at(6656, NSEQ, DH), M.at(3072, NSEQ, DH)]
        seqmask = DD.at(7680, NSEQ, NS)
        w_out_sb = DD.at(0, KT, D)
        x_sb = M.at(0, 3, D)
        hT = M.at(3072, KT, TOK)
        Dm = M.at(3072, H, P)
        Ml = [M.at(3840 + 768 * c, H, P) for c in range(2)]
        oT = M.at(3072, H, TOK)
        z = M.at(5376, 3, GW)
        h2T = M.at(5376, KT, TOK)
        R0 = 7680
        ident, iota = M.at(R0, P), M.at(R0 + 128, P)
        F0 = R0 + 256
        ones, upto, after, tril = [M.at(F0 + P * i, P) for i in range(4)]
        f = F0 + 4 * P
        upto_s, after_s, tril_s = [M.at(f + NS * i, NS) for i in range(3)]
        f += 3 * NS
        of_seq = M.at(f, NSEQ); f += NSEQ
        invwin = M.at(f, NU); f += NU
        invcnt = M.at(f, NU, 16); f += NU * 16
        consts_sb = M.at(R0, f - R0)
        gdnw = M.at(f, DH); f += DH
        poolT = M.at(f, NU, TOK); f += NU * TOK
        P1 = [M.at(f + 768 * c, H, P) for c in range(2)]
        mix_s = M.at(f, D)
        tail = M.at(f, NT, TAIL)
        ab = M.at(f + NT * TAIL, 3, 2 * H)
        spt = [M.at(f + NT * TAIL + 36 + 18 * i, 3, H) for i in range(3)]
        gseq = M.at(f + NT * TAIL + 90, NSEQ, H)
        f += 1536
        cT = M.at(f, KT, 32)
        negeb, orr = M.at(f + 102, 3, H), M.at(f + 120, 3, H)
        f += 256
        assert f >= F0 + 3 * D
        modT = M.at(f, 4, KT * SEQS).rearrange("p g (k q) -> p g k q", k=KT); f += 4 * KT * SEQS
        vecT = M.at(f, 66 + 72); f += 138
        gg = M.at(f, 3, H); f += 18
        beta = M.at(f, 3, H); f += 18
        egc = M.at(f, 3, H); f += 18
        egr = M.at(f, 3, H); f += 18
        egl = M.at(f, 3, H); f += 18
        egls = M.at(f, NSEQ, H); f += 48
        alog = M.at(f, H); f += H
        dtb = M.at(f, H); f += H
        assert f <= WM, f
        acc = M.at(0, 3, D)
        h2 = M.at(F0, 3, D)
        lgT = M.at(0, TOK)
        lg = M.at(288, 3, NE)
        top8 = M.at(384, 3, 8)
        eqm = M.at(408, 3, NE)
        sel01 = M.at(504, 3, NE)
        exg = M.at(600, 3, NE)
        rk_t = M.at(696, 3, NE)
        rst = M.at(800, 16)
        cnt = M.at(816, NE)
        cntb = M.at(848, NE)
        cumf = M.at(880, NE + 2)
        rones, rbefore = M.at(4800, P), M.at(4928, P)
        bgu_rows = M.at(4096, 4, P)
        b_down_sb = M.at(3072, D)
        gT = M.at(7336, TOK)
        rw = M.at(5090, KT, NE)
        E0 = 3072
        xTm = M.at(E0, 4, 2, SLOTS)
        xg = M.at(E0 + 512, 512)
        gu_sb = M.at(E0 + 1024, 2, 512)
        hidg, hidu = gu_sb[:, 0, :], gu_sb[:, 1, :]
        sig = M.at(E0 + 2048, 512)
        y_sb = M.at(E0 + 2560, D)
        selGT = M.at(E0 + 3584, TOK)
        selA = M.at(E0 + 3872, 3, SLOTS)
        f = F0 + 3 * D
        bguT = M.at(f, NE * 2 * KT); f += NE * 2 * KT
        cur = M.at(f, 3, 3); f += 9
        f2 = E0 + 3872 + 192
        rank_gate = M.at(f2, 2, 3, NE)
        rank, gate = rank_gate[:, 0], rank_gate[:, 1]
        assert f2 + 6 * NE <= R0 and f <= WM
        selG = Arena(lmask_t, LEVEL_COLS // 2).at(0, 3, P)
        rvalid, rb_row = M.at(5056, 2), M.at(5058, NE)
        st, fst = sb("stats", [P, 16]), sb("final_stats", [P, 16])
        cum_i = sb("first_rounds", [1, NE + 2], I32)
        ends_i = sb("through_rounds", [1, NE], I32)

        def cc(name):
            off, n = CONST[name]
            return consts[:, off:off + n]

        def gate_rows(sp, g, dst, name):
            for t in range(2):
                row = gm_dram[:, :, 2 * g + t, :].rearrange("j q n -> q j n")
                sp.dma_start(dst[0].rearrange("p (t j n) -> p t j n", t=2, j=4)[:, t],
                             row[0:1].to_broadcast([P, 4, P])).then_inc(s[name], 16)
                for b in range(NSEQ):
                    sp.dma_start(dst[2].rearrange("p (t j n) -> p t j n", t=2, j=4)[DSEQ * b:DSEQ * b + DSEQ, t],
                                 row[1 + b:2 + b].to_broadcast([DSEQ, 4, P])).then_inc(s[name], 16)

        ORDER = (2, 0, 1)
        STEPS = [(0, 1)] + [(o, l) for l in range(1, LEVELS) for o in (1, 2)]

        def step_of(o, l):
            return STEPS.index((o, l)) + 1

        def last_step(o):
            return step_of(o, (SLEVELS if o == 0 else LEVELS) - 1)

        def buffers(o):
            if o == 0:
                return (M.at(4608 + 192, H, NS), M.at(4608, H, NS), Us, M.at(3840, H, NS),
                        P1[0].rearrange("p h t -> p (h t)")[:, 0:H * NS].rearrange("p (h t) -> p h t", h=H), QKTs, 0, 2)
            c = ORDER[o]
            return Lm[c], Tm[c], Um[c], Ml[c], P1[c], QKT[c], 4 * c, 4 * c + 2

        def dmat(o):
            return M.at(3072, H, NS) if o == 0 else Dm

        def masks(o):
            return (upto_s, after_s, tril_s) if o == 0 else (upto, after, tril)

        def heads(b, n, m=P):
            return bank(b, 2)[0:n, 0:H * m].rearrange("p (h t) -> p h t", h=H)

        def span(c):
            return slice(AT[c], AT[c] + ROWS[c])

        N_UNITS = 3 + NT + 3
        Z_UNITS = (0, 1, 2, N_UNITS - 3, N_UNITS - 2, N_UNITS - 1)

        def unit_slot(u):
            if u < 3:
                return RING_SLOTS.index(("in", 0)), u == 2
            if u < 3 + NT:
                return RING_SLOTS.index(("in", 1 + (u - 3) // 4)), (u - 3) % 4 == 3
            return RING_SLOTS.index(("in", N_IN - 1)), u == N_UNITS - 1

        def units_of(n):
            return [u for u in range(N_UNITS) if unit_slot(u)[0] == n]

        def unit_bank(u):
            return bank(4 + u % 4)

        def wait_unit(eng, u):
            slot, last = unit_slot(u)
            if last:
                eng.wait_ge(s["slot_used"], slot + 1)
            else:
                eng.wait_ge(s["proj_ps"], sum(not unit_slot(v)[1] for v in range(u + 1)))

        def wait_unit_read(eng, u):
            if u in Z_UNITS:
                eng.wait_ge(s["z_sb"], Z_UNITS.index(u) + 1)
            elif u < 3 + NU:
                eng.wait_ge(s["u_sb"], u - 3 + 1)
            else:
                eng.wait_ge(s["conv_done"], u - 3 - NU + 1)

        ADA_SLOTS = [n for n, (kind, _) in enumerate(RING_SLOTS) if kind == "ada"]
        TAIL_BANKS = (2, 3, 6, 7, 2)
        NORM_LAG = 4
        SAMPLE_NORM = 16
        SAMPLE_TAPS = 13
        N_CONST, N_VEC, N_HIST, N_SMALL = 1, 5, 2, 20

        def levels(pe, mm, steps):
            for i in steps:
                o, l = STEPS[i]
                c = ORDER[o]
                n = ROWS[c]
                _, T, U, Mk, Pb, _, A, B = buffers(o)
                pe.wait_ge(s["ml"], i + 1)
                if i in (1, 2):
                    for name in ("lmat", "qkd", "qkdT", "u0"):
                        pe.wait_ge(s[name], 3)
                if i == 0:
                    pe.wait_ge(s["u0"], 1)
                    pe.wait_ge(s["lmat"], 1)
                if l > 1:
                    pe.wait_ge(s["tu_done"], step_of(o, l - 1))
                for h in range(H):
                    last = mm(heads(A, n, n)[:, h, :], Mk[0:n, h, :], U[0:n, h, :], start=True, stop=True)
                last.then_inc(s["p1_ps"], 1)
                if i in (0, 2) or i > 2 and o == 2:
                    for j in ([0] if i == 0 else [i - 1, i]):
                        finish_level(pe, mm, j)

        def finish_level(pe, mm, i):
            o, l = STEPS[i]
            n = ROWS[ORDER[o]]
            _, T, U, _, Pb, _, A, B = buffers(o)
            pe.wait_ge(s["p1"], i + 1)
            if i != 0 and l < LEVELS - 1:
                for h in range(H):
                    mm(heads(A, n, n)[:, h, :], Pb[0:n, h, :], T[0:n, h, :], start=True, stop=True)
            for h in range(H):
                last = mm(heads(B, n, n)[:, h, :], T[0:n, h, :], Pb[0:n, h, :], start=True, stop=True)
            last.then_inc(s["tn_ps"], 1)

        SUM_BANKS = (6, 7, 2, 3, 6)

        def sum_rows(u):
            return P if u < 4 else 2 * NS

        def sums(u):
            return acc[:, u // 2, 512 * (u % 2):512 * (u % 2) + 512] if u < 4 else acc[0:2 * NS, 2, 0:512]

        def experts_pe(pe, mm, tr):
            XB, SB, GB, TB, YB = 0, 1, 2, 4, 6

            def gather(i, last_read=None):
                pe.wait_ge(s["sel"], i)
                if last_read is not None:
                    pe.wait_ge(s["xTm"], last_read)
                for c in range(3):
                    for half in range(2):
                        last = mm(bank(XB)[64 * half:64 * half + 64, :], selA[:, c, :],
                                  h2[:, c, 512 * half:512 * half + 512], start=c == 0, stop=c == 2)
                last.then_inc(s["xg_ps"], 1)

            def scatter(i):
                pe.wait_ge(s["y_sb"], i)
                pe.wait_ge(s["sgT"], i)
                for u in range(4):
                    c, half = u // 2, u % 2
                    mm(bank(SUM_BANKS[u]), selGT[:, span(c)], y_sb[:, 512 * half:512 * half + 512],
                       start=True, stop=True).then_inc(s["sc_ps"], 1)
                pe.wait_ge(s["acc_add"], 5 * i + 1)
                for half in range(2):
                    last = mm(bank(SUM_BANKS[4])[32 * half:32 * half + 32, :], selGT[:, span(2)],
                              y_sb[:, 512 * half:512 * half + 512], start=True, stop=True)
                last.then_inc(s["sc_ps"], 1)

            pe.wait_ge(s["acc_add"], 5)
            pe.wait_ge(s["cum"], 2)
            pe.wait_ge(s["bguT"], 1)
            gather(1)
            transposes_x(pe, tr, 1)
            with pe.Fori(0, NE // 2) as pair:
                for par in range(2):
                    gu = (G0, G1)[par].at(0, KT, 2 * FF)
                    dn = DD.at(0, KT, D)
                    first = pe.value_load(cum_i[0:1, bass.ds(pair * 2 + par, 1)], min_val=1, max_val=257)
                    end = pe.value_load(cum_i[0:1, bass.ds(pair * 2 + par + 1, 1)], min_val=2, max_val=257)
                    with pe.Fori(first, end) as i:
                        pe.wait_ge(s["xTm"], i)
                        for k in range(KT):
                            if k % 2 == 0:
                                pe.wait_ge(s[f"gu_in{par}{k // 2}"], pair * 16 + 16)
                            for half in range(2):
                                for t in range(2):
                                    col = FF * t + 512 * half
                                    last = mm(bank(GB + half)[64 * t:64 * t + 64, :], xTm[:, k % 4, k // 4, :],
                                              gu[:, k, col:col + 512], start=k == 0, stop=k == KT - 1)
                            if k in (1, 3, 5):
                                last.then_inc(s["gu_read"], 1)
                        last.then_inc(s["gu_ps"], 1)
                        gather(i + 1, i)
                        pe.wait_ge(s["gu_a"], i)
                        pe.wait_ge(s["gu_v"], i)
                        for k in range(KT):
                            last = tr(bank(TB + k // 4)[:, P * (k % 4):P * (k % 4) + P],
                                      gu_sb[:, k // 4, P * (k % 4):P * (k % 4) + P], ident)
                        last.then_inc(s["hid_ps"], 1)
                        transposes_x(pe, tr, i + 1)
                        scatter(i)
                        pe.wait_ge(s["selg"], i)
                        for c in range(3):
                            last = tr(bank(SB)[:, span(c)], selG[0:ROWS[c], c, :], ident[0:ROWS[c], 0:ROWS[c]])
                        last.then_inc(s["sgT_ps"], 1)
                        pe.wait_ge(s["hid"], i)
                        pe.wait_ge(s["acc_add"], 5 * i + 5)
                        for k in range(KT // 2):
                            for half in range(2):
                                for t in range(2):
                                    kk = k + KT // 2 * t
                                    if half == 0 and k == 0:
                                        pe.wait_ge(s[f"d_in{t}"], pair * 32 + (par + 1) * 16)
                                    last = mm(bank(YB + half)[64 * t:64 * t + 64, :],
                                              hidg.rearrange("p (k t) -> p k t", k=KT)[:, kk, :],
                                              dn[:, kk, 512 * half:512 * half + 512],
                                              start=k == 0, stop=k == KT // 2 - 1)
                        last.then_inc(s["y_ps"], 1)
            rounds = pe.value_load(cum_i[0:1, NE:NE + 1], min_val=2, max_val=257)
            scatter(rounds)

        def transposes_x(pe, tr, i):
            pe.wait_ge(s["xg"], i)
            for j in range(4):
                last = tr(bank(0)[:, P * j:P * j + P], xg[:, P * j:P * j + P], ident)
            last.then_inc(s["xTm_ps"], 1)

        block = ctx.enter_context(nc.Block())

        @block.sync
        def _(sp):
            sp.dma_start(c_sb[0:1, :], c_prompt).then_inc(s["c_in"], 16)
            sp.dma_start(c_sb[1:SEQS, :], c_sample).then_inc(s["c_in"], 16)
            first, last = CONST["ident"], CONST["invcnt"]
            sp.dma_start(consts_sb, consts[:, first[0]:last[0] + last[1]]).then_inc(s["const_in"], 16)

            def ring_load(n):
                kind, g = RING_SLOTS[n]
                if n >= RING:
                    sp.wait_ge(s["slot_used"], n - RING + 1)
                c0, w = (512 * g, 512) if kind == "ada" else IN_SLOTS[g]
                src = (w_ada if kind == "ada" else w_in)[0][:, c0:c0 + w].rearrange("(k p) n -> p k n", p=P)
                sp.dma_start(ring[n % RING][:, :, 0:w], src).then_inc(s[f"ring{n % RING}"], 16)

            for n in range(len(RING_SLOTS)):
                ring_load(n)
                if n == 0:
                    sp.dma_start(x_sb[:, 0:2, :], x_prompt.rearrange("a (b p) d -> p (a b) d", p=P)
                                 ).then_inc(s["x_in"], 16)
                    sp.dma_start(x_sb[0:NS, 2, :], x_sample.rearrange("b t d -> (b t) d")).then_inc(s["x_in"], 16)
            sp.wait_ge(s["slot_used"], len(RING_SLOTS))
            gu_view = w_gu[0].rearrange("e (q j p) n -> e q p j n", p=P, j=2)
            d_view = w_down[0].rearrange("e (q j p) n -> e q p j n", p=P, j=4)
            gu_buf = [G0.at(0, KT, 2 * FF), G1.at(0, KT, 2 * FF)]
            d_buf = DD.at(0, KT, D)

            for q in range(4):
                sp.dma_start(gu_buf[0][:, 2 * q:2 * q + 2, :], gu_view[0, q]).then_inc(s[f"gu_in0{q}"], 16)

            sp.wait_ge(s["tail_rows"], 5)
            tr = tail_rows[0:TAIL, :]
            sp.dma_start(pool_prompt[0, 0], tr[0:PBUF, 0:POOLW]).then_inc(s["tail_st"], 16)
            sp.dma_start(conv_prompt[0, 0], tr[PBUF - 3:PBUF, POOLW:]).then_inc(s["tail_st"], 16)
            for b in range(NSEQ):
                r = PBUF + DSEQ * b
                sp.dma_start(pool_sample[0, b, PBUF - DSEQ:PBUF], tr[r:r + DSEQ, 0:POOLW]).then_inc(s["tail_st"], 16)
                sp.dma_start(conv_sample[0, b], tr[r + 1:r + DSEQ, POOLW:]).then_inc(s["tail_st"], 16)
            sp.dma_start(pool_sample[0, :, 0:PBUF - DSEQ, :], state_pool[0, :, DSEQ:PBUF, :]).then_inc(s["tail_st"], 16)
            sp.wait_ge(s["tail_st"], 16 * (3 + 2 * NSEQ))
            sp.wait_ge(s["modG_st"], 16)
            sp.wait_ge(s["pool_ps"], 2)
            sp.wait_ge(s["s_taps"], 2)
            sp.wait_ge(s["norm_ps"], H + 1)
            for b in range(NSEQ):
                sp.dma_start(Ssm[:, b], state_ssm[0, b].rearrange("h k v -> k h v")).then_inc(s["ssm_in"], 16)
            sp.dma_start(seqmask, cc("seqmask").rearrange("p (b t) -> p b t", b=NSEQ)).then_inc(s["ssm_in"], 16)

            sp.wait_ge(s["s_new"], H)
            sp.dma_start(ssm_sample[0].rearrange("b h k v -> k b h v"), Ssm).then_inc(s["ssm_out"], 16)
            sp.wait_ge(s["ssm_out"], 16)
            sp.dma_start(w_out_sb, w_out[0].rearrange("(k p) n -> p k n", p=P)).then_inc(s["wout_in"], 16)
            sp.wait_ge(s["vn_ps"], 3)
            gate_rows(sp, 0, gm_tok, "gm_in")
            sp.dma_start(rones, cc("ones")).then_inc(s["rt_in"], 16)
            sp.dma_start(rvalid, cc("valid")).then_inc(s["rt_in"], 16)
            sp.dma_start(rbefore, cc("before")).then_inc(s["rt_in"], 16)
            sp.dma_start(rb_row[0:1, :], router_b).then_inc(s["rt_in"], 16)
            sp.dma_start(rw, router_w[0].rearrange("(k p) n -> p k n", p=P)).then_inc(s["rt_in"], 16)
            sp.wait_ge(s["s_new"], H + 1)
            sp.dma_start(ssm_prompt[0, 0].rearrange("h k v -> k h v"), Sp).then_inc(s["ssm_out"], 16)

            sp.wait_ge(s["s_ps"], H + 2)
            for q in range(2):
                sp.dma_start(gu_buf[1][:, 2 * q:2 * q + 2, :], gu_view[1, q]).then_inc(s[f"gu_in1{q}"], 16)

            sp.wait_ge(s["mix_ps"], 3)
            sp.dma_start(bgu_rows, b_gu[0].rearrange("e (c n) -> (e c) n", n=P).rearrange("(q p) n -> p q n", p=P)
                         ).then_inc(s["rt_in"], 16)
            sp.dma_start(b_down_sb[0:NE, :], b_down[0]).then_inc(s["rt_in"], 16)
            for q in range(2):
                sp.dma_start(d_buf[:, 4 * q:4 * q + 4, :], d_view[0, q]).then_inc(s[f"d_in{q}"], 16)
            for c in range(3):
                sp.wait_ge(s["x1"], c + 1)
                n = ROWS[c]
                sp.dma_start(x1_dram[AT[c]:AT[c] + n, :], x_sb[0:n, c, :]).then_inc(s["x1_st"], 16)
            sp.wait_ge(s["ssm_out"], 32)
            sp.wait_ge(s["ssq"], 9)
            for q in range(2, 4):
                sp.dma_start(gu_buf[1][:, 2 * q:2 * q + 2, :], gu_view[1, q]).then_inc(s[f"gu_in1{q}"], 16)
            sp.wait_ge(s["cum"], 2)

            def load_gu(par, nxt, rounds):
                for q in range(4):
                    if q < 3:
                        sp.wait_ge(s["gu_read"], rounds * 3 + (q + 1))
                    else:
                        sp.wait_ge(s["gu_ps"], rounds)
                    sp.dma_start(gu_buf[par][:, 2 * q:2 * q + 2, :],
                                 gu_view[bass.ds(nxt, 1), q].rearrange("e p j n -> p (e j) n")
                                 ).then_inc(s[f"gu_in{par}{q}"], 16)

            def load_d(nxt, rounds):
                for q in range(2):
                    if q == 0:
                        sp.wait_ge(s["y_ps"], rounds)
                    sp.dma_start(d_buf[:, 4 * q:4 * q + 4, :],
                                 d_view[bass.ds(nxt, 1), q].rearrange("e p j n -> p (e j) n")
                                 ).then_inc(s[f"d_in{q}"], 16)

            with sp.Fori(0, NE // 2 - 1) as pair:
                for par in range(2):
                    through = sp.value_load(ends_i[0:1, bass.ds(pair * 2 + par, 1)], min_val=1, max_val=256)
                    load_gu(par, pair * 2 + par + 2, through)
                    load_d(pair * 2 + par + 1, through)
            through = sp.value_load(ends_i[0:1, NE - 2:NE - 1], min_val=1, max_val=256)
            load_d(NE - 1, through)

            sp.wait_ge(s["gu_ps"], through)
            sp.dma_start(fin_x[:, 0:2, :], x1_dram[0:SEQ].rearrange("(b p) d -> p b d", p=P)).then_inc(s["fin_in"], 16)
            sp.dma_start(fin_x[0:NS, 2, :], x1_dram[SEQ:TOK]).then_inc(s["fin_in"], 16)
            gate_rows(sp, 1, fin_g, "fin_in")
            for c in range(3):
                sp.wait_ge(s["fin_y"], c + 1)
                dst = y_prompt[0, P * c:P * c + P, :] if c < 2 else y_sample.rearrange("b t d -> (b t) d")
                sp.dma_start(dst, fin_x[0:ROWS[c], c, :]).then_inc(s["y_st"], 16)
            sp.wait_ge(s["y_st"], 48)

        @block.tensor
        def _(pe):
            mm, tr = pe.matmul, pe.transpose

            pe.wait_ge(s["const_in"], 16 * N_CONST)
            pe.wait_ge(s["c_silu"], 1)
            for k in range(KT):
                last = tr(bank(0)[:, SEQS * k:SEQS * (k + 1)], c_sb[0:SEQS, P * k:P * (k + 1)], ident[0:SEQS, 0:SEQS])
            last.then_inc(s["setup_ps"], 1)
            pe.wait_ge(s["vec_in"], 16 * N_VEC)
            tr(bank(1)[:, 0:66], v1[0:66, :], ident[0:66, 0:66])
            tr(bank(1)[:, 66:138], v2[0:72, :], ident[0:72, 0:72]).then_inc(s["setup_ps"], 1)
            pe.wait_ge(s["hist_in"], 16 * N_HIST)
            for m in range(CT):
                last = tr(bank(2)[:, 24 * m:24 * m + 24], hist_rows[0:24, P * m:P * m + P], ident[0:24, 0:24])
            last.then_inc(s["setup_ps"], 1)
            for m in range(NU):
                last = tr(bank(3)[:, 120 * m:120 * m + 120], phist_rows[0:120, P * m:P * m + P], ident[0:120, 0:120])
            last.then_inc(s["setup_ps"], 1)

            def ada(i):
                n = ADA_SLOTS[i]
                pe.wait_ge(s[f"ring{n % RING}"], 16 * (n // RING + 1))
                if i < 2:
                    pe.wait_ge(s["setup_sb"], 1)
                    pe.wait_ge(s["setup_sb"], 2)
                else:
                    pe.wait_ge(s["mod_sb"], i - 1)
                for k in range(KT):
                    for j in range(4):
                        last = mm(bank(i % 2)[32 * j:32 * j + 32, 0:P], cT[:, k, :],
                                  ring[n % RING][:, k, P * j:P * j + P], start=k == 0, stop=k == KT - 1)
                last.then_inc(s["slot_used"], 1)

            MODT = [0, 1, 2, 3, 6, 7, 8, 9]

            def ada_T(i):
                t = MODT.index(i)
                pe.wait_ge(s["mod_sb"], i + 1)
                if t == 0:
                    pe.wait_ge(s["setup_sb"], 3)
                if t == 4:
                    pe.wait_ge(s["modT"], 1)
                tr(bank(2)[:, P * (t % 4):P * (t % 4) + P], mraw, ident).then_inc(s["modT_ps"], 1)

            ada(0)
            pe.wait_ge(s["xn"], 3)
            pe.wait_ge(s["setup_sb"], 4)
            for k in range(KT):
                last = tr(bank(3)[:, 256 + NS * k:256 + NS * (k + 1)], xn[0:NS, 2, P * k:P * k + P], ident[0:NS, 0:NS])
            last.then_inc(s["xT_ps"], 1)
            for k in range(KT):
                for c in range(2):
                    at = 256 * (k % 2) + P * c
                    last = tr(bank(4 + k // 2)[:, at:at + P], xn[:, c, P * k:P * k + P], ident)
                if k % 2:
                    last.then_inc(s["xT_ps"], 1)
            for i in range(ADA_FIRST):
                if i:
                    ada(i)
                ada_T(i)

            def projection(u):
                slot, last_of_slot = unit_slot(u)
                pe.wait_ge(s[f"ring{slot % RING}"], 16 * (slot // RING + 1))
                if u >= 4:
                    wait_unit_read(pe, u - 4)
                w = ring[slot % RING]
                for k in range(KT):
                    if u in Z_UNITS:
                        c, cols = Z_UNITS.index(u) % 3, (IN_SLOTS[0][1] if u < 3 else 512)
                        last = mm(unit_bank(u)[0:ROWS[c], 0:cols], hT[:, k, span(c)], w[:, k, 0:cols],
                                  start=k == 0, stop=k == KT - 1)
                    else:
                        i = (u - 3) % 4
                        last = mm(unit_bank(u)[:, 0:TOK], w[:, k, P * i:P * i + P], hT[:, k, :],
                                  start=k == 0, stop=k == KT - 1)
                last.then_inc(s["slot_used" if last_of_slot else "proj_ps"], 1)

            def norms(p):
                if p:
                    pe.wait_ge(s["norm_root"], p)
                else:
                    pe.wait_ge(s["hT_s"], 1)
                if p < H:
                    pe.wait_ge(s["sq"], 2 * p + 2)
                    for i in range(2):
                        last = mm(bank(3)[:, SEQ * i:SEQ * i + SEQ], ones, sq[(2 * p + i) % 4][:, 0:SEQ],
                                  start=True, stop=True)
                else:
                    pe.wait_ge(s["sq"], 2 * H + 1)
                    last = mm(bank(3)[:, 0:2 * H * NS], ones, sq_s, start=True, stop=True)
                last.then_inc(s["norm_ps"], 1)

            pe.wait_ge(s["hT_a"], KT)
            pe.wait_ge(s["hT_s"], 1)
            due = None
            for n in range(ADA_FIRST, len(RING_SLOTS)):
                kind, i = RING_SLOTS[n]
                if kind == "ada":
                    if due is not None:
                        ada_T(due)
                    ada(i)
                    due = i if i in MODT else None
                for u in units_of(n):
                    projection(u)
                    if due is not None:
                        ada_T(due)
                        due = None
                    h = u - 3 - NU - NORM_LAG
                    if h in range(0, 2 * H, 2):
                        norms(h // 2)
                    if u == 3 + NU + SAMPLE_NORM:
                        norms(H)

            pe.wait_ge(s["gates"], 2)
            pe.wait_ge(s["norm_root"], H + 1)
            for c in range(2):
                mm(bank(3)[:, 8 * c:8 * c + H], upto, gg[:, c, :], start=True, stop=True)
                mm(bank(3)[:, 32 + 8 * c:32 + 8 * c + H], after, gg[:, c, :], start=True, stop=True)
                mm(bank(3)[:, 64 + 8 * c:64 + 8 * c + H], ones, gg[:, c, :], start=True, stop=True)
            mm(bank(3)[0:NS, 16:16 + H], upto_s[0:NS, :], gg[0:NS, 2, :], start=True, stop=True)
            mm(bank(3)[0:NS, 48:48 + H], after_s[0:NS, :], gg[0:NS, 2, :], start=True, stop=True)
            mm(bank(3)[:, 96:96 + NSEQ * H], ones[0:NS, :], gseq[0:NS].rearrange("p b h -> p (b h)"),
               start=True, stop=True).then_inc(s["gate_ps"], 1)

            for g in range(6):
                c, b = g % 3, 4 * (g % 2)
                if g == 0:
                    pe.wait_ge(s["mod_sb"], 12)
                    pe.wait_ge(s["qk_n"], H + 1)
                if g == 1:
                    wait_unit_read(pe, N_UNITS - 1)
                if g == 3:
                    pe.wait_ge(s["silu_done"], CT)
                    pe.wait_ge(s["s_silu"], 2)
                if g >= 2:
                    pe.wait_ge(s["kv_tok"], g - 1)
                for h in range(H):
                    src = qkvT[:, (6 if g < 3 else 12) + h, span(c)]
                    last = tr(bank(b, 2)[0:ROWS[c], P * h:P * h + P], src, ident)
                last.then_inc(s["kvT_ps"], 1)

            pe.wait_ge(s["pooled"], 1)
            pe.wait_ge(s["wpool_in"], 64)
            for m in range(NU):
                mm(bank(6 + m)[:, 0:TOK], wpbd[:, m, :], pooled[:, m, :], start=True, stop=True
                   ).then_inc(s["pool_ps"], 1)

            for q in range(5):
                b = TAIL_BANKS[q]
                if q == 0:
                    pe.wait_ge(s["modT"], 2)
                elif q == 1:
                    pe.wait_ge(s["egates"], 1)
                elif q < 4:
                    pe.wait_ge(s["poolT"], q - 1)
                else:
                    pe.wait_ge(s["tail_rows"], 1)
                for i in range(4):
                    last = tr(bank(b)[0:TAIL, P * i:P * i + P], tail[:, 4 * q + i, :], ident)
                last.then_inc(s["tailT_ps"], 1)

            for o in range(3):
                c = ORDER[o]
                n = ROWS[c]
                L, T, U, Mk, Pb, QT, A, B = buffers(o)
                if o == 0:
                    pe.wait_ge(s["kv_tok"], 6)
                    pe.wait_ge(s["egates"], 1)
                    pe.wait_ge(s["tail_rows"], 5)
                else:
                    pe.wait_ge(s["u0"], o)
                pe.wait_ge(s["ga"], o + 1)
                ga = Mk[0:n].rearrange("p h t -> p (h t)")
                for lo in range(0, H * n, 512):
                    hi = min(lo + 512, H * n)
                    last = mm(bank(0, 2)[0:n, lo:hi], masks(o)[0][0:n, 0:n], ga[:, lo:hi], start=True, stop=True)
                last.then_inc(s["diff_ps"], 1)
                if o >= 1:
                    pe.wait_ge(s["lmat"], o)
                for h in range(H):
                    last = mm(heads(2, n, n)[:, h, :], qkvT[:, H + h, span(c)], qkvT[:, H + h, span(c)],
                              start=True, stop=True)
                last.then_inc(s["kk_ps"], 1)
                if o >= 1:
                    pe.wait_ge(s["qkd"], o)
                for h in range(H):
                    last = mm(heads(4, n, n)[:, h, :], qkvT[:, h, span(c)], qkvT[:, H + h, span(c)],
                              start=True, stop=True)
                last.then_inc(s["qk_ps"], 1)
                pe.wait_ge(s["qkd"], o + 1)
                if o >= 1:
                    pe.wait_ge(s["qkdT"], o)
                for h in range(H):
                    last = tr(heads(6, n, n)[:, h, :], dmat(o)[0:n, h, :], ident[0:n, 0:n])
                last.then_inc(s["qkdT_ps"], 1)
                pe.wait_ge(s["t0"], o + 1)
                pe.wait_ge(s["dexp"], o + 1)
                for h in range(H):
                    last = tr(heads(0, n, n)[:, h, :], T[0:n, h, :], ident[0:n, 0:n])
                last.then_inc(s["u0_ps"], 1)
                if o == 0:
                    levels(pe, mm, [0])
            levels(pe, mm, range(1, len(STEPS)))

            pe.wait_ge(s["ssm_in"], 16 * (NSEQ + 1))
            pe.wait_ge(s["tu_done"], len(STEPS))
            for h in range(H):
                pe.wait_ge(s["kqm"], h + 1)
                for b in range(NSEQ):
                    last = mm(bank(0, 2)[0:2 * NS, P * h:P * h + P], kq_mask[h % 2][:, b, :], Ssm[:, b, h, :],
                              start=b == 0, stop=b == NSEQ - 1)
                last.then_inc(s["ks_ps"], 1)

            def new_values(o):
                n, c, U = ROWS[ORDER[o]], ORDER[o], buffers(o)[2]
                pe.wait_ge(s["rr"], o + 1)
                if o:
                    pe.wait_ge(s["vn"], o)
                for h in range(H):
                    last = mm(heads(2, n)[:, h, :], U[0:n, h, :], tokV[0:n, c, P * h:P * h + P], start=True, stop=True)
                last.then_inc(s["vn_ps"], 1)

            def outputs(o):
                n, c, QT = ROWS[ORDER[o]], ORDER[o], buffers(o)[5]
                pe.wait_ge(s["vn"], o + 1)
                if o >= 1:
                    pe.wait_ge(s["o_tok"], o)
                for h in range(H):
                    last = mm(heads(4, n)[:, h, :], QT[0:n, h, :], tokV[0:n, c, P * h:P * h + P], start=True, stop=True)
                last.then_inc(s["o_ps"], 1)

            def state_products(o):
                c = ORDER[o]
                pe.wait_ge(s["kdec"], o + 1)
                pe.wait_ge(s["vn"], o + 1)
                for h in range(H):
                    last = mm(heads(0, P)[:, h, :], tokK[:, c, P * h:P * h + P], tokV[:, c, P * h:P * h + P],
                              start=True, stop=True)
                last.then_inc(s["s_ps"], 1)

            new_values(0)
            new_values(1)
            outputs(0)
            pe.wait_ge(s["qs_sb"], 1)
            state_products(1)
            pe.wait_ge(s["kdec"], 1)
            pe.wait_ge(s["sp_e"], 1)
            for h in range(H):
                pe.wait_ge(s["vmask"], h + 1)
                if h >= 2:
                    pe.wait_ge(s["s_new"], h - 1)
                vm = vmask[h % 2].rearrange("p b v -> p (b v)")
                for half in range(2):
                    last = mm(bank((6, 0)[h % 2] + half), tokK[:, 2, P * h:P * h + P],
                              vm[:, 512 * half:512 * half + 512], start=True, stop=True)
                last.then_inc(s["s_ps"], 1)
            outputs(1)
            pe.wait_ge(s["s_new"], H)
            for h in range(H):
                last = mm(heads(0, P)[:, h, :], qkvT[:, H + h, span(1)], Sp[:, h, :], start=True, stop=True)
            last.then_inc(s["ks_ps"], 1)
            for h in range(H):
                last = mm(heads(6, P)[:, h, :], qkvT[:, h, span(1)], Sp[:, h, :], start=True, stop=True)
            last.then_inc(s["ks_ps"], 1)
            new_values(2)
            outputs(2)
            state_products(2)

            for o in range(3):
                c = ORDER[o]
                n = ROWS[c]
                pe.wait_ge(s["gated"], o + 1)
                pe.wait_ge(s["vn"], 3)
                if o >= 1:
                    pe.wait_ge(s["oT"], o)
                for h in range(H):
                    last = tr(bank(2, 2)[:, n * h:n * h + n], z[0:n, c, P * h:P * h + P], ident[0:n, 0:n])
                last.then_inc(s["oT_ps"], 1)

            pe.wait_ge(s["oT"], 3)
            pe.wait_ge(s["wout_in"], 16)
            pe.wait_ge(s["o_tok"], 3)
            pe.wait_ge(s["qs_sb"], 2)
            pe.wait_ge(s["s_new"], H + 1)
            for c in range(3):
                b = (4, 6, 0)[c]
                for k in range(KT):
                    lhsT = poolT[:, k, span(c)] if k < NU else oT[:, k - NU, span(c)]
                    if c < 2:
                        for half in range(2):
                            last = mm(bank(b + half), lhsT, w_out_sb[:, k, 512 * half:512 * half + 512],
                                      start=k == 0, stop=k == KT - 1)
                    else:
                        for j in range(4):
                            last = mm(bank(b)[32 * j:32 * j + 32, 0:256], lhsT, w_out_sb[:, k, 256 * j:256 * j + 256],
                                      start=k == 0, stop=k == KT - 1)
                last.then_inc(s["mix_ps"], 1)

            pe.wait_ge(s["xn2"], 3)
            for k in range(KT):
                last = tr(bank(2)[:, NS * k:NS * (k + 1)], h2[0:NS, 2, P * k:P * k + P], ident[0:NS, 0:NS])
            last.then_inc(s["x2T_ps"], 1)
            for k in range(KT):
                for c in range(2):
                    at = 256 * (k % 2) + P * c
                    last = tr(bank(4 + k // 2)[:, at:at + P], h2[:, c, P * k:P * k + P], ident)
                if k % 2:
                    last.then_inc(s["x2T_ps"], 1)
            pe.wait_ge(s["h2T"], KT + 1)
            pe.wait_ge(s["rt_in"], 16 * 7)
            for k in range(KT):
                last = mm(bank(3)[0:NE, 0:TOK], rw[:, k, :], h2T[:, k, :], start=k == 0, stop=False)
                if k < 3:
                    last.then_inc(s["gu_read"], 1)
            for c in range(3):
                last = mm(bank(3)[0:NE, span(c)], rb_row[0:1, :], rones[0:1, 0:ROWS[c]], start=False, stop=c == 2)
            last.then_inc(s["router_ps"], 1)
            for c in range(3):
                for k in range(KT):
                    last = tr(bank((4, 6, 0)[c] + k // 4)[0:ROWS[c], P * (k % 4):P * (k % 4) + P],
                              h2T[:, k, span(c)], ident)
                last.then_inc(s["h2_ps"], 1)
            pe.wait_ge(s["rl_sb"], 1)
            for c in range(3):
                last = tr(bank(2)[0:ROWS[c], NE * c:NE * c + NE], lgT[0:NE, span(c)], ident[0:NE, 0:NE])
            last.then_inc(s["router_ps"], 1)
            pe.wait_ge(s["h2"], 3)
            for q in range(4):
                last = tr(bank(4)[:, P * q:P * q + P], bgu_rows[:, q, :], ident)
            last.then_inc(s["router_ps"], 1)
            pe.wait_ge(s["top_e"], 1)
            for c in range(3):
                for e in range(c + 1):
                    last = mm(bank(5)[0:P, NE * c:NE * c + NE], rbefore if e == c else rones, sel01[:, e, :],
                              start=e == 0, stop=e == c)
            last.then_inc(s["router_ps"], 1)
            for c in range(3):
                last = mm(bank(6)[:, 0:NE], rones, sel01[:, c, :], start=c == 0, stop=c == 2)
            last.then_inc(s["router_ps"], 1)
            pe.wait_ge(s["gate_done"], 1)
            for c in range(3):
                last = tr(bank(7)[0:NE, AT[c]:AT[c] + ROWS[c]], gate[0:ROWS[c], c, :], ident[0:ROWS[c], 0:ROWS[c]])
            last.then_inc(s["router_ps"], 1)
            pe.wait_ge(s["gT"], 1)
            for u in range(5):
                if u >= 2:
                    pe.wait_ge(s["acc_add"], u - 1)
                for half in ((u % 2,) if u < 4 else (0, 1)):
                    out = bank(u % 2) if u < 4 else bank(0)[32 * half:32 * half + 32, :]
                    last = mm(out, gT[0:NE, span(u // 2)], b_down_sb[0:NE, 512 * half:512 * half + 512],
                              start=True, stop=True)
                last.then_inc(s["sc_ps"], 1)

            experts_pe(pe, mm, tr)

        @block.scalar
        def _(act):
            fn = act.activation
            own = Chain(act, s["ch_act"])

            act.dma_start(hist_rows[0:24, :], state_conv[0].rearrange("b t c -> (b t) c")).then_inc(s["hist_in"], 16)
            act.dma_start(phist_rows[0:120, :], state_pool[0].rearrange("b t c -> (b t) c")).then_inc(s["hist_in"], 16)
            vr = b_ada.rearrange("a (r n) -> (a r) n", n=P)
            act.dma_start(v1[0:48, :], vr).then_inc(s["vec_in"], 16)
            act.dma_start(v1[48:56, :], g_pre_mix.rearrange("a (r n) -> (a r) n", n=P)).then_inc(s["vec_in"], 16)
            act.dma_start(v1[56:64, :], g_pre_ffn.rearrange("a (r n) -> (a r) n", n=P)).then_inc(s["vec_in"], 16)
            act.dma_start(v1[64:66, :], pool_scale.rearrange("a (r n) -> (a r) n", n=P)).then_inc(s["vec_in"], 16)
            act.dma_start(v2[0:72, :], conv_w.rearrange("a j (r n) -> (a j r) n", n=P)).then_inc(s["vec_in"], 16)
            act.wait_ge(s["c_in"], 32)
            fn(c_sb[0:SEQS, :], c_sb[0:SEQS, :], ACT.Silu).then_inc(s["c_silu"], 1)
            def root(t, c0, c1, n=P):
                fn(t[0:n, 4 + c0:4 + c1], t[0:n, c0:c1], ACT.Sqrt, bias=st[0:n, 12:13]).then_inc(s["root"], 1)

            act.wait_ge(s["x_in"], 32)
            act.wait_ge(s["stats_set"], 1)
            for c in range(3):
                n = ROWS[c]
                if c:
                    act.wait_ge(s["ssq"], c)
                fn(junk[0:n, :], x_sb[0:n, c, :], ACT.Square, scale=D ** -0.5, accum_out=st[0:n, c:c + 1]
                   ).then_inc(s["ssq"], 1)
            act.wait_ge(s["ssq"], 3)
            root(st, 0, 3)

            act.wait_ge(s["modT"], 1)
            for k in range(KT):
                act.wait_ge(s["xT_ps"], 2 + k // 2)
                fn(hT[:, k, 0:SEQ], bank(4 + k // 2)[:, 256 * (k % 2):256 * (k % 2) + 256], ACT.Identity,
                   scale=modT[:, 1, k, 0:1], bias=modT[:, 0, k, 0:1]).then_inc(s["hT_a"], 1)

            def norm_root(p, n):
                act.wait_ge(s["norm_ps"], p + 1)
                if p:
                    act.wait_ge(s["qk_n"], p)
                fn(rnorm[:, 0:n], bank(3)[:, 0:n], ACT.Sqrt, bias=st[:, 12:13]).then_inc(s["norm_root"], 1)

            def silu_tile(h):
                act.wait_ge(s["conv_done"], h + 1)
                fn(qkvT[:, h, 0:SEQ], qkvT[:, h, 0:SEQ], ACT.Silu).then_inc(s["silu_done"], 1)

            act.wait_ge(s["setup_sb"], 4)
            for u in range(N_UNITS):
                wait_unit(act, u)
                ps = unit_bank(u)
                if u in Z_UNITS:
                    c = Z_UNITS.index(u) % 3
                    n = ROWS[c]
                    if u < 3:
                        fn(z[0:n, c, 512:GW], ps[0:n, 0:256], ACT.Silu)
                        act.copy(ab[0:n, c, :], ps[0:n, 256:268]).then_inc(s["z_sb"], 1)
                    else:
                        fn(z[0:n, c, 0:512], ps[0:n, 0:512], ACT.Silu).then_inc(s["z_sb"], 1)
                elif u < 3 + NU:
                    m = u - 3
                    act.copy(tail[:, m, :], ps[:, SEQ - PBUF:TOK])
                    act.copy(uext[:, m, PBUF:], ps[:, 0:SEQ])
                    act.copy(uexs[:, m, :, PBUF:], ps[:, SEQ:TOK].rearrange("p (b t) -> p b t", b=NSEQ)
                             ).then_inc(s["u_sb"], 1)
                else:
                    h = u - 3 - NU
                    act.copy(tail[:, NU + h, :], ps[:, SEQ - PBUF:TOK])
                    act.copy(cexs[:, h, :, 3:], ps[:, SEQ:TOK].rearrange("p (b t) -> p b t", b=NSEQ))
                    tap = 66 + 3 * CT + h
                    fn(qkvT[:, h, 0:SEQ], ps[:, 0:SEQ], ACT.Identity, scale=vecT[:, tap:tap + 1]
                       ).then_inc(s["tap3"], 1)
                    if h >= 1:
                        silu_tile(h - 1)
                    if h - NORM_LAG in range(0, 2 * H, 2):
                        norm_root((h - NORM_LAG) // 2, 2 * SEQ)
                    if h == SAMPLE_NORM:
                        norm_root(H, 2 * H * NS)
                    if h == 4:
                        act.wait_ge(s["softplus_v"], 1)
                        act.wait_ge(s["small_in"], 16 * N_SMALL)
                        fn(spt[1], spt[1], ACT.Exp)
                        fn(beta, ab[:, :, H:2 * H], ACT.Exp, scale=-1.0)
                        fn(alog, alog, ACT.Exp).then_inc(s["softplus_a"], 1)
                    if h == 6:
                        act.wait_ge(s["softplus_v"], 2)
                        fn(spt[1], spt[1], ACT.Ln).then_inc(s["softplus_a"], 1)
                    if h == SAMPLE_TAPS + 1:
                        act.wait_ge(s["s_taps"], 1)
                        fn(qkvT[:, 0:2 * H, SEQ:TOK], s_tap[:, 0:2 * H], ACT.Silu).then_inc(s["s_silu"], 1)
            silu_tile(CT - 1)
            act.wait_ge(s["s_taps"], 2)
            fn(qkvT[:, 2 * H:, SEQ:TOK], s_tap[:, 2 * H:], ACT.Silu).then_inc(s["s_silu"], 1)

            act.wait_ge(s["gate_ps"], 1)
            ps = bank(3)
            two = lambda at: ps[:, at:at + 16].rearrange("p (c h) -> p c h", c=2)[:, :, 0:H]
            fn(egc[:, 0:2, :], two(0), ACT.Exp)
            fn(egr[:, 0:2, :], two(32), ACT.Exp)
            fn(egl[:, 0:2, :], two(64), ACT.Exp)
            fn(egc[0:NS, 2, :], ps[0:NS, 16:16 + H], ACT.Exp)
            fn(egr[0:NS, 2, :], ps[0:NS, 48:48 + H], ACT.Exp)
            fn(egls, ps[:, 96:96 + NSEQ * H].rearrange("p (b h) -> p b h", b=NSEQ), ACT.Exp
               ).then_inc(s["egates"], 1)

            act.wait_ge(s["zeroed"], 1)
            for g in range(6):
                c = g % 3
                n = ROWS[c]
                act.wait_ge(s["kvT_ps"], g + 1)
                act.copy((tokK if g < 3 else tokV)[0:n, c, :], bank(4 * (g % 2), 2)[0:n, 0:GW]
                         ).then_inc(s["kv_tok"], 1)

            for m in range(NU):
                act.wait_ge(s["pool_ps"], m + 1)
                fn(poolT[:, m, :], bank(6 + m)[:, 0:TOK], ACT.Identity, scale=vecT[:, 64 + m:65 + m]
                   ).then_inc(s["poolT"], 1)
            for q in range(5):
                act.wait_ge(s["tailT_ps"], q + 1)
                act.copy(tail_rows[0:TAIL, 512 * q:512 * q + 512], bank(TAIL_BANKS[q])[0:TAIL, :]
                         ).then_inc(s["tail_rows"], 1)
            act.wait_ge(s["modG"], 4)
            act.dma_start(gm_dram.rearrange("j q u n -> (j q) u n"), modG).then_inc(s["modG_st"], 16)

            for o in range(3):
                n = ROWS[ORDER[o]]
                L, T, U, Mk, Pb, QT, A, B = buffers(o)
                act.wait_ge(s["diff_ps"], o + 1)
                if o >= 1:
                    act.wait_ge(s["qkdT_ps"], o)
                fn(dmat(o)[0:n], heads(0, n, n), ACT.Exp).then_inc(s["dexp"], 1)
                act.wait_ge(s["qkdT_ps"], o + 1)
                act.copy(QT[0:n], heads(6, n, n)).then_inc(s["qkdT"], 1)
                act.wait_ge(s["u0_ps"], o + 1)
                act.copy(U[0:n], heads(0, n, n)).then_inc(s["u0"], 1)
                if o == 0:
                    act.wait_ge(s["p1_ps"], 1)
                    act.wait_ge(s["tailT_ps"], 5)
                    act.copy(Pb[0:n], heads(A, n, n)).then_inc(s["p1"], 1)
            for i in range(1, len(STEPS)):
                o = STEPS[i][0]
                n = ROWS[ORDER[o]]
                _, _, _, _, Pb, _, A, _ = buffers(o)
                act.wait_ge(s["p1_ps"], i + 1)
                act.copy(Pb[0:n], heads(A, n, n)).then_inc(s["p1"], 1)

            def values(o):
                n, c = ROWS[ORDER[o]], ORDER[o]
                act.wait_ge(s["vn_ps"], o + 1)
                act.copy(tokV[0:n, c, :], bank(2, 2)[0:n, 0:GW]).then_inc(s["vn"], 1)

            def output_root(o):
                n, c = ROWS[ORDER[o]], ORDER[o]
                act.wait_ge(s["o_ms"], o + 1)
                fn(orr[0:n, c, :], orr[0:n, c, :], ACT.Sqrt, bias=st[0:n, 12:13]).then_inc(s["o_root"], 1)

            values(0)
            values(1)
            act.wait_ge(s["s_ps"], 1)
            act.copy(Sp, heads(0, P)).then_inc(s["sp_e"], 1)
            output_root(0)
            output_root(1)
            values(2)
            output_root(2)

            for o in range(3):
                n, c = ROWS[ORDER[o]], ORDER[o]
                act.wait_ge(s["oT_ps"], o + 1)
                act.copy(oT[:, :, span(c)], bank(2, 2)[:, 0:H * n].rearrange("p (h t) -> p h t", h=H)
                         ).then_inc(s["oT"], 1)

            for c in range(3):
                n = ROWS[c]
                act.wait_ge(s["mix_ps"], c + 1)
                if c == 2:
                    for j in range(4):
                        last = act.copy(mix_s[0:NS, 256 * j:256 * j + 256], bank(0)[32 * j:32 * j + 32, 0:256])
                    own(last)
                act.wait_ge(s["ssq"], 3 + c)
                fn(mixjunk[0:n, :], mix_s[0:n, :] if c == 2 else bank((4, 6)[c], 2), ACT.Square, scale=D ** -0.5,
                   accum_out=st[0:n, c:c + 1]).then_inc(s["ssq"], 1)
                act.wait_ge(s["ssq"], 4 + c)
                root(st, c, c + 1, n)
            for c in range(3):
                n = ROWS[c]
                act.wait_ge(s["x1"], c + 1)
                act.wait_ge(s["ssq"], 6 + c)
                fn(mixjunk[0:n, :], x_sb[0:n, c, :], ACT.Square, scale=D ** -0.5, accum_out=st[0:n, c:c + 1]
                   ).then_inc(s["ssq"], 1)
            act.wait_ge(s["ssq"], 9)
            root(st, 0, 3)

            for k in range(KT):
                act.wait_ge(s["x2T_ps"], 2 + k // 2)
                fn(h2T[:, k, 0:SEQ], bank(4 + k // 2)[:, 256 * (k % 2):256 * (k % 2) + 256], ACT.Identity,
                   scale=modT[:, 3, k, 0:1], bias=modT[:, 2, k, 0:1]).then_inc(s["h2T"], 1)
            act.wait_ge(s["rt_in"], 16 * 7)
            act.wait_ge(s["router_ps"], 1)
            act.wait_ge(s["x1_st"], 48)
            act.copy(lgT[0:NE, :], bank(3)[0:NE, 0:TOK]).then_inc(s["rl_sb"], 1)
            for c in range(3):
                act.wait_ge(s["h2_ps"], c + 1)
                act.copy(h2[0:ROWS[c], c, :], bank((4, 6, 0)[c], 2)[0:ROWS[c], :]).then_inc(s["h2"], 1)
            act.wait_ge(s["router_ps"], 3)
            act.copy(bguT, bank(4)).then_inc(s["bguT"], 1)
            act.wait_ge(s["gex"], 1)
            fn(exg, exg, ACT.Exp).then_inc(s["gex"], 1)
            act.wait_ge(s["router_ps"], 6)
            act.copy(gT[0:NE, :], bank(7)[0:NE, 0:TOK]).then_inc(s["gT"], 1)
            act.wait_ge(s["cum"], 2)

            def take_x(i):
                act.wait_ge(s["xg_ps"], i)
                act.copy(xg, bank(0)).then_inc(s["xg"], 1)
                act.wait_ge(s["xTm_ps"], i)
                act.copy(xTm.rearrange("p j h t -> p (j h t)"), bank(0)).then_inc(s["xTm"], 1)

            act.wait_ge(s["y_sb"], 1)
            take_x(1)
            with act.Fori(0, NE // 2) as pair:
                for par in range(2):
                    first = act.value_load(cum_i[0:1, bass.ds(pair * 2 + par, 1)], min_val=1, max_val=257)
                    end = act.value_load(cum_i[0:1, bass.ds(pair * 2 + par + 1, 1)], min_val=2, max_val=257)
                    with act.Fori(first, end) as i:
                        act.wait_ge(s["gu_ps"], i)
                        act.copy(gu_sb[:, 0, :], bank(2)).then_inc(s["gu_a"], 1)
                        take_x(i + 1)
                        act.wait_ge(s["g_ready"], i)
                        fn(sig, hidg, ACT.Sigmoid, scale=ALPHA).then_inc(s["sig"], 1)
                        act.wait_ge(s["sgT_ps"], i + 1)
                        act.copy(selGT, bank(1)[:, 0:TOK]).then_inc(s["sgT"], 1)
                        act.wait_ge(s["y_ps"], i)
                        act.copy(y_sb, bank(6, 2)).then_inc(s["y_sb"], 1)

            rounds = act.value_load(cum_i[0:1, NE:NE + 1], min_val=2, max_val=257)
            act.wait_ge(s["fin_in"], 16 * 20)
            for c in range(3):
                n = ROWS[c]
                act.wait_ge(s["acc_add"], rounds * 5 + 2 * c + 2)
                act.wait_ge(s["ssq"], 9 + c)
                fn(fin_junk[0:n, :], acc[0:n, c, :], ACT.Square, scale=D ** -0.5, accum_out=fst[0:n, c:c + 1]
                   ).then_inc(s["ssq"], 1)
                act.wait_ge(s["ssq"], 10 + c)
                root(fst, c, c + 1, n)

        @block.vector
        def _(v):
            own = Chain(v, s["ch_dve"])
            tt, ts, stt = v.tensor_tensor, v.tensor_scalar, v.scalar_tensor_tensor

            def rstd(t, c0, c1, root, n=P):
                v.wait_ge(s["root"], root)
                return v.reciprocal(t[0:n, 4 + c0:4 + c1], t[0:n, 4 + c0:4 + c1])

            def per_head(a, n, m=P):
                return a.unsqueeze(2).to_broadcast([n, H, m])

            def every_head(a, n, m=P):
                return a.unsqueeze(1).to_broadcast([n, H, m])

            own(v.memset(st[:, :], 0.0))
            v.memset(st[:, 12:13], EPS)
            v.memset(fst[:, :], 0.0).then_inc(s["stats_set"], 1)

            own(v.memset(cT, 0.0))
            v.memset(ab, 0.0)
            v.wait_ge(s["setup_ps"], 1)
            v.tensor_copy(cT[:, :, 0:SEQS], bank(0)[:, 0:KT * SEQS].rearrange("p (k q) -> p k q", k=KT)
                          ).then_inc(s["setup_sb"], 1)
            v.wait_ge(s["setup_ps"], 2)
            v.tensor_copy(vecT, bank(1)[:, 0:138]).then_inc(s["setup_sb"], 1)
            v.wait_ge(s["setup_ps"], 3)
            v.tensor_copy(cexs[:, :, :, 0:3], bank(2)[:, 0:432].rearrange("p (m b t) -> p m b t", m=CT, b=NSEQ)
                          ).then_inc(s["setup_sb"], 1)
            v.wait_ge(s["setup_ps"], 4)
            v.tensor_copy(uexs[:, :, :, 0:PBUF], bank(3)[:, 0:240].rearrange("p (m b t) -> p m b t", m=NU, b=NSEQ)
                          ).then_inc(s["setup_sb"], 1)
            own(rstd(st, 0, 3, 1))
            for c in range(3):
                n = ROWS[c]
                ts(xn[0:n, c, :], x_sb[0:n, c, :], st[0:n, 4 + c:5 + c], None, ALU.mult).then_inc(s["xn"], 1)

            MODT = [0, 1, 2, 3, 6, 7, 8, 9]

            def mod_evac(i):
                v.wait_ge(s["slot_used"], ADA_SLOTS[i] + 1)
                ps = bank(i % 2)[:, 0:P]
                if i in MODT:
                    if MODT.index(i):
                        v.wait_ge(s["modT_ps"], MODT.index(i))
                    v.tensor_copy(mraw, ps).then_inc(s["mod_sb"], 1)
                else:
                    u = (4, 5, 10, 11).index(i)
                    tt(modG[:, u, :], ps, b_row[:, u, :], ALU.add).then_inc(s["mod_sb"], 1)
                    v.wait_ge(s["mod_sb"], i + 1)
                    tt(modG[:, u, :], modG[:, u, :], gpost[:, u, :], ALU.mult).then_inc(s["modG"], 1)

            def mod_transposed(g, b0, gvec):
                v.wait_ge(s["modT_ps"], 4 * (g // 2) + 4)
                for t in range(2):
                    ps = bank(2)[:, 256 * t:256 * t + 256].rearrange("p (k q) -> p k q", k=KT)[:, :, 0:SEQS]
                    b = vecT[:, b0 + KT * t:b0 + KT * t + KT].unsqueeze(2).to_broadcast([P, KT, SEQS])
                    own(tt(modT[:, g + t], ps, b, ALU.add))
                stt(modT[:, g + 1], modT[:, g + 1], 1.0, gvec.unsqueeze(2).to_broadcast([P, KT, SEQS]),
                    ALU.add, ALU.mult).then_inc(s["modT"], 1)

            def modulate_samples(dst, ps, g, done):
                def per_seq(a):
                    return a[:, :, 1:SEQS].unsqueeze(3).to_broadcast([P, KT, NSEQ, DSEQ])
                out = dst[:, :, SEQ:TOK].rearrange("p k (b t) -> p k b t", b=NSEQ)
                own(tt(out, ps.rearrange("p (k b t) -> p k b t", k=KT, b=NSEQ), per_seq(modT[:, g + 1]), ALU.mult))
                tt(out, out, per_seq(modT[:, g]), ALU.add).then_inc(s[done], 1)

            for i in range(ADA_FIRST):
                mod_evac(i)
            mod_transposed(0, 0, vecT[:, 48:56])
            v.wait_ge(s["modT"], 1)
            v.wait_ge(s["xT_ps"], 1)
            modulate_samples(hT, bank(3)[:, 256:512], 0, "hT_s")

            def conv(h):
                v.wait_ge(s["tap3"], h + 1)
                ps = unit_bank(3 + NU + h)
                for j in (2, 1, 0):
                    sh = 3 - j
                    tap = 66 + j * CT + h
                    ins = stt(qkvT[:, h, sh:SEQ], ps[:, 0:SEQ - sh], vecT[:, tap:tap + 1], qkvT[:, h, sh:SEQ],
                              ALU.mult, ALU.add)
                    if j:
                        own(ins)
                    else:
                        ins.then_inc(s["conv_done"], 1)

            def sample_conv(lo, hi):
                def tap_of(j):
                    return vecT[:, 66 + j * CT + lo:66 + j * CT + hi].unsqueeze(2).unsqueeze(3) \
                        .to_broadcast([P, hi - lo, NSEQ, DSEQ])
                acc4 = s_tap[:, lo:hi].rearrange("p m (b t) -> p m b t", b=NSEQ)
                tmp4 = s_tmp[:, 0:hi - lo].rearrange("p m (b t) -> p m b t", b=NSEQ)
                own(tt(acc4, cexs[:, lo:hi, :, 0:DSEQ], tap_of(0), ALU.mult))
                for j in (1, 2, 3):
                    own(tt(tmp4, cexs[:, lo:hi, :, j:j + DSEQ], tap_of(j), ALU.mult))
                    ins = tt(acc4, acc4, tmp4, ALU.add)
                    own(ins) if j < 3 else ins.then_inc(s["s_taps"], 1)

            def inverse(p, n):
                v.wait_ge(s["norm_root"], p + 1)
                own(v.reciprocal(rnorm[:, 0:n], rnorm[:, 0:n]))

            for n in range(ADA_FIRST, len(RING_SLOTS)):
                kind, i = RING_SLOTS[n]
                if kind == "ada":
                    if i == ADA_FIRST:
                        v.wait_ge(s["small_in"], 16 * N_SMALL)
                    mod_evac(i)
                    if i == 10:
                        mod_transposed(2, 24, vecT[:, 56:64])
                for u in units_of(n):
                    h = u - 3 - NU
                    if not 0 <= h < CT:
                        continue
                    conv(h)
                    if 0 <= h - 2 < 2 * H:
                        g = h - 2
                        v.wait_ge(s["silu_done"], g + 1)
                        if g >= 4:
                            v.wait_ge(s["norm_ps"], (g - 4) // 2 + 1)
                        tt(sq[g % 4][:, 0:SEQ], qkvT[:, g, 0:SEQ], qkvT[:, g, 0:SEQ], ALU.mult).then_inc(s["sq"], 1)
                    p = (h - NORM_LAG - 1) / 2
                    if p in range(H):
                        p = int(p)
                        inverse(p, 2 * SEQ)
                        pair = qkvT[:, 2 * p:2 * p + 2, 0:SEQ]
                        stt(pair, pair, DH ** -0.5 if 2 * p < H else 1.0,
                            rnorm.rearrange("p (h t) -> p h t", h=2), ALU.mult, ALU.mult).then_inc(s["qk_n"], 1)
                    if h == SAMPLE_TAPS:
                        v.wait_ge(s["norm_ps"], H - 1)
                        sample_conv(0, 2 * H)
                    if h == SAMPLE_TAPS + 2:
                        v.wait_ge(s["s_silu"], 1)
                        v.wait_ge(s["s_taps"], 1)
                        qk_s = qkvT[:, 0:2 * H, SEQ:TOK]
                        tt(sq_s.rearrange("p (h t) -> p h t", h=2 * H), qk_s, qk_s, ALU.mult).then_inc(s["sq"], 1)
                    if h == CT - 1:
                        v.wait_ge(s["norm_ps"], H + 1)
                        sample_conv(2 * H, CT)
                        inverse(H, 2 * H * NS)
                        rs = rnorm[:, 0:2 * H * NS].rearrange("p (h t) -> p h t", h=2 * H)
                        stt(qkvT[:, 0:H, SEQ:TOK], qkvT[:, 0:H, SEQ:TOK], DH ** -0.5, rs[:, 0:H], ALU.mult, ALU.mult)
                        tt(qkvT[:, H:2 * H, SEQ:TOK], qkvT[:, H:2 * H, SEQ:TOK], rs[:, H:], ALU.mult).then_inc(s["qk_n"], 1)
                    if h == 0:
                        v.wait_ge(s["z_sb"], 3)
                        v.wait_ge(s["small_in"], 16 * N_SMALL)
                        own(tt(spt[0], ab[:, :, 0:H], dtb.unsqueeze(1).to_broadcast([P, 3, H]), ALU.add))
                        own(ts(spt[1], spt[0], -1.0, None, ALU.mult))
                        tt(spt[1], spt[0], spt[1], ALU.min).then_inc(s["softplus_v"], 1)
                    if h == 5:
                        v.wait_ge(s["softplus_a"], 1)
                        ts(spt[1], spt[1], 1.0, None, ALU.add).then_inc(s["softplus_v"], 1)
                        own(ts(spt[2], spt[0], 0.0, None, ALU.max))
                        own(ts(beta, beta, 1.0, None, ALU.add))
                        own(v.reciprocal(beta, beta))
                    if h == 7:
                        v.wait_ge(s["softplus_a"], 2)
                        own(tt(spt[2], spt[1], spt[2], ALU.add))
                        stt(gg, spt[2], -1.0, alog.unsqueeze(1).to_broadcast([P, 3, H]), ALU.mult, ALU.mult
                            ).then_inc(s["gates"], 1)
                        v.wait_ge(s["gates"], 1)
                        tt(gseq[0:NS], gg[0:NS, 2, :].unsqueeze(1).to_broadcast([NS, NSEQ, H]),
                           of_seq[0:NS, :].unsqueeze(2).to_broadcast([NS, NSEQ, H]), ALU.mult
                           ).then_inc(s["gates"], 1)
            v.wait_ge(s["egates"], 1)
            own(stt(negeb[:, 0:2, :], egc[:, 0:2, :], -1.0, beta[:, 0:2, :], ALU.mult, ALU.mult))
            own(stt(negeb[0:NS, 2, :], egc[0:NS, 2, :], -1.0, beta[0:NS, 2, :], ALU.mult, ALU.mult))

            def by_head(a, c, n):
                return a[0:n, c, :].rearrange("p (h d) -> p h d", h=H)

            def scale_values(o):
                n, c = ROWS[ORDER[o]], ORDER[o]
                return tt(by_head(tokV, c, n), by_head(tokV, c, n), per_head(beta[0:n, c, :], n), ALU.mult)

            def level_mask(o, l, n):
                at = LEVELS * P + NS * l if o == 0 else P * l
                return every_head(lmask[0:n, at:at + n], n, n)

            def masked(i):
                o, l = STEPS[i]
                n = ROWS[ORDER[o]]
                L, _, _, Mk = buffers(o)[:4]
                tt(Mk[0:n], L[0:n], level_mask(o, l, n), ALU.mult).then_inc(s["ml"], 1)

            def update(i):
                o, l = STEPS[i]
                n = ROWS[ORDER[o]]
                _, T, U, _, _, _, A, B = buffers(o)
                v.wait_ge(s["tn_ps"], i + 1)
                if o and l < LEVELS - 1:
                    tt(T[0:n], T[0:n], heads(A, n, n), ALU.subtract)
                tt(U[0:n], U[0:n], heads(B, n, n), ALU.subtract).then_inc(s["tu_done"], 1)

            for o in range(3):
                c = ORDER[o]
                n = ROWS[c]
                L, T, U, Mk = buffers(o)[:4]
                Dx = dmat(o)[0:n]
                upto_m, after_m, tril_m = masks(o)
                if o == 0:
                    v.wait_ge(s["slot_used"], len(RING_SLOTS))
                else:
                    v.wait_ge(s["tn_ps"], 1)
                    v.wait_ge(s["tu_done"], 1)
                tt(Mk[0:n], every_head(after_m[0:n, 0:n], n, n), per_head(gg[0:n, c, :], n, n), ALU.mult
                   ).then_inc(s["ga"], 1)
                v.wait_ge(s["dexp"], o + 1)
                own(tt(Dx, Dx, every_head(tril_m[0:n, 0:n], n, n), ALU.mult))
                v.wait_ge(s["kk_ps"], o + 1)
                for h in range(H):
                    ins = stt(L[0:n, h, :], heads(2, n, n)[:, h, :], beta[0:n, c, h:h + 1], Dx[:, h, :],
                              ALU.mult, ALU.mult)
                ins.then_inc(s["lmat"], 1)
                v.wait_ge(s["qk_ps"], o + 1)
                v.wait_ge(s["lmat"], o + 1)
                tt(Dx, heads(4, n, n), Dx, ALU.mult).then_inc(s["qkd"], 1)
                own(tt(Mk[0:n], L[0:n], level_mask(o, 0, n), ALU.mult))
                tt(T[0:n], every_head(ident[0:n, 0:n], n, n), Mk[0:n], ALU.subtract).then_inc(s["t0"], 1)
                v.wait_ge(s["t0"], o + 1)
                if o == 0:
                    masked(0)
                    v.wait_ge(s["u0"], 1)
                    update(0)
            masked(1)
            masked(2)
            v.wait_ge(s["kv_tok"], 6)
            own(scale_values(0))
            own(scale_values(2))
            for i in range(1, len(STEPS)):
                v.wait_ge(s["u0"], 3)
                update(i)
                if i + 2 < len(STEPS):
                    masked(i + 2)

            v.wait_ge(s["ssm_in"], 16 * (NSEQ + 1))
            for h in range(H):
                if h >= 2:
                    v.wait_ge(s["ks_ps"], h - 1)
                for t in range(2):
                    ins = tt(kq_mask[h % 2][:, :, NS * t:NS * t + NS],
                             qkvT[:, H * (1 - t) + h, SEQ:TOK].unsqueeze(1).to_broadcast([P, NSEQ, NS]), seqmask,
                             ALU.mult)
                ins.then_inc(s["kqm"], 1)

            O, O2 = P1[0], P1[1]

            def residual(o, ps):
                n, c = ROWS[ORDER[o]], ORDER[o]
                for h in range(H):
                    val = tokV[0:n, c, P * h:P * h + P]
                    ins = stt(val, ps[0:n, h, :], negeb[0:n, c, h:h + 1], val, ALU.mult, ALU.add)
                ins.then_inc(s["rr"], 1)

            def decayed_keys(o):
                n, c = ROWS[ORDER[o]], ORDER[o]
                tt(by_head(tokK, c, n), by_head(tokK, c, n), per_head(egr[0:n, c, :], n), ALU.mult
                   ).then_inc(s["kdec"], 1)

            def gated_norm(o):
                n, c = ROWS[ORDER[o]], ORDER[o]
                v.wait_ge(s["o_tok"], o + 1)
                own(stt(O2[0:n], O[0:n], 1.0 / DH, O[0:n], ALU.mult, ALU.mult))
                v.tensor_reduce(orr[0:n, c, :], O2[0:n], AX.X, ALU.add).then_inc(s["o_ms"], 1)
                v.wait_ge(s["o_root"], o + 1)
                own(v.reciprocal(orr[0:n, c, :], orr[0:n, c, :]))
                own(tt(O[0:n], O[0:n], per_head(orr[0:n, c, :], n), ALU.mult))
                own(tt(O[0:n], O[0:n], every_head(gdnw[0:n, :], n), ALU.mult))
                tt(by_head(z, c, n), by_head(z, c, n), O[0:n], ALU.mult).then_inc(s["gated"], 1)

            v.wait_ge(s["ks_ps"], H)
            own(v.tensor_copy(O[0:NS], bank(0, 2)[NS:2 * NS, 0:GW].rearrange("p (h d) -> p h d", h=H)))
            residual(0, heads(0, NS))
            tt(O[0:NS], O[0:NS], per_head(egc[0:NS, 2, :], NS), ALU.mult).then_inc(s["qs_sb"], 1)
            decayed_keys(0)
            scale_values(1).then_inc(s["rr"], 1)
            decayed_keys(1)
            decayed_keys(2)
            v.wait_ge(s["o_ps"], 1)
            v.wait_ge(s["qs_sb"], 1)
            tt(O[0:NS], O[0:NS], heads(4, NS), ALU.add).then_inc(s["o_tok"], 1)
            for h in range(H):
                v.wait_ge(s["s_ps"], h + 2)
                for b in range(NSEQ):
                    ins = stt(Ssm[:, b, h, :], Ssm[:, b, h, :], egls[:, b, h:h + 1],
                              bank((6, 0)[h % 2], 2)[:, DH * b:DH * b + DH], ALU.mult, ALU.add)
                ins.then_inc(s["s_new"], 1)
            v.wait_ge(s["z_sb"], 6)
            gated_norm(0)
            v.wait_ge(s["ks_ps"], H + 1)
            residual(2, heads(0, P))
            v.wait_ge(s["gated"], 1)
            v.wait_ge(s["o_ps"], 2)
            v.tensor_copy(O, heads(4, P)).then_inc(s["o_tok"], 1)
            gated_norm(1)
            v.wait_ge(s["gated"], 2)
            v.wait_ge(s["ks_ps"], H + 2)
            tt(O, heads(6, P), per_head(egc[:, 1, :], P), ALU.mult).then_inc(s["qs_sb"], 1)
            v.wait_ge(s["o_ps"], 3)
            v.wait_ge(s["qs_sb"], 2)
            tt(O, O, heads(4, P), ALU.add).then_inc(s["o_tok"], 1)
            v.wait_ge(s["s_ps"], H + 2)
            v.wait_ge(s["sp_e"], 1)
            for h in range(H):
                ins = stt(Sp[:, h, :], Sp[:, h, :], egl[:, 1, h:h + 1], heads(0, P)[:, h, :], ALU.mult, ALU.add)
            ins.then_inc(s["s_new"], 1)
            gated_norm(2)

            v.wait_ge(s["gm_in"], 16 * 18)
            for c in range(3):
                n = ROWS[c]
                own(rstd(st, c, c + 1, c + 2, n))
                if c == 2:
                    v.wait_ge(s["x1"], 1)
                own(stt(xt[c % 2][0:n, :], mix_s[0:n, :] if c == 2 else bank((4, 6)[c], 2), st[0:n, 4 + c:5 + c],
                        gm_tok[c][0:n, :], ALU.mult, ALU.mult))
                tt(x_sb[0:n, c, :], x_sb[0:n, c, :], xt[c % 2][0:n, :], ALU.add).then_inc(s["x1"], 1)
            own(v.memset(h2[:, 2, :], 0.0))
            own(rstd(st, 0, 3, 5))
            for c in range(3):
                n = ROWS[c]
                ts(h2[0:n, c, :], x_sb[0:n, c, :], st[0:n, 4 + c:5 + c], None, ALU.mult).then_inc(s["xn2"], 1)
            v.wait_ge(s["x2T_ps"], 1)
            v.wait_ge(s["modT"], 2)
            modulate_samples(h2T, bank(2)[:, 0:256], 2, "h2T")

            v.wait_ge(s["rt_in"], 16 * 7)
            v.wait_ge(s["x1_st"], 48)
            own(v.memset(lg, 0.0))
            v.wait_ge(s["router_ps"], 2)
            v.tensor_copy(lg[:, 0:2, :], bank(2)[:, 0:2 * NE].rearrange("p (c e) -> p c e", c=2))
            own(v.tensor_copy(lg[0:NS, 2, :], bank(2)[0:NS, 2 * NE:3 * NE]))
            for c in range(3):
                own(v.max(top8[:, c, :], lg[:, c, :]))
            tt(exg, lg, top8[:, :, 0:1].to_broadcast([P, 3, NE]), ALU.subtract).then_inc(s["gex"], 1)
            own(v.memset(top8[:, :, TOPK:8], 3.0e38))
            for c in range(3):
                own(v.match_replace(eqm[:, c, :], top8[:, c, :], lg[:, c, :], -3.0e38))
            own(tt(sel01, eqm, lg, ALU.not_equal))
            v.wait_ge(s["gex"], 2)
            own(tt(exg, exg, sel01, ALU.mult))
            own(v.tensor_reduce(rst[:, 0:3], exg, AX.X, ALU.add))
            ts(sel01[:, 2, :], sel01[:, 2, :], rvalid[:, 0:1], None, ALU.mult).then_inc(s["top_e"], 1)
            own(v.reciprocal(rst[:, 3:6], rst[:, 0:3]))
            v.wait_ge(s["h2_ps"], 3)
            tt(gate, exg, rst[:, 3:6].unsqueeze(2).to_broadcast([P, 3, NE]), ALU.mult).then_inc(s["gate_done"], 1)
            v.wait_ge(s["router_ps"], 5)
            step = Chain(v, s["hid_step"])
            step(ts(cntb, bank(6)[:, 0:NE], float(SLOTS), 1.0, ALU.is_gt, ALU.add))
            for r in range(2, (TOK + SLOTS - 1) // SLOTS):
                step(stt(cntb, bank(6)[:, 0:NE], float(SLOTS * r), cntb, ALU.is_gt, ALU.add))
            own(v.memset(cumf, 1.0))
            own(v.memset(cnt, 0.0))
            own(v.tensor_tensor_scan(cumf[:, 1:NE + 1], cntb, cnt, 1.0, ALU.add, ALU.add))
            ts(ends_i[0:1, :], cumf[0:1, 1:NE + 1], -1.0, None, ALU.add).then_inc(s["cum"], 1)
            v.tensor_copy(cum_i[0:1, :], cumf[0:1, :]).then_inc(s["cum"], 1)
            v.wait_ge(s["router_ps"], 4)
            v.wait_ge(s["top_e"], 1)
            own(stt(rank, bank(5)[:, 0:3 * NE].rearrange("p (c e) -> p c e", c=3), 1.0, sel01, ALU.add, ALU.mult))
            ts(rank, rank, -1.0, None, ALU.add).then_inc(s["rank_done"], 1)
            v.memset(y_sb, 0.0).then_inc(s["y_sb"], 1)
            v.memset(selGT, 0.0).then_inc(s["sgT"], 1)

            v.wait_ge(s["rank_done"], 1)
            v.wait_ge(s["cum"], 2)
            for u in range(5):
                v.wait_ge(s["sc_ps"], u + 1)
                v.tensor_copy(sums(u), (bank(u % 2) if u < 4 else bank(0))[0:sum_rows(u), :]).then_inc(s["acc_add"], 1)
            v.wait_ge(s["bguT"], 1)
            hg = hidg.rearrange("p (k t) -> p k t", k=KT)
            hu = hidu.rearrange("p (k t) -> p k t", k=KT)
            T2 = bank(4, 2).rearrange("p (k x t) -> p k x t", k=KT, x=2)

            def add_back(i, u):
                a = sums(u)
                v.wait_ge(s["sc_ps"], i * 5 + (u + 1))
                tt(a, a, bank(SUM_BANKS[u])[0:sum_rows(u), :], ALU.add).then_inc(s["acc_add"], 1)

            with v.Fori(0, NE // 2) as pair:
                for par in range(2):
                    first = v.value_load(cum_i[0:1, bass.ds(pair * 2 + par, 1)], min_val=1, max_val=257)
                    end = v.value_load(cum_i[0:1, bass.ds(pair * 2 + par + 1, 1)], min_val=2, max_val=257)
                    with v.Fori(first, end) as i:
                        v.wait_ge(s["gu_ps"], i)
                        v.tensor_copy(gu_sb[:, 1, :], bank(3)).then_inc(s["gu_v"], 1)
                        v.wait_ge(s["hid_ps"], i)
                        bias = [bguT[:, bass.ds((pair * 2 + par) * 16 + KT * t, KT)].unsqueeze(2)
                                .to_broadcast([P, KT, SLOTS]) for t in range(2)]
                        tt(hg, T2[:, :, 0, :], bias[0], ALU.add).then_inc(s["hid_step"], 1)
                        tt(hu, T2[:, :, 1, :], bias[1], ALU.add).then_inc(s["hid_step"], 1)
                        v.wait_ge(s["hid_step"], i * 4 + 1)
                        ts(hidg, hidg, LIMIT, None, ALU.min).then_inc(s["g_ready"], 1)
                        v.wait_ge(s["hid_step"], i * 4 + 2)
                        ts(hidu, hidu, LIMIT, -LIMIT, ALU.min, ALU.max).then_inc(s["hid_step"], 1)
                        add_back(i, 0)
                        v.wait_ge(s["hid_step"], i * 4 + 3)
                        v.wait_ge(s["g_ready"], i)
                        v.wait_ge(s["sig"], i)
                        stt(hidg, hidu, 1.0, hidg, ALU.add, ALU.mult).then_inc(s["hid_step"], 1)
                        add_back(i, 1)
                        v.wait_ge(s["hid_step"], i * 4 + 4)
                        tt(hidg, hidg, sig, ALU.mult).then_inc(s["hid"], 1)
                        for u in range(2, 5):
                            add_back(i, u)
            rounds = v.value_load(cum_i[0:1, NE:NE + 1], min_val=2, max_val=257)
            for u in range(5):
                add_back(rounds, u)
            v.wait_ge(s["acc_add"], rounds * 5 + 5)
            v.tensor_copy(acc[0:NS, 2, 512:D], acc[32:32 + NS, 2, 0:512]).then_inc(s["acc_add"], 1)

            v.wait_ge(s["fin_in"], 16 * 20)
            for c in range(3):
                n = ROWS[c]
                own(rstd(fst, c, c + 1, 6 + c, n))
                own(stt(fin_t[0:n, c, :], acc[0:n, c, :], fst[0:n, 4 + c:5 + c], fin_g[c][0:n, :], ALU.mult, ALU.mult))
                tt(fin_x[0:n, c, :], fin_x[0:n, c, :], fin_t[0:n, c, :], ALU.add).then_inc(s["fin_y"], 1)

        @block.gpsimd
        def _(g):
            own = Chain(g, s["ch_pool"])
            own(g.memset(wpbd, 0.0))
            own(g.memset(uext[:, :, 0:PBUF], 0.0))
            g.memset(tokK[:, 2, :], 0.0).then_inc(s["zeroed"], 1)

            for i in range(4):
                r = 64 * (i % 2)
                g.dma_start(wpbd[r:r + 64, i // 2, r:r + 64], w_pool[0, i]).then_inc(s["wpool_in"], 16)
            g.dma_start(alog, a_log.to_broadcast([P, H])).then_inc(s["small_in"], 16)
            g.dma_start(dtb, dt_bias.to_broadcast([P, H])).then_inc(s["small_in"], 16)
            g.dma_start(gdnw, gdn_norm_w.to_broadcast([P, DH])).then_inc(s["small_in"], 16)
            ba = b_ada.rearrange("a (u j n) -> a u j n", j=4, n=P)
            for j in range(4):
                rows = slice(32 * j, 32 * j + 32)
                for i in range(2):
                    u = 4 + 6 * i
                    g.dma_start(b_row[rows, 2 * i:2 * i + 2, :], ba[:, u:u + 2, j].to_broadcast([32, 2, P])
                                  ).then_inc(s["small_in"], 16)
                    gp = (g_post_mix, g_post_ffn)[i].rearrange("a (u j n) -> a u j n", j=4, n=P)
                    g.dma_start(gpost[rows, 2 * i:2 * i + 2, :], gp[:, :, j].to_broadcast([32, 2, P])
                                  ).then_inc(s["small_in"], 16)
            g.dma_start(lmask_t[:, :], cc("levels")).then_inc(s["small_in"], 16)

            g.wait_ge(s["u_sb"], 2)
            g.wait_ge(s["setup_sb"], 4)
            g.wait_ge(s["const_in"], 16 * N_CONST)
            add = lambda o, a, b: g.tensor_tensor(o, a, b, ALU.add)
            E = PBUF + SEQ
            own(add(win_a[:, :, 1:E], uext[:, :, 1:E], uext[:, :, 0:E - 1]))
            own(add(win_b[:, :, 3:E], win_a[:, :, 3:E], win_a[:, :, 1:E - 2]))
            own(add(win_a[:, 1, 7:E], win_b[:, 1, 7:E], win_b[:, 1, 3:E - 4]))
            own(add(win_b[64:, 1, 15:E], win_a[64:, 1, 15:E], win_a[64:, 1, 7:E - 8]))
            F = PBUF + DSEQ
            own(add(win_sa[:, :, :, 1:F], uexs[:, :, :, 1:F], uexs[:, :, :, 0:F - 1]))
            own(add(win_sb[:, :, :, 3:F], win_sa[:, :, :, 3:F], win_sa[:, :, :, 1:F - 2]))
            own(add(win_sa[:, 1, :, 7:F], win_sb[:, 1, :, 7:F], win_sb[:, 1, :, 3:F - 4]))
            own(add(win_sb[64:, 1, :, 15:F], win_sa[64:, 1, :, 15:F], win_sa[64:, 1, :, 7:F - 8]))
            for lo, m, w, ws in ((0, 0, win_a, win_sa), (64, 0, win_b, win_sb), (0, 1, win_a, win_sa),
                                 (64, 1, win_b, win_sb)):
                r = slice(lo, lo + 64)
                own(g.tensor_scalar(pooled[r, m, 0:SEQ], w[r, m, PBUF:], invwin[r, m:m + 1], None, ALU.mult))
                own(g.tensor_scalar(pooled[r, m, SEQ:TOK].rearrange("p (b t) -> p b t", b=NSEQ), ws[r, m, :, PBUF:],
                                    invwin[r, m:m + 1], None, ALU.mult))
                own(g.tensor_tensor(pooled[r, m, 0:16], w[r, m, PBUF:PBUF + 16], invcnt[r, m, :], ALU.mult))
            own(g.tensor_tensor(pooled[:, :, 0:SEQ], pooled[:, :, 0:SEQ], uext[:, :, PBUF:], ALU.subtract))
            for m in range(NU):
                ps = pooled[:, m, SEQ:TOK].rearrange("p (b t) -> p b t", b=NSEQ)
                ins = g.tensor_tensor(ps, ps, uexs[:, m, :, PBUF:], ALU.subtract)
                own(ins) if m == 0 else ins.then_inc(s["pooled"], 1)

            g.wait_ge(s["ssm_in"], 16 * (NSEQ + 1))
            own(g.memset(vmask[0], 0.0))
            g.wait_ge(s["tu_done"], len(STEPS))
            own(g.memset(vmask[1], 0.0))
            g.wait_ge(s["vn"], 1)
            for h in range(H):
                if h >= 2:
                    g.wait_ge(s["s_ps"], h)
                g.tensor_tensor(vmask[h % 2][0:NS], tokV[0:NS, 2, P * h:P * h + P].unsqueeze(1).to_broadcast([NS, NSEQ, DH]),
                                of_seq[0:NS, :].unsqueeze(2).to_broadcast([NS, NSEQ, DH]), ALU.mult
                                ).then_inc(s["vmask"], 1)

            g.wait_ge(s["rank_done"], 1)
            g.wait_ge(s["gate_done"], 1)
            g.wait_ge(s["cum"], 2)
            g.wait_ge(s["bguT"], 1)

            g.memset(cur[:, 2, :], float(SLOTS)).then_inc(s["sgT_ps"], 1)
            g.wait_ge(s["sgT_ps"], 1)

            def select():
                for c in range(3):
                    ins = g.tensor_scalar(selA[:, c, :], iota[:, 0:SLOTS], cur[:, 0, c:c + 1], None, ALU.is_equal)
                ins.then_inc(s["sel"], 1)

            with g.Fori(1, NE + 1) as e:
                first = g.value_load(cum_i[0:1, bass.ds(e - 1, 1)], min_val=1, max_val=257)
                end = g.value_load(cum_i[0:1, bass.ds(e, 1)], min_val=2, max_val=257)
                g.tensor_copy(cur[:, 0:2, :], rank_gate[:, :, :, bass.ds(e - 1, 1)].rearrange("p x c e -> p x (c e)")
                              ).then_inc(s["cur_set"], 1)
                with g.Fori(first, end) as i:
                    g.wait_ge(s["bguT"], 1)
                    g.wait_ge(s["cur_set"], e)
                    select()
                    g.wait_ge(s["bguT"], 1)
                    g.wait_ge(s["sgT_ps"], i)
                    for c in range(3):
                        ins = g.tensor_scalar(selG[:, c, :], iota, cur[:, 0, c:c + 1], cur[:, 1, c:c + 1],
                                              ALU.is_equal, ALU.mult)
                    ins.then_inc(s["selg"], 1)
                    g.wait_ge(s["selg"], i)
                    g.tensor_tensor(cur[:, 0, :], cur[:, 0, :], cur[:, 2, :], ALU.subtract).then_inc(s["sel_step"], 1)
                    g.wait_ge(s["xg_ps"], i)
                    g.wait_ge(s["sel_step"], i)
            select()


_INS = ["x_prompt", "x_sample", "c_prompt", "c_sample", "state_pool", "state_conv", "state_ssm", "w_ada", "b_ada",
        "g_pre_mix", "g_post_mix", "g_pre_ffn", "g_post_ffn", "w_in", "w_pool", "pool_scale", "conv_w", "a_log",
        "dt_bias", "gdn_norm_w", "w_out", "router_w", "router_b", "w_gu", "b_gu", "w_down", "b_down"]
_OUTS = [(1, SEQ, D), (NSEQ, DSEQ, D), (1, 1, PBUF, POOLW), (1, 1, 3, CW), (1, 1, H, DH, DH),
         (1, NSEQ, PBUF, POOLW), (1, NSEQ, 3, CW), (1, NSEQ, H, DH, DH)]


def program(nc, inputs):
    arrays, args = {}, []
    for name in _INS:
        a = np.ascontiguousarray(inputs[name])
        arrays[f"in_{name}"] = a
        args.append(nc.dram_tensor(f"in_{name}", a.shape, mybir.dt.from_np(a.dtype), kind="ExternalInput").ap())
    arrays["shape_consts"] = shape_constants()
    args.append(nc.dram_tensor("shape_consts", arrays["shape_consts"].shape, F32, kind="ExternalInput").ap())
    for i, shape in enumerate(_OUTS):
        args.append(nc.dram_tensor(f"out_{i}", shape, F32, kind="ExternalOutput").ap())
    build(nc, *args)
    return arrays


def kernel(**inputs):
    import concourse.bacc as bacc
    from concourse.bass_utils import run_bass_kernel_spmd

    nc = bacc.Bacc("TRN2", target_bir_lowering=False, num_devices=1)
    arrays = program(nc, inputs)
    r = run_bass_kernel_spmd(nc, [arrays], core_ids=[0])
    return tuple(r.results[0][f"out_{i}"] for i in range(len(_OUTS)))
```
